# Optimizing a Trainium2 kernel written in Bass

```python
import math
import jax, jax.numpy as jnp
from jax import lax
import numpy as np

D_MODEL = 1024
BATCH = 1
SEQ = 256
DEPTH = 1

LRU_WIDTH = D_MODEL // 4
LRU_BLOCKS = 4
LRU_BLOCK_W = LRU_WIDTH // LRU_BLOCKS
LRU_CONV = 4
LRU_C = 8.0
GLA_HEADS = 4
GLA_DV = (D_MODEL // 4) // GLA_HEADS
GLA_DK = GLA_DV // 2
GLA_GATE_RANK = 16
GLA_TAU = 16.0
GLA_CHUNK = 64
MOBA_HEADS = 8
MOBA_DH = (D_MODEL // 2) // MOBA_HEADS
MOBA_BLOCK = 256
MOBA_TOPK = 3
MOBA_Q_CHUNK = 128
REL_BUCKETS = 32
REL_MAX_DIST = 128
D_FF = -(-8 * D_MODEL // (3 * 256)) * 256

GLA_QK_W = GLA_HEADS * GLA_DK
GLA_V_W = GLA_HEADS * GLA_DV
MOBA_W = MOBA_HEADS * MOBA_DH
D_MIX = LRU_WIDTH + GLA_V_W + MOBA_W
IN_SPLITS = (LRU_WIDTH, LRU_WIDTH, GLA_QK_W, GLA_QK_W, GLA_V_W, GLA_GATE_RANK, GLA_V_W, MOBA_W, MOBA_W, MOBA_W)
D_IN = sum(IN_SPLITS)
RMS_EPS = 1e-6
NEG_INF = -1e30


def rms_norm(x, g):
    xf = x.astype(jnp.float32)
    y = xf * lax.rsqrt(jnp.mean(xf * xf, axis=-1, keepdims=True) + RMS_EPS)
    return (y * g.astype(jnp.float32)).astype(x.dtype)

def split_heads(t, n):
    b, s, w = t.shape
    return t.astype(jnp.float32).reshape(b, s, n, w // n).transpose(0, 2, 1, 3)

def t5_bucket(rel):
    n = jnp.maximum(rel, 0)
    max_exact = REL_BUCKETS // 2
    nf = jnp.maximum(n, 1).astype(jnp.float32)
    large = max_exact + (jnp.log(nf / max_exact) / math.log(REL_MAX_DIST / max_exact)
                         * (REL_BUCKETS - max_exact)).astype(jnp.int32)
    large = jnp.minimum(large, REL_BUCKETS - 1)
    return jnp.where(n < max_exact, n, large)

def rg_lru_branch(xb, gb, conv_w, conv_b, wa, ba, wx, bx, lam):
    b, s, c = xb.shape
    xc = lax.conv_general_dilated(xb, conv_w[:, None, :].astype(xb.dtype), window_strides=(1,),
                                  padding=[(LRU_CONV - 1, 0)],
                                  dimension_numbers=('NWC', 'WIO', 'NWC'),
                                  feature_group_count=c)
    xc = xc.astype(jnp.float32) + conv_b.astype(jnp.float32)
    xg = xc.reshape(b, s, LRU_BLOCKS, LRU_BLOCK_W)
    r = jax.nn.sigmoid(jnp.einsum('bsgi,gij->bsgj', xg, wa.astype(jnp.float32)).reshape(b, s, c)
                       + ba.astype(jnp.float32))
    i = jax.nn.sigmoid(jnp.einsum('bsgi,gij->bsgj', xg, wx.astype(jnp.float32)).reshape(b, s, c)
                       + bx.astype(jnp.float32))
    log_a = -LRU_C * r * jax.nn.softplus(-lam.astype(jnp.float32))
    a = jnp.exp(log_a)
    mult = jnp.sqrt(-jnp.expm1(2.0 * log_a))
    mult = mult.at[:, 0].set(1.0)
    u = mult * (i * xc)

    def combine(left, right):
        a1, b1 = left
        a2, b2 = right
        return a1 * a2, a2 * b1 + b2

    _, h = lax.associative_scan(combine, (a, u), axis=1)
    return h * jax.nn.gelu(gb.astype(jnp.float32))

def gla_chunked(q, k, v, g):
    b, h, s, dk = q.shape
    dv = v.shape[-1]
    c = GLA_CHUNK
    n = s // c
    q = q.reshape(b, h, n, c, dk) * (dk ** -0.5)
    k = k.reshape(b, h, n, c, dk)
    v = v.reshape(b, h, n, c, dv)
    cum = jnp.cumsum(g.reshape(b, h, n, c, dk), axis=3)
    last = cum[:, :, :, -1:, :]
    q_d = q * jnp.exp(cum)
    k_d = k * jnp.exp(-cum)
    causal = jnp.tril(jnp.ones((c, c), dtype=bool))
    attn = jnp.where(causal, jnp.einsum('bhncd,bhned->bhnce', q_d, k_d), 0.0)
    intra = jnp.einsum('bhnce,bhnev->bhncv', attn, v)
    kv = jnp.einsum('bhncd,bhncv->bhndv', k * jnp.exp(last - cum), v)
    decay = jnp.exp(last[:, :, :, 0, :])

    def step(state, inp):
        kv_n, d_n = inp
        return d_n[..., None] * state + kv_n, state

    init = jnp.zeros((b, h, dk, dv), jnp.float32)
    _, s_prev = lax.scan(step, init, (kv.transpose(2, 0, 1, 3, 4), decay.transpose(2, 0, 1, 3)))
    s_prev = s_prev.transpose(1, 2, 0, 3, 4)
    inter = jnp.einsum('bhncd,bhndv->bhncv', q_d, s_prev)
    return (intra + inter).reshape(b, h, s, dv)

def moba_attention(q, k, v, rel_bias):
    b, h, s, d = q.shape
    nb = -(-s // MOBA_BLOCK)
    pad = nb * MOBA_BLOCK - s
    k_blk = jnp.pad(k, ((0, 0), (0, 0), (0, pad), (0, 0))).reshape(b, h, nb, MOBA_BLOCK, d)
    v_blk = jnp.pad(v, ((0, 0), (0, 0), (0, pad), (0, 0))).reshape(b, h, nb, MOBA_BLOCK, d)
    k_mean = jnp.mean(k_blk, axis=3)
    topk = min(MOBA_TOPK, nb)
    scale = d ** -0.5
    bias_h = rel_bias.T.astype(jnp.float32)
    bi = jnp.arange(b)[:, None, None]
    hi = jnp.arange(h)[None, :, None]
    blk_ids = jnp.arange(nb)
    offs = jnp.arange(MOBA_BLOCK)

    def chunk(ci):
        q0 = ci * MOBA_Q_CHUNK
        qc = lax.dynamic_slice_in_dim(q, q0, MOBA_Q_CHUNK, axis=2)
        qpos = q0 + jnp.arange(MOBA_Q_CHUNK)
        n_past = q0 // MOBA_BLOCK
        gate = jnp.einsum('bhqd,bhnd->bhqn', qc, k_mean)
        gate = jnp.where(blk_ids < n_past, gate, -jnp.inf)
        _, sel = lax.top_k(gate, topk)
        k_own = lax.dynamic_index_in_dim(k_blk, n_past, axis=2, keepdims=False)
        v_own = lax.dynamic_index_in_dim(v_blk, n_past, axis=2, keepdims=False)
        rel_own = qpos[:, None] - (n_past * MOBA_BLOCK + offs)[None, :]
        logit_own = (jnp.einsum('bhqd,bhkd->bhqk', qc, k_own) * scale
                     + bias_h[:, t5_bucket(rel_own)])
        logit_own = jnp.where(rel_own >= 0, logit_own, NEG_INF)
        logits = []
        for j in range(topk):
            idx = sel[..., j]
            kj = k_blk[bi, hi, idx]
            rel = qpos[:, None] - (idx[..., None] * MOBA_BLOCK + offs)
            bias = bias_h[hi[..., None], t5_bucket(rel)]
            lj = jnp.einsum('bhqd,bhqkd->bhqk', qc, kj) * scale + bias
            logits.append(jnp.where(j < n_past, lj, NEG_INF))
        logits.append(logit_own)
        p = jax.nn.softmax(jnp.concatenate(logits, axis=-1), axis=-1)
        p = p.reshape(b, h, MOBA_Q_CHUNK, topk + 1, MOBA_BLOCK)
        out = jnp.einsum('bhqk,bhkd->bhqd', p[..., topk, :], v_own)
        for j in range(topk):
            vj = v_blk[bi, hi, sel[..., j]]
            out = out + jnp.einsum('bhqk,bhqkd->bhqd', p[..., j, :], vj)
        return out

    out = lax.map(chunk, jnp.arange(s // MOBA_Q_CHUNK))
    return out.transpose(1, 2, 0, 3, 4).reshape(b, h, s, d)

def hybrid_mixer(h, w_in, conv_w, conv_b, wa, ba, wx, bx, lam, gate_w2, gate_b, gla_gain, rel_bias):
    bsz, s, _ = h.shape
    proj = h @ w_in
    split_points = [int(p) for p in np.cumsum(IN_SPLITS)[:-1]]
    lru_x, lru_g, gq, gk, gv, g_lr, g_out, mq, mk, mv = jnp.split(proj, split_points, axis=-1)
    y_lru = rg_lru_branch(lru_x, lru_g, conv_w, conv_b, wa, ba, wx, bx, lam)
    log_alpha = jax.nn.log_sigmoid((g_lr @ gate_w2 + gate_b).astype(jnp.float32)) / GLA_TAU
    o = gla_chunked(split_heads(gq, GLA_HEADS), split_heads(gk, GLA_HEADS),
                    split_heads(gv, GLA_HEADS), split_heads(log_alpha, GLA_HEADS))
    o = o.transpose(0, 2, 1, 3)
    o = o * lax.rsqrt(jnp.mean(o * o, axis=-1, keepdims=True) + RMS_EPS)
    y_gla = (o.reshape(bsz, s, GLA_V_W) * gla_gain.astype(jnp.float32)
             * jax.nn.silu(g_out.astype(jnp.float32)))
    y_moba = moba_attention(split_heads(mq, MOBA_HEADS), split_heads(mk, MOBA_HEADS),
                            split_heads(mv, MOBA_HEADS), rel_bias)
    y_moba = y_moba.transpose(0, 2, 1, 3).reshape(bsz, s, MOBA_W)
    return jnp.concatenate([y_lru, y_gla, y_moba], axis=-1).astype(h.dtype)

def first_inputs(seed: int = 0) -> dict:
    key = jax.random.key(seed)
    ks = jax.random.split(key, 24)
    f32 = jnp.float32
    L = DEPTH

    def nrm(k, shape, scale):
        return jax.random.normal(k, shape, f32) * scale

    u = jax.random.uniform(ks[12], (L, LRU_WIDTH), f32, 0.9, 0.999) ** (1.0 / LRU_C)
    return {
        'x': nrm(ks[0], (BATCH, SEQ, D_MODEL), 1.0),
        'pre_mix_norm': 1.0 + nrm(ks[1], (L, D_MODEL), 0.02),
        'post_mix_norm': 1.0 + nrm(ks[2], (L, D_MODEL), 0.02),
        'pre_ffn_norm': 1.0 + nrm(ks[3], (L, D_MODEL), 0.02),
        'post_ffn_norm': 1.0 + nrm(ks[4], (L, D_MODEL), 0.02),
        'w_in': nrm(ks[5], (L, D_MODEL, D_IN), D_MODEL ** -0.5),
        'w_out': nrm(ks[6], (L, D_MIX, D_MODEL), D_MIX ** -0.5),
        'lru_conv_w': nrm(ks[7], (L, LRU_CONV, LRU_WIDTH), LRU_CONV ** -0.5),
        'lru_conv_b': nrm(ks[8], (L, LRU_WIDTH), 0.01),
        'lru_wa': nrm(ks[9], (L, LRU_BLOCKS, LRU_BLOCK_W, LRU_BLOCK_W), LRU_BLOCK_W ** -0.5),
        'lru_ba': nrm(ks[10], (L, LRU_WIDTH), 0.01),
        'lru_wx': nrm(ks[11], (L, LRU_BLOCKS, LRU_BLOCK_W, LRU_BLOCK_W), LRU_BLOCK_W ** -0.5),
        'lru_bx': nrm(ks[13], (L, LRU_WIDTH), 0.01),
        'lru_lambda': jnp.log(u) - jnp.log1p(-u),
        'gla_gate_w2': nrm(ks[14], (L, GLA_GATE_RANK, GLA_QK_W), GLA_GATE_RANK ** -0.5),
        'gla_gate_b': nrm(ks[15], (L, GLA_QK_W), 0.01),
        'gla_norm': 1.0 + nrm(ks[16], (L, GLA_V_W), 0.02),
        'rel_bias': nrm(ks[17], (REL_BUCKETS, MOBA_HEADS), 0.2),
        'w_ffn_gate': nrm(ks[18], (L, D_MODEL, D_FF), D_MODEL ** -0.5),
        'w_ffn_up': nrm(ks[19], (L, D_MODEL, D_FF), D_MODEL ** -0.5),
        'w_ffn_down': nrm(ks[20], (L, D_FF, D_MODEL), D_FF ** -0.5),
    }

def first_block(x, pre_mix_norm, post_mix_norm, pre_ffn_norm, post_ffn_norm, w_in, w_out,
              lru_conv_w, lru_conv_b, lru_wa, lru_ba, lru_wx, lru_bx, lru_lambda,
              gla_gate_w2, gla_gate_b, gla_norm, rel_bias, w_ffn_gate, w_ffn_up, w_ffn_down):
    for l in range(DEPTH):
        h = rms_norm(x, pre_mix_norm[l])
        mix = hybrid_mixer(h, w_in[l], lru_conv_w[l], lru_conv_b[l], lru_wa[l], lru_ba[l],
                           lru_wx[l], lru_bx[l], lru_lambda[l], gla_gate_w2[l], gla_gate_b[l],
                           gla_norm[l], rel_bias)
        x = x + rms_norm(mix @ w_out[l], post_mix_norm[l])
        h = rms_norm(x, pre_ffn_norm[l])
        f = (jax.nn.silu(h @ w_ffn_gate[l]) * (h @ w_ffn_up[l])) @ w_ffn_down[l]
        x = x + rms_norm(f, post_ffn_norm[l])
    return x


DEPTH_2 = 2

CHUNK = 64
N_A = DEPTH_2 // 2
N_B = DEPTH_2 - N_A
CONV_WIDTH = 3
N_HEADS = 16
HEAD_DIM = D_MODEL // N_HEADS
D_FF_2 = -(-8 * D_MODEL // (3 * 256)) * 256
Q_BLOCK = 128
N_MOD = 6
LN_EPS = 1e-5
DEEPNORM_ALPHA = (2.0 * DEPTH_2) ** 0.25
DEEPNORM_BETA = (8.0 * DEPTH_2) ** -0.25


def layer_norm(x, g, b):
    xf = x.astype(jnp.float32)
    mu = jnp.mean(xf, axis=-1, keepdims=True)
    var = jnp.mean(jnp.square(xf - mu), axis=-1, keepdims=True)
    y = (xf - mu) * lax.rsqrt(var + LN_EPS) * g + b
    return y.astype(x.dtype)

def modulate(x, shift, scale):
    return x * (1.0 + scale[:, None, :]) + shift[:, None, :]

def short_conv_mixer(h, w_in, conv_w, w_out):
    d = h.shape[-1]
    gb, gc, v = jnp.split(h @ w_in, 3, axis=-1)
    u = gc * v
    conv = lax.conv_general_dilated(
        u, conv_w[:, None, :].astype(u.dtype),
        window_strides=(1,), padding=[(CONV_WIDTH - 1, 0)],
        dimension_numbers=("NWC", "WIO", "NWC"), feature_group_count=d)
    return (gb * conv) @ w_out

def shared_kv(x, c, w_ada_kv, b_ada_kv, w_k, w_v, w_f, b_f):
    bsz, s, _ = x.shape
    kv_shift, kv_scale = jnp.split(jax.nn.silu(c) @ w_ada_kv + b_ada_kv, 2, axis=-1)
    h = modulate(x, kv_shift, kv_scale)
    k = (h @ w_k).reshape(bsz, s, N_HEADS, HEAD_DIM).transpose(0, 2, 1, 3)
    v = (h @ w_v).reshape(bsz, s, N_HEADS, HEAD_DIM).transpose(0, 2, 1, 3)
    log_f = jax.nn.log_sigmoid((h @ w_f + b_f).astype(jnp.float32))
    log_fcum = jnp.cumsum(log_f, axis=1).transpose(0, 2, 1)
    return k, v, log_fcum

def forgetting_attention(h, w_q, k, v, log_fcum, w_o):
    bsz, s, d = h.shape
    q = (h @ w_q).reshape(bsz, s, N_HEADS, HEAD_DIM).transpose(0, 2, 1, 3) * (HEAD_DIM ** -0.5)
    outs = []
    for i in range(s // Q_BLOCK):
        q0 = i * Q_BLOCK
        kend = q0 + Q_BLOCK
        qb = q[:, :, q0:kend]
        kb = k[:, :, :kend]
        vb = v[:, :, :kend]
        logits = jnp.einsum("bhqd,bhkd->bhqk", qb, kb, preferred_element_type=jnp.float32)
        logits = logits + log_fcum[:, :, q0:kend, None] - log_fcum[:, :, None, :kend]
        qpos = q0 + jnp.arange(Q_BLOCK)
        kpos = jnp.arange(kend)
        logits = jnp.where(kpos[None, :] <= qpos[:, None], logits, -jnp.inf)
        p = jax.nn.softmax(logits, axis=-1)
        outs.append(jnp.einsum("bhqk,bhkd->bhqd", p.astype(vb.dtype), vb))
    o = jnp.concatenate(outs, axis=2).transpose(0, 2, 1, 3).reshape(bsz, s, d)
    return o @ w_o

def swiglu(h, w_gate, w_up, w_down):
    return (jax.nn.silu(h @ w_gate) * (h @ w_up)) @ w_down

def second_inputs(seed: int = 0) -> dict:
    key = jax.random.key(seed)
    ks = jax.random.split(key, 24)
    D, F, H = D_MODEL, D_FF_2, N_HEADS
    nrm = lambda k, shape, scale: jax.random.normal(k, shape, jnp.float32) * scale
    return {
        "x": nrm(ks[0], (BATCH, SEQ, D), 1.0),
        "c": nrm(ks[1], (BATCH, D), 1.0),
        "w_ada": nrm(ks[2], (DEPTH_2, D, N_MOD * D), 0.5 * D ** -0.5),
        "b_ada": nrm(ks[3], (DEPTH_2, N_MOD * D), 0.02),
        "conv_w_in": nrm(ks[4], (N_A, D, 3 * D), D ** -0.5),
        "conv_w": nrm(ks[5], (N_A, CONV_WIDTH, D), CONV_WIDTH ** -0.5),
        "conv_w_out": nrm(ks[6], (N_A, D, D), DEEPNORM_BETA * D ** -0.5),
        "w_ada_kv": nrm(ks[7], (D, 2 * D), 0.5 * D ** -0.5),
        "b_ada_kv": nrm(ks[8], (2 * D,), 0.02),
        "w_k": nrm(ks[9], (D, D), D ** -0.5),
        "w_v": nrm(ks[10], (D, D), DEEPNORM_BETA * D ** -0.5),
        "w_f": nrm(ks[11], (D, H), D ** -0.5),
        "b_f": jax.random.uniform(ks[12], (H,), jnp.float32, 1.0, 5.0),
        "attn_w_q": nrm(ks[13], (N_B, D, D), D ** -0.5),
        "attn_w_o": nrm(ks[14], (N_B, D, D), DEEPNORM_BETA * D ** -0.5),
        "ffn_w_gate": nrm(ks[15], (DEPTH_2, D, F), D ** -0.5),
        "ffn_w_up": nrm(ks[16], (DEPTH_2, D, F), D ** -0.5),
        "ffn_w_down": nrm(ks[17], (DEPTH_2, F, D), DEEPNORM_BETA * F ** -0.5),
        "ln1_g": 1.0 + nrm(ks[18], (DEPTH_2, D), 0.02),
        "ln1_b": nrm(ks[19], (DEPTH_2, D), 0.02),
        "ln2_g": 1.0 + nrm(ks[20], (DEPTH_2, D), 0.02),
        "ln2_b": nrm(ks[21], (DEPTH_2, D), 0.02),
    }

def second_block(x, c, w_ada, b_ada, conv_w_in, conv_w, conv_w_out, w_ada_kv, b_ada_kv,
              w_k, w_v, w_f, b_f, attn_w_q, attn_w_o, ffn_w_gate, ffn_w_up, ffn_w_down,
              ln1_g, ln1_b, ln2_g, ln2_b):
    c_act = jax.nn.silu(c)
    k = v = log_fcum = None
    for l in range(DEPTH_2):
        sh1, sc1, g1, sh2, sc2, g2 = jnp.split(c_act @ w_ada[l] + b_ada[l], N_MOD, axis=-1)
        h = modulate(x, sh1, sc1)
        if l < N_A:
            y = short_conv_mixer(h, conv_w_in[l], conv_w[l], conv_w_out[l])
        else:
            if l == N_A:
                k, v, log_fcum = shared_kv(x, c, w_ada_kv, b_ada_kv, w_k, w_v, w_f, b_f)
            j = l - N_A
            y = forgetting_attention(h, attn_w_q[j], k, v, log_fcum, attn_w_o[j])
        x = layer_norm(DEEPNORM_ALPHA * x + g1[:, None, :] * y, ln1_g[l], ln1_b[l])
        h = modulate(x, sh2, sc2)
        y = swiglu(h, ffn_w_gate[l], ffn_w_up[l], ffn_w_down[l])
        x = layer_norm(DEEPNORM_ALPHA * x + g2[:, None, :] * y, ln2_g[l], ln2_b[l])
    return x


def setup_inputs(seed=0):
    out = dict(first_inputs(seed))
    for name, value in second_inputs(seed + 1).items():
        if name != "x":
            out[name + "_2"] = value
    return out


def reference(
    x, pre_mix_norm, post_mix_norm, pre_ffn_norm, post_ffn_norm, w_in, w_out, lru_conv_w,
    lru_conv_b, lru_wa, lru_ba, lru_wx, lru_bx, lru_lambda, gla_gate_w2, gla_gate_b, gla_norm,
    rel_bias, w_ffn_gate, w_ffn_up, w_ffn_down, c_2, w_ada_2, b_ada_2, conv_w_in_2, conv_w_2,
    conv_w_out_2, w_ada_kv_2, b_ada_kv_2, w_k_2, w_v_2, w_f_2, b_f_2, attn_w_q_2, attn_w_o_2,
    ffn_w_gate_2, ffn_w_up_2, ffn_w_down_2, ln1_g_2, ln1_b_2, ln2_g_2, ln2_b_2,
):
    x = first_block(
        x, pre_mix_norm, post_mix_norm, pre_ffn_norm, post_ffn_norm, w_in, w_out, lru_conv_w,
        lru_conv_b, lru_wa, lru_ba, lru_wx, lru_bx, lru_lambda, gla_gate_w2, gla_gate_b,
        gla_norm, rel_bias, w_ffn_gate, w_ffn_up, w_ffn_down,
    )
    return second_block(
        x, c_2, w_ada_2, b_ada_2, conv_w_in_2, conv_w_2, conv_w_out_2, w_ada_kv_2, b_ada_kv_2,
        w_k_2, w_v_2, w_f_2, b_f_2, attn_w_q_2, attn_w_o_2, ffn_w_gate_2, ffn_w_up_2,
        ffn_w_down_2, ln1_g_2, ln1_b_2, ln2_g_2, ln2_b_2,
    )


_drawn_inputs = setup_inputs


def setup_inputs(seed=0):
    import zlib

    import numpy as np

    out = dict(_drawn_inputs(seed))
    spreads = {}
    factors = {'post_mix_norm': 3.05,
     'pre_ffn_norm': 3.246,
     'post_ffn_norm': 4.436,
     'lru_ba': 64.0,
     'lru_bx': 44.181,
     'gla_gate_b': 8.0,
     'gla_norm': 3.808,
     'w_ada_kv_2': 3.003,
     'b_ada_kv_2': 8.0,
     'w_k_2': 4.225,
     'w_f_2': 8.0,
     'b_f_2': 6.888,
     'attn_w_q_2': 4.186}
    for name, (base, spread) in spreads.items():
        noise = np.random.default_rng([zlib.crc32(name.encode()), seed]).standard_normal(out[name].shape)
        drawn = base * np.exp(spread * noise) if base else spread * noise
        out[name] = __import__('jax').numpy.asarray(drawn.astype(out[name].dtype))
    for name, factor in factors.items():
        out[name] = (out[name] * factor).astype(out[name].dtype)
    return out
```

```python
import math

import numpy as np

import concourse.bass as bass
from concourse import mybir
from concourse.alu_op_type import AluOpType as ALU

F32 = mybir.dt.float32
F32R = mybir.dt.float32r
BF16 = mybir.dt.bfloat16
ACT = mybir.ActivationFunctionType
AX = mybir.AxisListType

P = 128
S = 256
NT = S // P
D = 1024
KB = D // P
DFF = 2816
COLS = 256
TURNS = DFF // COLS
SLOT = KB * COLS
NRAW, NHL, NADA = 6, 3, 2
AHEAD = 2
RMS_EPS, LN_EPS = 1e-6, 1e-5
DEEPNORM_ALPHA = 4.0 ** 0.25
NEG = -1.0e30
LRU, GLA_V, GLA_QK, RANK, MOBA = 256, 256, 128, 16, 512
OFF = dict(zip(("lru_x", "lru_g", "gq", "gk", "gv", "g_lr", "g_out", "mq", "mk", "mv"),
               np.cumsum([0, LRU, LRU, GLA_QK, GLA_QK, GLA_V, RANK, GLA_V, MOBA, MOBA]).tolist()))
CHUNK = 64
FOX_HEADS, DH = 16, 64


class Track:

    def __init__(self, nc, engine, name):
        self.engine, self.sem, self.n = engine, nc.alloc_semaphore(name), 0

    def __call__(self, instruction):
        instruction.then_inc(self.sem, 1)
        self.n += 1
        return (self.sem, self.n)

    def wait(self, *tokens):
        for token in tokens:
            if token is not None:
                self.engine.wait_ge(*token)


def build(nc, t):
    pe, act, dve, pool, sp = nc.tensor, nc.scalar, nc.vector, nc.gpsimd, nc.sync
    PE, AC, DV, PO = (Track(nc, e, n) for e, n in ((pe, "pe_done"), (act, "act_done"), (dve, "dve_done"), (pool, "pool_done")))

    def sb(name, shape, dt=F32):
        return nc.alloc_sbuf_tensor(name, list(shape), dt)

    raw = sb("raw", [P, NRAW, SLOT])
    hi = sb("hi", [P, NHL, SLOT], F32R)
    lo = sb("lo", [P, NHL, SLOT], F32R)
    ada_raw = sb("ada_raw", [P, NADA, SLOT])
    x_res = sb("x_res", [P, NT, D])
    xs_a = sb("xs_a", [P, KB, 2, S], F32R)
    xs_b = sb("xs_b", [P, KB, 2, S], F32R)
    half = sb("half", [P, 2, 2, S])
    WORK = 11264
    work = sb("work", [P, WORK])
    ident = sb("ident", [P, P])
    ones = sb("ones", [P, P])
    zeros16 = sb("zeros16", [P, 512], BF16)
    cols_a = sb("cols_a", [P, 88])
    cols_b = sb("cols_b", [P, 96])
    ada_cols = sb("ada_cols", [P, 14 * KB])
    c_act = sb("c_act", [P, KB])
    small = sb("small", [P, 160])
    w16 = sb("w16", [P, 3, KB, 16])
    w16h = sb("w16h", [P, KB, 16], F32R)
    w16l = sb("w16l", [P, KB, 16], F32R)
    ps = nc.alloc_psum_tensor("ps", [P, 8, 512], F32)

    def view(base, at, *shape):
        n = int(np.prod(shape))
        ap = base[:, at:at + n]
        if len(shape) == 2:
            ap = ap.rearrange("p (a b) -> p a b", a=shape[0])
        if len(shape) == 3:
            ap = ap.rearrange("p (a b c) -> p a b c", a=shape[0], b=shape[1])
        return ap

    lent = raw[:, 3:6, :].rearrange("p a n -> p (a n)")

    raw_landed = [nc.alloc_semaphore(f"raw_landed{j}") for j in range(NRAW)]
    s_hi, s_lo, s_used = (nc.alloc_semaphore(n) for n in ("s_hi", "s_lo", "s_used"))
    ada_landed = [nc.alloc_semaphore(f"ada_landed{j}") for j in range(NADA)]
    s_ada_used, s_ada_mul = nc.alloc_semaphore("s_ada_used"), nc.alloc_semaphore("s_ada_mul")

    loads = [0] * NRAW
    where = {}
    free = [[] for _ in range(NRAW)]
    next_place = 0
    loaded, split_next, ada_loaded, ada_next, ada_muls = 0, 0, 0, 0, 0

    def load(source, place=None):
        nonlocal loaded, next_place
        if place is None:
            place, next_place = next_place, (next_place + 1) % NRAW
        for token in free[place]:
            sp.wait_ge(*token)
        s = loaded
        loads[place] += 1
        dst = raw[:, place, :].rearrange("p (k n) -> p k n", k=source.shape[1])
        sp.dma_start(dst, source).then_inc(raw_landed[place], 16)
        where[s] = (place, 16 * loads[place])
        free[place] = [(s_lo, s + 1)]
        loaded += 1

    def split(s=None, place=None, landed=None, s_value=None):
        nonlocal split_next
        if s is None:
            s = s_value = split_next
            place, landed = where[s]
            split_next += 1
        h = s % NHL
        act.wait_ge(raw_landed[place], landed)
        if s >= NHL:
            act.wait_ge(s_used, s_value - NHL + 1)
        act.activation(hi[:, h, :], raw[:, place, :], ACT.Copy).then_inc(s_hi, 1)
        dve.wait_ge(s_hi, s_value + 1)
        dve.tensor_tensor(lo[:, h, :], raw[:, place, :], hi[:, h, :].bitcast(F32), ALU.subtract).then_inc(s_lo, 1)

    def f_source(w, col, n=COLS):
        return w.rearrange("(k p) n -> p k n", p=P)[:, :, col:col + n]

    def t_source(w, row):
        return w[row:row + 2 * P, :].rearrange("(k p) n -> p k n", p=P)

    def f_matmuls(h, bank, xs):
        for b in range(2):
            out = ps[:, bank + b, :]
            for k in range(KB):
                w = slice(k * COLS + b * P, k * COLS + b * P + P)
                if k:
                    pe.matmul(out[:, 0:S], lo[:, h, w], xs[:, k, 0, :], start=False, stop=False)
                last = pe.matmul(out, hi[:, h, w], xs[:, k, :, :].rearrange("p a n -> p (a n)"),
                                 start=(k == 0), stop=(k == KB - 1))
                if not k:
                    pe.matmul(out[:, 0:S], lo[:, h, w], xs[:, k, 0, :], start=False, stop=False)
        return last

    def t_matmuls(h, xs, k0, first, final):
        for tb in range(NT):
            tok = slice(tb * P, tb * P + P)
            for k in range(2):
                for half_, (xpart, wpart) in [(a, b) for b in ((0, hi), (0, lo), (1, hi)) for a in range(2)]:
                    w = wpart[:, h, k * D + half_ * 512:k * D + half_ * 512 + 512]
                    start = first and k == 0 and xpart == 0 and wpart is hi
                    stop = final and k == 1 and xpart == 1
                    last = pe.matmul(ps[:, 4 + 2 * tb + half_, :], xs[:, k0 + k, xpart, tok], w,
                                     start=start, stop=stop, skip_group_check=True)
        return last

    def v_matmuls(h, bank, xs):
        for tb in range(NT):
            out, tok = ps[:, bank, tb * S:tb * S + S], slice(tb * P, tb * P + P)
            for k in range(KB):
                w = slice(k * COLS, k * COLS + COLS)
                for n, (xpart, wpart) in enumerate(((0, hi), (0, lo), (1, hi))):
                    last = pe.matmul(out, xs[:, k, xpart, tok], wpart[:, h, w],
                                     start=(k == 0 and n == 0), stop=(k == KB - 1 and n == 2))
        return last

    gemm_next = 0

    def gemm(kind, *args):
        nonlocal gemm_next
        s = gemm_next
        gemm_next += 1
        while split_next <= min(s + AHEAD, loaded - 1):
            split()
        pe.wait_ge(s_lo, s + 1)
        kind(s % NHL, *args).then_inc(s_used, 1)
        return (s_used, s + 1)

    acc = view(work, 0, 6, D)

    def ada_source(w, col, part):
        return w[part * 2 * P:(part + 1) * 2 * P, :].rearrange("(k p) n -> p k n", p=P)[:, :, col:col + D]

    def ada_load(source):
        nonlocal ada_loaded
        q = ada_loaded
        if q >= NADA:
            sp.wait_ge(s_ada_used, q - NADA + 1)
        sp.dma_start(ada_raw[:, q % NADA, :].rearrange("p (k n) -> p k n", k=2), source).then_inc(ada_landed[q % NADA], 16)
        ada_loaded += 1

    def ada_multiply(dst, part, q_place, landed, muls):
        dve.wait_ge(ada_landed[q_place], landed)
        for k in range(2):
            w = ada_raw[:, q_place, k * D:(k + 1) * D]
            scalar = c_act[:, 2 * part + k:2 * part + k + 1]
            if part == 0 and k == 0:
                last = dve.tensor_scalar(dst, w, scalar, None, ALU.mult)
            else:
                dve.wait_ge(s_ada_mul, muls + k)
                last = dve.scalar_tensor_tensor(dst, w, scalar, dst, ALU.mult, ALU.add)
            last.then_inc(s_ada_mul, 1)
        dve.wait_ge(s_ada_mul, muls + 2)
        dve.sem_inc(s_ada_used, 1)

    def ada_step(index, part):
        nonlocal ada_next, ada_muls
        q = ada_next
        ada_multiply(acc[:, index, :], part, q % NADA, 16 * (q // NADA + 1), ada_muls)
        ada_next += 1
        ada_muls += 2

    def ada_finish(pairs, bank, *after):
        PE.wait((s_ada_mul, ada_muls), *after)
        for n, (chunk, index) in enumerate(pairs):
            for b in range(KB):
                last = pe.matmul(ps[:, bank, n * KB + b:n * KB + b + 1], acc[:, index, b * P:(b + 1) * P], ones[:, 0:1],
                                 start=True, stop=True)
        summed = PE(last)
        DV.wait(summed)
        tokens = []
        for n, (chunk, index) in enumerate(pairs):
            bias = {0: cols_b[:, 0:48], 1: cols_a[:, 67:83], 2: cols_b[:, 48:96]}[0 if chunk < 6 else 1 if chunk < 8 else 2]
            at = (chunk if chunk < 6 else chunk - 6 if chunk < 8 else chunk - 8) * KB
            dst = ada_cols[:, chunk * KB:(chunk + 1) * KB]
            tokens.append(DV(dve.tensor_tensor(dst, ps[:, bank, n * KB:(n + 1) * KB], bias[:, at:at + KB], ALU.add)))
            if chunk in (1, 4, 7, 9, 12):
                DV.wait(tokens[-1])
                tokens[-1] = DV(dve.tensor_scalar(dst, dst, 1.0, None, ALU.add))
        return tokens[-1]

    def spread(chunk, dst, scratch, bank, *after):
        DV.wait(*after)
        for b in range(KB):
            token = DV(dve.tensor_scalar(scratch[:, b * P:(b + 1) * P], ident[:, :], ada_cols[:, chunk * KB + b:chunk * KB + b + 1],
                                         None, ALU.mult))
        PE.wait(token)
        for b in range(KB):
            last = pe.matmul(ps[:, bank + b // 4, (b % 4) * P:(b % 4) * P + P], ones[:, :], scratch[:, b * P:(b + 1) * P],
                             start=True, stop=True)
        AC.wait(PE(last))
        return AC(act.activation(dst, ps[:, bank:bank + 2, :].rearrange("p a n -> p (a n)"), ACT.Copy))

    small_landed = [nc.alloc_semaphore(f"small_landed{n}") for n in range(8)]
    n_small = [0] * 8

    def small_load(engine, group, dst, src):
        engine.dma_start(dst, src).then_inc(small_landed[group], 16)
        n_small[group] += 16
        return (small_landed[group], n_small[group])

    rows_a, rows_b = view(work, 10240, P), view(work, 10368, P)
    row_at = {}
    at = 0
    for name, n in (("pre_mix_norm", 8), ("pre_ffn_norm", 8), ("c_2", 8), ("lru_conv_w", 8), ("lru_conv_b", 2),
                    ("lru_ba", 2), ("lru_bx", 2), ("lru_lambda", 2), ("gla_gate_b", 1), ("gla_norm", 2),
                    ("conv_w_2", 24), ("b_ada_kv_2", 16)):
        flat = t[name]
        while len(flat.shape) > 1:
            letters = "abcd"[:len(flat.shape)]
            flat = flat.rearrange(f"{' '.join(letters)} -> ({' '.join(letters)})")
        rows_in = small_load(act, 0, rows_a[at:at + n, :], flat.rearrange("(r p) -> r p", p=P))
        row_at[name] = at
        at += n
    n_rows = at
    rows_in = small_load(act, 0, rows_b[0:96, :], t["b_ada_2"].rearrange("l (r p) -> (l r) p", p=P))
    x_in = small_load(sp, 1, x_res[:, :, :], t["x"].rearrange("a (t p) n -> p (a t) n", p=P))
    w16_in = small_load(act, 2, w16[:, 0, :, :], t["w_in"][0].rearrange("(k p) n -> p k n", p=P)[:, :, OFF["g_lr"]:OFF["g_lr"] + RANK])
    w16_in = small_load(act, 2, w16[:, 1, :, :], t["w_f_2"].rearrange("(k p) n -> p k n", p=P))
    gate_w2 = small[0:RANK, 32:160]
    w16_in = small_load(act, 2, gate_w2, t["gla_gate_w2"][0])
    b_f = small[0:FOX_HEADS, 0:1]
    w16_in = small_load(act, 2, b_f, t["b_f_2"].rearrange("(h a) -> h a", a=1))
    onehot = view(work, 9216, S)[0:32, :]
    rel = view(work, 9472, 8)[0:32, :]
    rel_in = small_load(act, 3, onehot, t["bucket_onehot"])
    rel_in = small_load(act, 3, rel, t["rel_bias"])

    def col(name, n=0):
        return cols_a[:, row_at[name] + n:row_at[name] + n + 1]

    masks = sb("masks", [P, 264])
    gla_mask = masks[:, 0:128]
    head_ones = masks[:, 128:256]
    head_cols = masks[:, 256:260]
    pow_half = masks[:, 260:262]
    def serial(instruction):
        token = PO(instruction)
        PO.wait(token)
        return token

    serial(pool.memset(ident[:, :], 0.0))
    ident_ok = serial(pool.affine_select(out=ident[:, :], in_=ident[:, :], compare_op=ALU.not_equal, fill=1.0, base=0,
                                         pattern=[[-1, P]], channel_multiplier=1))
    serial(pool.memset(ones[:, :], 1.0))
    serial(pool.memset(pow_half, -0.5))
    serial(pool.memset(gla_mask, 1.0))
    serial(pool.memset(masks[:, 128:260], 0.0))
    serial(pool.memset(zeros16[:, :], 0.0))
    serial(pool.affine_select(out=gla_mask, in_=gla_mask, compare_op=ALU.is_ge, fill=0.0, base=0, pattern=[[1, P]],
                              channel_multiplier=-1))
    serial(pool.memset(gla_mask[0:64, 64:128], 0.0))
    for h in range(2):
        serial(pool.memset(head_ones[64 * h:64 * h + 64, 64 * h:64 * h + 64], 1.0))
    for h in range(4):
        masks_ok = serial(pool.memset(head_cols[32 * h:32 * h + 32, h:h + 1], 1.0))

    PE.wait(ident_ok, rows_in)
    pe.transpose(ps[:, 0, 0:n_rows], rows_a[0:n_rows, :], ident[0:n_rows, 0:n_rows])
    rows_t = PE(pe.transpose(ps[:, 1, 0:96], rows_b[0:96, :], ident[0:96, 0:96]))
    DV.wait(rows_t)
    cols_ok = DV(dve.tensor_copy(cols_a[:, 0:n_rows], ps[:, 0, 0:n_rows]))
    dve.tensor_copy(cols_b[:, :], ps[:, 1, 0:96])
    AC.wait(cols_ok)
    c_cols = cols_a[:, row_at["c_2"]:row_at["c_2"] + KB]
    c_sig = AC(act.activation(c_act[:, :], c_cols, ACT.Sigmoid))
    DV.wait(c_sig)
    c_ok = DV(dve.tensor_tensor(c_act[:, :], c_act[:, :], c_cols, ALU.mult))
    DV.wait(c_ok)

    table = view(work, 9728, 512)[0:8, :]
    t0 = serial(pool.memset(table, NEG))
    PE.wait(rel_in)
    bias_mm = PE(pe.matmul(ps[0:8, 2, 0:S], rel, onehot, start=True, stop=True))
    DV.wait(bias_mm, t0)
    table_ok = DV(dve.tensor_copy(table[:, 0:S], ps[0:8, 2, 0:S]))
    table_dram = t["bias_table"]
    pool.wait_ge(*table_ok)
    written = small_load(pool, 4, table_dram, table)
    pool.wait_ge(*written)
    moba_bias = view(work, 4096, 8, S)
    from_last = view(lent, 0, 8, S)
    toeplitz = bass.AP(tensor=table_dram.tensor, offset=table_dram.offset, ap=[[1, P], [512, 8], [1, S]])
    with nc.allow_non_contiguous_dma(reason="Toeplitz rows overlap"):
        bias_in = small_load(pool, 5, from_last, toeplitz)

    scr = [view(work, 6 * D + n * D, D) for n in range(2)]
    row_gain = [view(work, 8 * D + n * D, D) for n in range(3)]
    stats = small[:, 4:32]

    def rstd(mean_square, dst, eps, scale, *after):
        PO.wait(*after)
        a = PO(pool.tensor_scalar(dst, mean_square, scale, eps, ALU.mult, ALU.add))
        PO.wait(a)
        return PO(pool.tensor_tensor(dst, dst, pow_half[:, 0:dst.shape[1]], ALU.pow))

    half_free = [None, None]
    halves = [0]

    def next_half():
        halves[0] ^= 1
        return halves[0]

    def turn_over(source, ready, targets, bank_free):
        got = {}
        for tb in range(NT):
            PE.wait(ready[tb], *(bank_free if tb == 0 else ()))
            for k in range(KB):
                tr = pe.transpose(ps[:, k // 2, (k % 2) * S + tb * P:(k % 2) * S + tb * P + P], source[tb][:, k * P:(k + 1) * P], ident[:, :])
                if tb == NT - 1 and k % 2:
                    got[k // 2] = PE(tr)
        last, read = [], None
        for j in range(KB // 2):
            for dst, scale, shift in targets:
                h = next_half()
                DV.wait(got[j], half_free[h])
                for k in (2 * j, 2 * j + 1):
                    src = ps[:, j, (k % 2) * S:(k % 2) * S + S]
                    if shift is None:
                        token = DV(dve.tensor_scalar(half[:, h, k % 2, :], src, scale(k), None, ALU.mult))
                    else:
                        token = DV(dve.tensor_scalar(half[:, h, k % 2, :], src, scale(k), shift(k), ALU.mult, ALU.add))
                read = token
                last.append(split_into(dst, 2 * j, half[:, h, :, :], token))
                half_free[h] = last[-1]
        return last[-1], read

    def split_into(dst, k, source, ready, reader_done=()):
        AC.wait(ready, *reader_done)
        h_ok = AC(act.activation(dst[:, k:k + 2, 0, :], source, ACT.Copy))
        DV.wait(h_ok, ready)
        return DV(dve.tensor_tensor(dst[:, k:k + 2, 1, :], source, dst[:, k:k + 2, 0, :].bitcast(F32), ALU.subtract))

    def f_sum(bank, done, dst, *dst_free):
        h = next_half()
        AC.wait(done, half_free[h])
        low = AC(act.activation(half[:, h, :, :], ps[:, bank:bank + 2, S:2 * S], ACT.Copy))
        DV.wait(low, *dst_free)
        token = DV(dve.tensor_tensor(dst, ps[:, bank:bank + 2, 0:S], half[:, h, :, :], ALU.add))
        half_free[h] = token
        return token

    Y = [ps[:, 4 + 2 * tb:6 + 2 * tb, :].rearrange("p a n -> p (a n)") for tb in range(NT)]

    def add_rms(done, gain, gain_ok, scratch_free):
        out = []
        for tb in range(NT):
            ss, r = stats[:, tb:tb + 1], stats[:, 2 + tb:3 + tb]
            AC.wait(done, scratch_free)
            sq = AC(act.activation(scr[tb], Y[tb], ACT.Square, accum_out=ss))
            r_ok = rstd(ss, r, RMS_EPS, 1.0 / D, sq)
            DV.wait(r_ok, gain_ok)
            a = DV(dve.scalar_tensor_tensor(scr[tb], Y[tb], r, gain, ALU.mult, ALU.mult))
            DV.wait(a)
            out.append(DV(dve.tensor_tensor(x_res[:, tb, :], x_res[:, tb, :], scr[tb], ALU.add)))
        return out

    def normed(ready):
        out = []
        for tb in range(NT):
            ss, r = stats[:, 4 + tb:5 + tb], stats[:, 6 + tb:7 + tb]
            AC.wait(ready[tb])
            sq = AC(act.activation(scr[tb], x_res[:, tb, :], ACT.Square, accum_out=ss))
            r_ok = rstd(ss, r, RMS_EPS, 1.0 / D, sq)
            DV.wait(r_ok)
            out.append(DV(dve.tensor_scalar(scr[tb], x_res[:, tb, :], r, None, ALU.mult)))
        return out

    def add_ln(done, gate, gate_ok, gain, bias, rows_ok, scratch_free=None):
        out = []
        for tb in range(NT):
            b = stats[:, 8 + 10 * tb:18 + 10 * tb]
            DV.wait(done, gate_ok, scratch_free)
            a = DV(dve.tensor_tensor(scr[tb], Y[tb], gate, ALU.mult))
            DV.wait(a)
            z = DV(dve.scalar_tensor_tensor(scr[tb], x_res[:, tb, :], DEEPNORM_ALPHA, scr[tb], ALU.mult, ALU.add))
            DV.wait(z)
            bn = bn_tile[:, tb, :]
            dve.bn_stats(bn[:, 0:6], scr[tb][:, 0:512])
            b2 = DV(dve.bn_stats(bn[:, 6:12], scr[tb][:, 512:1024]))
            DV.wait(b2)
            ag = DV(dve.bn_aggr(bn[:, 12:14], bn[:, 0:12]))
            r_ok = rstd(bn[:, 13:14], bn[:, 14:15], LN_EPS, 1.0, ag)
            DV.wait(r_ok)
            c = DV(dve.tensor_scalar(scr[tb], scr[tb], bn[:, 12:13], bn[:, 14:15], ALU.subtract, ALU.mult))
            DV.wait(c, rows_ok)
            d = DV(dve.tensor_tensor(scr[tb], scr[tb], gain, ALU.mult))
            DV.wait(d)
            out.append(DV(dve.tensor_tensor(x_res[:, tb, :], scr[tb], bias, ALU.add)))
        return out

    bn_tile = sb("bn_tile", [P, NT, 16])

    def row_load(n, source, *after):
        for token in after:
            if token is not None:
                sp.wait_ge(*token)
        flat = bass.AP(tensor=source.tensor, offset=source.offset, ap=[[0, P], [1, D]])
        with nc.allow_non_contiguous_dma(reason="one row on all partitions"):
            return small_load(sp, 6, row_gain[n], flat)

    def scores(q, k, minus_f=None, *after):
        PE.wait(*after)
        for j in range(4):
            for tb, (at, n) in enumerate(((0, P), (P, S))):
                out = ps[:, 4 + j, at:at + n]
                last = pe.matmul(out, q(j)[:, tb * P:tb * P + P], k(j)[:, 0:n], start=True, stop=(minus_f is None))
                if minus_f is not None:
                    last = pe.matmul(out, minus_f[0](j), minus_f[1][:, 0:n], start=False, stop=True)
        return PE(last)

    def softmax(probs, tile, logits, done, *free_):
        DV.wait(done, *free_)
        for j in range(4):
            for tb, (at, n) in enumerate(((0, P), (P, S))):
                read = DV(logits(j, tb, probs[:, j, at:at + n], ps[:, 4 + j, at:at + n]))
        DV.wait(read)
        neg, total = tile[:, 0:8], tile[:, 8:16]
        for tb, (at, n) in enumerate(((0, P), (P, S))):
            m = DV(dve.tensor_reduce(neg[:, tb * 4:tb * 4 + 4], probs[:, :, at:at + n], AX.X, ALU.max))
        DV.wait(m)
        m = DV(dve.tensor_scalar(neg, neg, -1.0, None, ALU.mult))
        AC.wait(m)
        for j in range(4):
            for tb, (at, n) in enumerate(((0, P), (P, S))):
                e = AC(act.activation(probs[:, j, at:at + n], probs[:, j, at:at + n], ACT.Exp,
                                      bias=neg[:, tb * 4 + j:tb * 4 + j + 1], accum_out=total[:, tb * 4 + j:tb * 4 + j + 1]))
        DV.wait(e)
        r = DV(dve.reciprocal(total, total))
        DV.wait(r)
        for j in range(4):
            for tb, (at, n) in enumerate(((0, P), (P, S))):
                p_ok = DV(dve.tensor_scalar(probs[:, j, at:at + n], probs[:, j, at:at + n],
                                            total[:, tb * 4 + j:tb * 4 + j + 1], None, ALU.mult))
        return p_ok

    def turn_probs(probs, probs_t, ready, *free_):
        PE.wait(ready)
        for j in range(4):
            for c in range(3):
                tr = pe.transpose(ps[:, 4 + j, c * P:(c + 1) * P], probs[:, j, c * P:(c + 1) * P], ident[:, :])
            tok = PE(tr)
            AC.wait(tok, *free_)
            last = AC(act.activation(probs_t[:, j, :], ps[:, 4 + j, 0:384], ACT.Copy))
        return last

    def weigh(probs_t, values, dst, k, ready, *after):
        PE.wait(ready, *after)
        for j in range(4):
            out = ps[64 * (j % 2):64 * (j % 2) + 64, 4, (j // 2) * S:(j // 2) * S + S]
            pe.matmul(out, values(0, j), probs_t[:, j, 0:S], start=True, stop=False, skip_group_check=True)
            last = pe.matmul(out[:, P:S], values(1, j), probs_t[:, j, S:S + P], start=False, stop=True, skip_group_check=True)
        return split_into(dst, k, ps[:, 4, :].rearrange("p (a n) -> p a n", a=2), PE(last))

    w_in, w_out = t["w_in"][0], t["w_out"][0]
    order = ["mq0", "mk0", "mv0", "qk", "mq1", "mk1", "lx", "mv1", "gv", "lg", "go"]
    at_col = {"mq0": OFF["mq"], "mk0": OFF["mk"], "mv0": OFF["mv"], "mq1": OFF["mq"] + COLS, "mk1": OFF["mk"] + COLS,
              "mv1": OFF["mv"] + COLS, "qk": OFF["gq"], "gv": OFF["gv"], "lx": OFF["lru_x"], "lg": OFF["lru_g"], "go": OFF["g_out"]}
    for n, name in enumerate(order):
        load(f_source(w_in, at_col[name]), n % 3)
        if n in (3, 5, 7, 9):
            ada_load(ada_source(t["w_ada_2"][0], 0, (n - 3) // 2))
    out_rows = [512, 768, 0, 256]
    for n, row in enumerate(out_rows):
        load(t_source(w_out, row), (len(order) + n) % 3)

    mq, mk = view(work, 1024, 4, S), view(work, 2048, 4, S)
    mv = view(work, 3072, NT, MOBA)
    probs, probs_t = view(work, 6144, 4, 384), view(work, 7680, 4, 384)
    gqk, gout, gv, lru_g = (view(work, 9216 + 512 * n, 2, S) for n in range(4))
    xpad = view(lent, 0, 2, S + 3)
    xc = view(lent, 520, 2, S)
    ri = view(lent, 1032, 4, S)
    aa, uu, hh, tt = (view(lent, 2056 + 512 * n, 2, S) for n in range(4))
    zz, ee, cum, qd = (view(lent, 4104 + 256 * n, S) for n in range(4))
    kd = view(work, 6144, 4, S)
    klast_t = view(work, 7168, NT, P)
    attn = view(work, 1024, 8, P)
    state = view(work, 2048, 3, S)
    oo, osq = view(work, 7424, 2, S), view(work, 7936, 2, S)
    soft = sb("soft", [P, 16])
    wab = view(lent, 5128, 4, P)
    serial(pool.memset(wab, 0.0))
    for g in range(4):
        part = slice(64 * (g % 2), 64 * (g % 2) + 64)
        small_load(pool, 7, wab[part, g // 2, part], t["lru_wa"][0, g])
        wab_in = small_load(pool, 7, wab[part, 2 + g // 2, part], t["lru_wx"][0, g])

    def flip_bias():
        flip = view(work, 1024, P)
        f = PO(pool.memset(flip, 0.0)); PO.wait(f)
        f = PO(pool.affine_select(out=flip, in_=flip, compare_op=ALU.not_equal, fill=1.0, base=1 - P, pattern=[[1, P]],
                                  channel_multiplier=1))
        PE.wait(f, bias_in)
        for n in range(4):
            last = pe.matmul(ps[:, 4 + n, :], flip, from_last[:, 2 * n:2 * n + 2, :].rearrange("p a n -> p (a n)"), start=True, stop=True)
        AC.wait(PE(last))
        return AC(act.activation(moba_bias.rearrange("p a n -> p (a n)"), ps[:, 4:8, :].rearrange("p a n -> p (a n)"), ACT.Copy))

    x_ready = normed([x_in, x_in])
    h_ok, t_read = turn_over(scr, x_ready, [(xs_a, lambda k: col("pre_mix_norm", k), None)], [cols_ok, table_ok])
    xs_ready = h_ok
    bias_ok = flip_bias()

    bank_free = {0: t_read, 2: t_read, 4: None}
    which = [0]

    def project(dst, xs, *dst_free):
        which[0] ^= 2
        b = which[0]
        PE.wait(xs_ready, bank_free[b])
        token = f_sum(b, gemm(f_matmuls, b, xs), dst, *dst_free)
        bank_free[b] = token
        return token

    def project_v(dst, xs, *dst_free):
        which[0] ^= 2
        b = which[0]
        PE.wait(xs_ready, bank_free[b])
        done = gemm(v_matmuls, b, xs)
        DV.wait(done, *dst_free)
        token = DV(dve.tensor_copy(dst, ps[:, b, :].rearrange("p (a n) -> p a n", a=NT)))
        bank_free[b] = token
        return token

    def head(tile, j0):
        return lambda j: tile[64 * (j % 2):64 * (j % 2) + 64, (j0 + j) // 2, :]

    def moba_logits(g):
        def write(j, tb, out, s_):
            b = moba_bias[:, 4 * g + j, :] if tb else moba_bias[:, 4 * g + j, P:S]
            return dve.scalar_tensor_tensor(out, s_, DH ** -0.5, b, ALU.mult, ALU.add)
        return write

    def values(tile, j0):
        return lambda kb, j: tile[:, kb, 64 * (j0 + j):64 * (j0 + j) + 64]

    def product16(n, xs, ready, bank, dst):
        AC.wait(w16_in, ready)
        a = AC(act.activation(w16h[:, :, :], w16[:, n, :, :], ACT.Copy))
        DV.wait(a)
        b = DV(dve.tensor_tensor(w16l[:, :, :], w16[:, n, :, :], w16h[:, :, :].bitcast(F32), ALU.subtract))
        PE.wait(b, bank_free[bank], ready)
        for tb in range(NT):
            out, tok = ps[:, bank, tb * 16:tb * 16 + 16], slice(tb * P, tb * P + P)
            for k in range(KB):
                for m, (xpart, w) in enumerate(((0, w16h), (0, w16l), (1, w16h))):
                    last = pe.matmul(out, xs[:, k, xpart, tok], w[:, k, :], start=(k == 0 and m == 0), stop=(k == KB - 1 and m == 2))
        DV.wait(PE(last))
        c = DV(dve.tensor_copy(w16[:, 2, 0:NT, :], ps[:, bank, 0:NT * 16].rearrange("p (a n) -> p a n", a=NT)))
        PE.wait(c)
        for tb in range(NT):
            last = pe.transpose(ps[0:16, bank, 64 + tb * P:64 + tb * P + P], w16[:, 2, tb, :], ident[:, :])
        DV.wait(PE(last))
        token = DV(dve.tensor_copy(dst, ps[0:16, bank, 64:64 + S]))
        bank_free[bank] = token
        return token

    q_ok = project(mq[:, 0:2, :], xs_a, bias_ok)
    k_ok = project(mk[:, 0:2, :], xs_a)
    v_ok = project_v(mv[:, :, 0:COLS], xs_a)
    s_ok = scores(head(mq, 0), head(mk, 0), None, q_ok, k_ok, bias_ok)
    p_ok = softmax(probs, soft, moba_logits(0), s_ok, bias_ok)
    qk_ok = project(gqk, xs_a)
    glr = view(lent, 5640, S)[0:16, :]
    glr_ok = product16(0, xs_a, xs_ready, 0 if which[0] else 2, glr)
    ada_step(0, 0)
    q_ok = project(mq[:, 2:4, :], xs_a)
    pt_ok = turn_probs(probs, probs_t, p_ok)
    PE.wait(glr_ok)
    k_ok = project(mk[:, 2:4, :], xs_a)
    o_ok = weigh(probs_t, values(mv, 0), xs_b, 4, pt_ok, v_ok)
    bank_free[4] = o_ok
    s_ok = scores(head(mq, 4), head(mk, 4), None, q_ok, k_ok, o_ok)
    p_ok = softmax(probs, soft, moba_logits(1), s_ok)
    ada_step(0, 1)
    PO.wait(bias_ok)
    pz = serial(pool.memset(xpad[:, :, 0:3], 0.0))
    lx_ok = project(xpad[:, :, 3:], xs_a, pz)
    v_ok = project_v(mv[:, :, COLS:], xs_a)
    pt_ok = turn_probs(probs, probs_t, p_ok)
    ada_step(0, 2)

    def conv(dst, src, taps, weight, bias, ready, *free_):
        DV.wait(ready, *free_)
        for b in range(2):
            if bias is None:
                token = DV(dve.tensor_scalar(dst[:, b, :], src[:, b, 0:S], weight(0, b), None, ALU.mult))
            else:
                token = DV(dve.tensor_scalar(dst[:, b, :], src[:, b, 0:S], weight(0, b), bias(b), ALU.mult, ALU.add))
        for j in range(1, taps):
            DV.wait(token)
            for b in range(2):
                token = DV(dve.scalar_tensor_tensor(dst[:, b, :], src[:, b, j:j + S], weight(j, b), dst[:, b, :], ALU.mult, ALU.add))
        return token

    xc_ok = conv(xc, xpad, 4, lambda j, b: col("lru_conv_w", 2 * j + b), lambda b: col("lru_conv_b", b), lx_ok)
    gv_ok = project_v(gv, xs_a)
    o_ok = weigh(probs_t, values(mv, 4), xs_b, 6, pt_ok, v_ok)
    moba_done = o_ok

    PE.wait(xc_ok, wab_in, moba_done)
    for n in range(4):
        last = pe.matmul(ps[:, 5 + n // 2, (n % 2) * S:(n % 2) * S + S], wab[:, n, :], xc[:, n % 2, :], start=True, stop=True)
    gates = PE(last)
    PE.wait(glr_ok)
    gz = PE(pe.matmul(ps[:, 7, 0:S], gate_w2, glr, start=True, stop=True))
    AC.wait(gates)
    for n in range(4):
        ri_ok = AC(act.activation(ri[:, n, :], ps[:, 5 + n // 2, (n % 2) * S:(n % 2) * S + S], ACT.Sigmoid,
                                  bias=col("lru_ba" if n < 2 else "lru_bx", n % 2)))
    lam = cols_a[:, row_at["lru_lambda"]:row_at["lru_lambda"] + 2]
    sv = lambda n: soft2[:, 2 * n:2 * n + 2]
    soft2 = sb("soft2", [P, 16])
    AC.wait(cols_ok)
    a0 = AC(act.activation(sv(0), lam, ACT.Abs))
    AC.wait(a0)
    a1 = AC(act.activation(sv(0), sv(0), ACT.Exp, scale=-1.0))
    DV.wait(a1)
    a2 = DV(dve.tensor_scalar(sv(1), sv(0), 2.0, None, ALU.add)); DV.wait(a2)
    a2 = DV(dve.reciprocal(sv(1), sv(1))); DV.wait(a2)
    a2 = DV(dve.tensor_tensor(sv(1), sv(1), sv(0), ALU.mult)); DV.wait(a2)
    a2 = DV(dve.tensor_tensor(sv(2), sv(1), sv(1), ALU.mult)); DV.wait(a2)
    a2 = DV(dve.tensor_scalar(sv(3), sv(2), 1.0 / 17, 1.0 / 15, ALU.mult, ALU.add)); DV.wait(a2)
    for m in (13, 11, 9, 7, 5, 3, 1):
        a2 = DV(dve.tensor_tensor(sv(3), sv(3), sv(2), ALU.mult)); DV.wait(a2)
        a2 = DV(dve.tensor_scalar(sv(3), sv(3), 1.0 / m, None, ALU.add)); DV.wait(a2)
    a2 = DV(dve.tensor_tensor(sv(3), sv(3), sv(1), ALU.mult)); DV.wait(a2)
    a2 = DV(dve.tensor_scalar(sv(3), sv(3), 2.0, None, ALU.mult)); DV.wait(a2)
    a2 = DV(dve.tensor_scalar(sv(4), lam, -1.0, 0.0, ALU.mult, ALU.max)); DV.wait(a2)
    a2 = DV(dve.tensor_tensor(sv(3), sv(3), sv(4), ALU.add)); DV.wait(a2)
    sp_ok = DV(dve.tensor_scalar(sv(3), sv(3), 4.0, None, ALU.mult))
    AC.wait(sp_ok, ri_ok)
    for b in range(2):
        w_ok = AC(act.activation(tt[:, b, :], ri[:, b, :], ACT.Tanh, scale=sv(3)[:, b:b + 1]))
    DV.wait(w_ok)
    b1 = DV(dve.tensor_scalar(aa, tt, -1.0, 1.0, ALU.mult, ALU.add))
    b2 = DV(dve.tensor_scalar(hh, tt, 1.0, None, ALU.add)); DV.wait(b2)
    b3 = DV(dve.tensor_scalar(tt, tt, 1e-30, None, ALU.max))
    b4 = DV(dve.reciprocal(hh, hh)); DV.wait(b4)
    a_ok = DV(dve.tensor_tensor(aa, aa, hh, ALU.mult))
    AC.wait(b3)
    rt = AC(act.activation(tt, tt, ACT.Sqrt))
    DV.wait(rt, a_ok)
    b5 = DV(dve.scalar_tensor_tensor(uu, tt, 2.0, hh, ALU.mult, ALU.mult)); DV.wait(b5)
    b6 = DV(dve.memset(uu[:, :, 0:1], 1.0)); DV.wait(b6)
    b7 = DV(dve.tensor_tensor(xc, xc, ri[:, 2:4, :], ALU.mult)); DV.wait(b7)
    b8 = DV(dve.tensor_tensor(uu, uu, xc, ALU.mult)); DV.wait(b8)
    for b in range(2):
        h_ok = DV(dve.tensor_tensor_scan(hh[:, b, :], aa[:, b, :], uu[:, b, :], 0.0, ALU.mult, ALU.add))

    lg_ok = project(lru_g, xs_a)
    DV.wait(gz, cols_ok)
    c1 = DV(dve.tensor_scalar(zz, ps[:, 7, 0:S], col("gla_gate_b"), None, ALU.add))
    AC.wait(c1)
    c2 = AC(act.activation(ee, zz, ACT.Abs)); AC.wait(c2)
    c2 = AC(act.activation(ee, ee, ACT.Exp, scale=-1.0)); AC.wait(c2)
    c2 = AC(act.activation(ee, ee, ACT.Ln, bias=1.0))
    DV.wait(c1, c2)
    c3 = DV(dve.tensor_scalar(zz, zz, 0.0, 1.0 / 16, ALU.min, ALU.mult)); DV.wait(c3)
    c3 = DV(dve.scalar_tensor_tensor(zz, ee, -1.0 / 16, zz, ALU.mult, ALU.add)); DV.wait(c3, masks_ok)
    for c in range(S // CHUNK):
        part = slice(c * CHUNK, (c + 1) * CHUNK)
        cum_ok = DV(dve.tensor_tensor_scan(cum[:, part], ones[:, 0:CHUNK], zz[:, part], 0.0, ALU.mult, ALU.add))
    go_ok = project(gout, xs_a)
    AC.wait(cum_ok)
    e1 = AC(act.activation(ee, cum, ACT.Exp))
    DV.wait(e1, qk_ok)
    qd_ok = DV(dve.scalar_tensor_tensor(qd, gqk[:, 0, :], 32.0 ** -0.5, ee, ALU.mult, ALU.mult))
    AC.wait(qd_ok)
    e2 = AC(act.activation(ee, cum, ACT.Exp, scale=-1.0))
    DV.wait(e2, moba_done, pt_ok)
    e3 = DV(dve.tensor_tensor(zz, gqk[:, 1, :], ee, ALU.mult)); DV.wait(e3)
    for h in range(4):
        kd_ok = DV(dve.tensor_scalar(kd[:, h, :], zz, head_cols[:, h:h + 1], None, ALU.mult))
    last_cum = cum.rearrange("p (c n) -> p c n", n=CHUNK)[:, :, CHUNK - 1]
    AC.wait(kd_ok)
    for c in range(S // CHUNK):
        e4 = AC(act.activation(ee[:, c * CHUNK:(c + 1) * CHUNK], cum[:, c * CHUNK:(c + 1) * CHUNK], ACT.Exp, scale=-1.0,
                               bias=cum[:, (c + 1) * CHUNK - 1:(c + 1) * CHUNK]))
    decay = soft[:, 0:4]
    e5 = AC(act.activation(decay, last_cum, ACT.Exp))
    DV.wait(e4)
    kl_ok = DV(dve.tensor_tensor(zz, gqk[:, 1, :], ee, ALU.mult))
    PE.wait(kd_ok, qd_ok)
    for h in range(4):
        for pr in range(2):
            n = 2 * h + pr
            last = pe.matmul(ps[:, 4 + n // 4, (n % 4) * P:(n % 4) * P + P], kd[:, h, pr * P:(pr + 1) * P], qd[:, pr * P:(pr + 1) * P],
                             start=True, stop=True)
    at_ok = PE(last)
    PE.wait(kl_ok, ri_ok)
    for tb in range(NT):
        last = pe.transpose(ps[:, 6, tb * P:(tb + 1) * P], zz[:, tb * P:(tb + 1) * P], ident[:, :])
    kt = PE(last)
    DV.wait(at_ok)
    for n in range(2):
        am_ok = DV(dve.tensor_tensor(attn[:, 4 * n:4 * n + 4, :], ps[:, 4 + n, :].rearrange("p (a n) -> p a n", a=4),
                                     gla_mask[:, None, :].to_broadcast([P, 4, P]), ALU.mult))
    DV.wait(kt)
    klt_ok = DV(dve.tensor_copy(klast_t, ps[:, 6, 0:S].rearrange("p (a n) -> p a n", a=NT)))
    PE.wait(klt_ok, gv_ok, am_ok)
    for c in range(3):
        rows = slice(64 * (c % 2), 64 * (c % 2) + 64)
        last = pe.matmul(ps[:, (6, 7, 4)[c], 0:S] if c != 1 else ps[:, 7, S:2 * S], klast_t[rows, c // 2, :], gv[rows, c // 2, :], start=True, stop=True)
    kv_ok = PE(last)
    kvs = [ps[:, 6, 0:S], ps[:, 7, S:2 * S], ps[:, 4, 0:S]]
    DV.wait(kv_ok, e5)
    f0 = DV(dve.tensor_copy(state[:, 0, :], kvs[0])); DV.wait(f0)
    for c in (1, 2):
        f0 = DV(dve.scalar_tensor_tensor(state[:, c, :], state[:, c - 1, :], decay[:, c:c + 1], kvs[c], ALU.mult, ALU.add)); DV.wait(f0)
    for h in range(4):
        part = state[:, :, 64 * h:64 * h + 64]
        st_ok = DV(dve.tensor_scalar(part, part, head_cols[:, h:h + 1], None, ALU.mult))
    PE.wait(st_ok, am_ok)
    first = True
    for hp in range(2):
        for c in range(1, 4):
            pe.matmul(ps[:, 5, hp * S + c * CHUNK:hp * S + (c + 1) * CHUNK], state[:, c - 1, hp * P:(hp + 1) * P],
                      qd[:, c * CHUNK:(c + 1) * CHUNK], start=first, stop=False, skip_group_check=True)
            first = False
    for h in range(4):
        for pr in range(2):
            last = pe.matmul(ps[64 * (h % 2):64 * (h % 2) + 64, 5, (h // 2) * S + pr * P:(h // 2) * S + (pr + 1) * P],
                             gv[:, pr, 64 * h:64 * h + 64], attn[:, 2 * h + pr, :], start=False, stop=True, skip_group_check=True)
    og = PE(last)
    AC.wait(og)
    g1 = AC(act.activation(oo, ps[:, 5, :].rearrange("p (a n) -> p a n", a=2), ACT.Copy))
    g2 = AC(act.activation(osq, ps[:, 5, :].rearrange("p (a n) -> p a n", a=2), ACT.Square))
    PE.wait(g2)
    g3 = PE(pe.matmul(ps[:, 6, :], head_ones, osq.rearrange("p a n -> p (a n)"), start=True, stop=True))
    DV.wait(g3)
    g4 = DV(dve.tensor_scalar(osq, ps[:, 6, :].rearrange("p (a n) -> p a n", a=2), 1.0 / 64, RMS_EPS, ALU.mult, ALU.add))
    AC.wait(g4)
    g5 = AC(act.activation(osq, osq, ACT.Sqrt))
    DV.wait(g5)
    g6 = DV(dve.reciprocal(osq, osq))
    DV.wait(g6, g1)
    g7 = DV(dve.tensor_tensor(oo, oo, osq, ALU.mult)); DV.wait(g7)
    for b in range(2):
        g8 = DV(dve.tensor_scalar(oo[:, b, :], oo[:, b, :], col("gla_norm", b), None, ALU.mult))
    AC.wait(go_ok)
    AC.wait(g8)
    g9 = AC(act.activation(osq, gout, ACT.Sigmoid))
    DV.wait(g9, g8)
    g10 = DV(dve.tensor_tensor(osq, osq, gout, ALU.mult)); DV.wait(g10)
    g11 = DV(dve.tensor_tensor(oo, oo, osq, ALU.mult))
    gla_ok = split_into(xs_b, 2, oo, g11)
    DV.wait(lg_ok)
    k1 = DV(dve.tensor_tensor(uu, lru_g, lru_g, ALU.mult)); DV.wait(k1)
    k1 = DV(dve.tensor_scalar(uu, uu, 0.044715, 1.0, ALU.mult, ALU.add)); DV.wait(k1)
    k1 = DV(dve.tensor_tensor(uu, uu, lru_g, ALU.mult))
    AC.wait(k1)
    k2 = AC(act.activation(uu, uu, ACT.Sigmoid, scale=2.0 * math.sqrt(2.0 / math.pi)))
    DV.wait(k2, h_ok)
    k3 = DV(dve.tensor_tensor(hh, hh, lru_g, ALU.mult)); DV.wait(k3)
    k4 = DV(dve.tensor_tensor(hh, hh, uu, ALU.mult))
    lru_ok = split_into(xs_b, 0, hh, k4)
    ada_step(0, 3)

    PE.wait(gla_ok)
    for n, k0 in enumerate((4, 6, 0, 2)):
        PE.wait(lru_ok)
        done = gemm(t_matmuls, xs_b, k0, n == 0, n == 3)
    for place in (3, 4, 5):
        free[place] = [lru_ok, gla_ok]
    next_place = 3

    def row_pair(names, after):
        tok = None
        for n, src in names:
            tok = row_load(n, src, after)
        return tok

    rows_ok = row_load(0, t["post_mix_norm"][0], gla_ok)
    ready = add_rms(done, row_gain[0], rows_ok, g11)
    ready = normed(ready)
    h_ok, t_read = turn_over(scr, ready, [(xs_a, lambda k: col("pre_ffn_norm", k), None)], [bank_free[0], bank_free[2]])

    names = ("gate_mm", "up_mm", "gate_low", "gate_sum", "gate_sig", "silu_ok", "up_low", "up_sum", "h_ok", "h_hi", "h_lo")
    F = {n: nc.alloc_semaphore("ffn_" + n) for n in names}
    s_down = nc.alloc_semaphore("ffn_down_mm")
    hs = xs_b[:, :, :, :].rearrange("p (u k) a n -> p u k a n", u=4)[:, 0:2]
    gg = view(work, 6 * D, 2, 2, S)
    sig_tile = view(work, 7 * D, 2, S)

    def feed_forward(number, w_gate, w_up, w_down, ready, bank_tokens, ada):
        nonlocal loaded, next_place, split_next, gemm_next, ada_loaded, ada_next, ada_muls
        base, s0, p0 = number * TURNS, loaded, next_place
        assert s0 == gemm_next
        wg = w_gate.rearrange("(k p) n -> p k n", p=P)
        wu = w_up.rearrange("(k p) n -> p k n", p=P)

        def gate_part(turn, s, u):
            for name, bank, before, d in (("gate_mm", 0, "gate_sum", 0), ("up_mm", 2, "up_sum", 1)):
                pe.wait_ge(s_lo, s[1] + d + 1)
                if turn is not 0:
                    pe.wait_ge(F[before], base + turn)
                f_matmuls((s[0] + d) % NHL, bank, xs_a).then_inc(s_used, 1)

        def hidden(turn, s, u):
            n = turn + (base + 1)
            for name, d, bank in (("gate", 0, 0), ("up", 1, 2)):
                act.wait_ge(s_used, s[1] + d + 1)
                if turn is not 0:
                    act.wait_ge(F[name + "_sum"], base + turn)
                act.activation(half[:, d, :, :], ps[:, bank:bank + 2, S:2 * S], ACT.Copy).then_inc(F[name + "_low"], 1)
                dve.wait_ge(F[name + "_low"], n)
                if turn is not 0:
                    dve.wait_ge(F["h_lo"], base + turn)
                dve.tensor_tensor(gg[:, d, :, :], ps[:, bank:bank + 2, 0:S], half[:, d, :, :], ALU.add).then_inc(F[name + "_sum"], 1)
                if d == 0:
                    act.wait_ge(F["gate_sum"], n)
                    act.activation(sig, gg[:, 0, :, :], ACT.Sigmoid).then_inc(F["gate_sig"], 1)
                    dve.wait_ge(F["gate_sig"], n)
                    dve.wait_ge(F["gate_sum"], n)
                    dve.tensor_tensor(gg[:, 0, :, :], gg[:, 0, :, :], sig, ALU.mult).then_inc(F["silu_ok"], 1)
                    yield
            dve.wait_ge(F["up_sum"], n)
            dve.wait_ge(F["silu_ok"], n)
            dve.tensor_tensor(gg[:, 1, :, :], gg[:, 0, :, :], gg[:, 1, :, :], ALU.mult).then_inc(F["h_ok"], 1)
            act.wait_ge(F["h_ok"], n)
            act.activation(hs[:, u, :, 0, :], gg[:, 1, :, :], ACT.Copy).then_inc(F["h_hi"], 1)
            dve.wait_ge(F["h_hi"], n)
            dve.tensor_tensor(hs[:, u, :, 1, :], gg[:, 1, :, :], hs[:, u, :, 0, :].bitcast(F32), ALU.subtract).then_inc(F["h_lo"], 1)
            yield

        def down_part(turn, s, u):
            pe.wait_ge(s_lo, s[1] + 1)
            pe.wait_ge(F["h_lo"], turn + (base + 1))
            t_matmuls(s[0] % NHL, hs[:, u], 0, False, False).then_inc(s_used, 1)

        sig = sig_tile

        for w in (wg, wu):
            load(w[:, :, 0:COLS])
        for token in (ready, *bank_tokens):
            PE.wait(token)
        for n in range(4):
            last = pe.matmul(ps[:, 4 + n, :], zeros16[:, 0:P], zeros16[:, :], start=True, stop=False, skip_group_check=True)
        s = (s0, s0)
        while split_next < s0 + AHEAD:
            split()
        gate_part(0, s, 0)
        parts = hidden(0, s, 0)
        next(parts)
        next(parts)
        loop_s, loop_split = s0 + 2, s0 + 2
        place_of = lambda n: (n - s0 + p0) % NRAW
        count = {}
        for n in range(6):
            count[place_of(loop_s + n)] = 16 * (loads[place_of(loop_s + n)] + 1)
        with nc.Fori(0, (TURNS - 1) // 2, 1) as i:
            s_reg = i * 6 + loop_s
            for n in range(6):
                turn_col = (i * 2 + (1 + n // 3)) * COLS
                place = place_of(loop_s + n)
                if n % 3 < 2:
                    src = (wg, wu)[n % 3][:, :, bass.ds(turn_col, COLS)]
                else:
                    src = w_down[bass.ds(turn_col - COLS, COLS), :].rearrange("(k p) n -> p k n", p=P)
                sp.wait_ge(s_lo, s_reg + (n - NRAW + 1))
                sp.dma_start(raw[:, place, :].rearrange("p (k n) -> p k n", k=src.shape[1]), src).then_inc(raw_landed[place], 16)
                if ada is not None and n in (0, 2, 3, 5):
                    part = (0, 2, 3, 5).index(n)
                    q = ada_loaded + part
                    src = ada[part * 2 * P:(part + 1) * 2 * P, bass.ds(i * D + D, D)].rearrange("(k p) n -> p k n", p=P)
                    sp.wait_ge(s_ada_used, i * 4 + (q - NADA + 1))
                    sp.dma_start(ada_raw[:, q % NADA, :].rearrange("p (k n) -> p k n", k=2), src).then_inc(ada_landed[q % NADA], 16)
            for v in range(2):
                turn = i * 2 + (1 + v)
                s = (loop_s + 3 * v, s_reg + 3 * v)
                u = (1 + v) % 2
                parts = hidden(turn, s, u)

                def split_at(n):
                    n += 3 * v
                    place = place_of(loop_s + n)
                    split(loop_split + n, place, i * 16 + count[place], s_reg + n)

                def ada_at(part):
                    if ada is not None:
                        q = ada_next + part
                        ada_multiply(acc[:, bass.ds(i + 1, 1), :].rearrange("p a n -> p (a n)"), part, q % NADA,
                                     i * 32 + 16 * (q // NADA + 1), i * 8 + (ada_muls + 2 * part))

                split_at(0)
                split_at(1)
                gate_part(turn, s, u)
                split_at(2)
                ada_at(2 * v)
                next(parts)
                ada_at(2 * v + 1)
                next(parts)
                down_part(turn - 1, (s[0] + 2, s[1] + 2), 1 - u)
        n_it = (TURNS - 1) // 2
        for n in range(6):
            loads[place_of(loop_s + n)] += n_it
        loaded += 6 * n_it
        split_next += 6 * n_it
        gemm_next += 2 + 6 * n_it
        if ada is not None:
            ada_loaded += 4 * n_it
            ada_next += 4 * n_it
            ada_muls += 8 * n_it
        for place in range(NRAW):
            free[place] = [(s_lo, loaded)]
        next_place = place_of(loaded)
        load(w_down[DFF - COLS:DFF, :].rearrange("(k p) n -> p k n", p=P))

    def last_down(number):
        pe.wait_ge(F["h_lo"], (number + 1) * TURNS)
        done = gemm(t_matmuls, hs[:, (TURNS - 1) % 2], 0, False, True)
        return done

    feed_forward(0, t["w_ffn_gate"][0], t["w_ffn_up"][0], t["w_ffn_down"][0], h_ok, [*ready], t["w_ada_2"][0])
    rows_ok = row_load(0, t["post_ffn_norm"][0], ready[-1])
    conv_in = t["conv_w_in_2"][0]
    s_base = loaded

    conv_sources = [f_source(conv_in, third * D + j * COLS) for j in range(4) for third in (1, 2, 0)]
    conv_sources += [t_source(t["conv_w_out_2"][0], n * 2 * P) for n in range(4)]
    ada_sources = [ada_source(w, c, part) for w, c in ((t["w_ada_kv_2"], 0), (t["w_ada_kv_2"], D), (t["w_ada_2"][1], 0)) for part in range(4)]
    for src in conv_sources:
        load(src)
        if ada_sources:
            ada_load(ada_sources.pop(0))
    done = last_down(0)
    mods = ada_finish([(c, c) for c in range(6)], 0, (F["up_sum"], TURNS))
    ready = add_rms(done, row_gain[0], rows_ok, None)
    gate_ok = spread(2, row_gain[1], row_gain[2], 2, mods, (F["up_sum"], TURNS))

    def acol(chunk):
        return lambda k: ada_cols[:, chunk * KB + k:chunk * KB + k + 1]

    half_free[0] = half_free[1] = (F["up_sum"], TURNS)
    xs_ready, t_read = turn_over([x_res[:, tb, :] for tb in range(NT)], ready, [(xs_a, acol(1), acol(0))],
                                 [gate_ok, mods])
    bank_free.update({0: t_read, 2: t_read})
    cpad, cc_, vv_, bb_ = view(work, 3 * D, 2, S + 2), view(work, 3 * D + 520, 2, S), view(work, 3 * D + 1032, 2, S), view(work, 3 * D + 1544, 2, S)
    pz = None
    PO.wait(ready[-1], (s_ada_mul, ada_muls), mods)
    pz = serial(pool.memset(cpad[:, :, 0:2], 0.0))
    a_n = 0
    mixed = None
    for j in range(4):
        c_ok = project(cc_, xs_a, mixed, mods)
        ada_step(a_n // 4 if a_n // 4 < 3 else 0, a_n % 4); a_n += 1
        v_ok = project(vv_, xs_a, mixed)
        DV.wait(c_ok, v_ok, pz)
        u_ok = DV(dve.tensor_tensor(cpad[:, :, 2:], cc_, vv_, ALU.mult))
        ada_step(a_n // 4, a_n % 4); a_n += 1
        cv = conv(cc_, cpad, 3, lambda n, b: col("conv_w_2", 8 * n + 2 * j + b), None, u_ok)
        b_ok = project(bb_, xs_a, mixed)
        DV.wait(b_ok, cv)
        m_ok = DV(dve.tensor_tensor(bb_, bb_, cc_, ALU.mult))
        mixed = split_into(xs_b, 2 * j, bb_, m_ok)
        ada_step(a_n // 4, a_n % 4); a_n += 1
    rows_ok = row_load(0, t["ln1_g_2"][0], ready[-1])
    PE.wait(mixed, ready[-1])
    for n in range(4):
        done = gemm(t_matmuls, xs_b, 2 * n, n == 0, n == 3)
    mods = ada_finish([(6, 0), (7, 1), (8, 2)], 0, bank_free[0])
    rows_ok = row_load(2, t["ln1_b_2"][0], gate_ok)
    ready = add_ln(done, row_gain[1], gate_ok, row_gain[0], row_gain[2], rows_ok)
    h_ok, t_read = turn_over([x_res[:, tb, :] for tb in range(NT)], ready, [(xs_a, acol(4), acol(3))], [mods, bank_free[2]])
    gate_ok = spread(5, row_gain[1], row_gain[2], 2, h_ok, ready[-1])
    feed_forward(1, t["ffn_w_gate_2"][0], t["ffn_w_up_2"][0], t["ffn_w_down_2"][0], h_ok, [*ready, gate_ok], t["w_ada_2"][1])
    rows_ok = row_load(0, t["ln2_g_2"][0], ready[-1])
    rows_ok = row_load(2, t["ln2_b_2"][0], gate_ok)

    fox_sources = [f_source(t["w_k_2"], j * COLS) for j in range(4)] + [t_source(t["w_v_2"], j * 2 * P) for j in range(4)]
    fox_sources += [f_source(t["attn_w_q_2"][0], j * COLS) for j in range(4)] + [t_source(t["attn_w_o_2"][0], j * 2 * P) for j in range(4)]
    fox_base = loaded
    for n, src in enumerate(fox_sources):
        load(src, (n + 2) % 3)
    done = last_down(1)
    mods = ada_finish([(8 + c, c) for c in range(1, 6)], 0, (F["up_sum"], 2 * TURNS))
    ready = add_ln(done, row_gain[1], gate_ok, row_gain[0], row_gain[2], rows_ok)
    half_free[0] = half_free[1] = (F["up_sum"], 2 * TURNS)
    xs_ready, t_read = turn_over([x_res[:, tb, :] for tb in range(NT)], ready,
                                 [(xs_b, acol(7), acol(6)), (xs_a, acol(9), acol(8))], [mods])
    bank_free.update({0: t_read, 2: t_read})
    kT = view(lent, 0, KB, S)
    vN = view(lent, 2048, NT, D)
    qT = [view(lent, 4096 + 512 * n, 2, S) for n in range(2)]
    probs, probs_t = view(work, 0, 4, 384), view(work, 1536, 4, 384)
    sel = view(work, 3072, FOX_HEADS, P)[0:16]
    zf, ef, ff, nf = (view(work, 5120 + S * n, S)[0:16, :] for n in range(4))
    f_cols = small[:, 32:64]
    lent_free = (s_lo, fox_base)
    PO.wait(mods)
    z0 = PO(pool.memset(sel, 0.0)); PO.wait(z0)
    sel_ok = PO(pool.affine_select(out=sel, in_=sel, compare_op=ALU.not_equal, fill=1.0, base=0,
                                   pattern=[[1, FOX_HEADS], [0, P]], channel_multiplier=-1))
    causal = scr[1][:, 0:384]
    PO.wait(xs_ready)
    z1 = PO(pool.memset(causal, 0.0)); PO.wait(z1)
    serial(pool.affine_select(out=causal[:, 0:P], in_=causal[:, 0:P], compare_op=ALU.is_ge, fill=NEG, base=0, pattern=[[-1, P]],
                              channel_multiplier=1))
    causal_ok = PO(pool.affine_select(out=causal[:, P:], in_=causal[:, P:], compare_op=ALU.is_ge, fill=NEG, base=P,
                                      pattern=[[-1, S]], channel_multiplier=1))
    DV.wait(mods)
    zf_ok = product16(1, xs_b, xs_ready, 0, zf)
    DV.wait(zf_ok)
    c1 = DV(dve.tensor_scalar(zf, zf, b_f, None, ALU.add))
    AC.wait(c1)
    c2 = AC(act.activation(ef, zf, ACT.Abs)); AC.wait(c2)
    c2 = AC(act.activation(ef, ef, ACT.Exp, scale=-1.0)); AC.wait(c2)
    c2 = AC(act.activation(ef, ef, ACT.Ln, bias=1.0))
    DV.wait(c1, c2)
    c3 = DV(dve.tensor_scalar(zf, zf, 0.0, None, ALU.min)); DV.wait(c3)
    c3 = DV(dve.tensor_tensor(zf, zf, ef, ALU.subtract)); DV.wait(c3)
    c4 = DV(dve.memset(nf, 1.0)); DV.wait(c4)
    c5 = DV(dve.tensor_tensor_scan(ff, nf, zf, 0.0, ALU.mult, ALU.add)); DV.wait(c5)
    nf_ok = DV(dve.tensor_scalar(nf, ff, -1.0, None, ALU.mult))
    PE.wait(c5, bank_free[0])
    for tb in range(NT):
        last = pe.transpose(ps[:, 0, tb * 16:tb * 16 + 16], ff[:, tb * P:(tb + 1) * P], ident[0:16, 0:16])
    DV.wait(PE(last))
    fc_ok = DV(dve.tensor_copy(f_cols, ps[:, 0, 0:32]))
    bank_free[0] = fc_ok
    for j in range(4):
        k_ok = project(kT[:, 2 * j:2 * j + 2, :], xs_b, lent_free)
    PE.wait(ready[-1])
    for n in range(4):
        v_done = gemm(t_matmuls, xs_b, 2 * n, n == 0, n == 3)
    DV.wait(v_done)
    v_ok = DV(dve.tensor_copy(vN[:, 0, :], Y[0]))
    AC.wait(v_done, lent_free)
    v_ok2 = AC(act.activation(vN[:, 1, :], Y[1], ACT.Copy))
    DV.wait(v_ok2)
    o_ok = DV(dve.memset(soft[:, 0:1], 0.0))

    def fox_logits(g):
        def write(j, tb, out, s_):
            h = 4 * g + j
            c = causal[:, P:] if tb else causal[:, 0:P]
            return dve.scalar_tensor_tensor(out, s_, f_cols[:, tb * 16 + h:tb * 16 + h + 1], c, ALU.add, ALU.add)
        return write

    q_free = [None, None]
    PE.wait(sel_ok, nf_ok)
    for g in range(4):
        q_ok = project(qT[g % 2], xs_a, q_free[g % 2])
        DV.wait(q_ok)
        q_ok = DV(dve.tensor_scalar(qT[g % 2], qT[g % 2], DH ** -0.5, None, ALU.mult))
        s_ok = scores(lambda j: qT[g % 2][64 * (j % 2):64 * (j % 2) + 64, j // 2, :], lambda j: kT[64 * (j % 2):64 * (j % 2) + 64, 2 * g + j // 2, :],
                      (lambda j: sel[:, 4 * g + j, :], nf), q_ok, k_ok, o_ok)
        q_free[g % 2] = s_ok
        p_ok = softmax(probs, soft, fox_logits(g), s_ok, causal_ok)
        pt_ok = turn_probs(probs, probs_t, p_ok)
        o_ok = weigh(probs_t, values(vN, 4 * g), xs_b, 2 * g, pt_ok, o_ok)
    PE.wait(o_ok)
    for n in range(4):
        done = gemm(t_matmuls, xs_b, 2 * n, n == 0, n == 3)
    for place in (3, 4, 5):
        free[place] = [o_ok]
    next_place = 3
    rows_ok = row_load(0, t["ln1_g_2"][1], ready[-1])
    rows_ok = row_load(2, t["ln1_b_2"][1], ready[-1])
    gate_ok = spread(10, row_gain[1], scr[0], 0, ready[-1], bank_free[0], bank_free[2])
    ready = add_ln(done, row_gain[1], gate_ok, row_gain[0], row_gain[2], rows_ok, gate_ok)
    h_ok, t_read = turn_over([x_res[:, tb, :] for tb in range(NT)], ready, [(xs_a, acol(12), acol(11))], [gate_ok, bank_free[2]])
    gate_ok = spread(13, row_gain[1], scr[0], 2, h_ok, ready[-1])
    feed_forward(2, t["ffn_w_gate_2"][1], t["ffn_w_up_2"][1], t["ffn_w_down_2"][1], h_ok, [*ready, gate_ok], None)
    rows_ok = row_load(0, t["ln2_g_2"][1], ready[-1])
    rows_ok = row_load(2, t["ln2_b_2"][1], ready[-1])
    done = last_down(2)
    ready = add_ln(done, row_gain[1], gate_ok, row_gain[0], row_gain[2], rows_ok, gate_ok)
    s_out = nc.alloc_semaphore("s_out")
    out = t["out"].rearrange("a (t p) n -> p (a t) n", p=P)
    for tb in range(NT):
        sp.wait_ge(*ready[tb])
        sp.dma_start(out[:, tb, :], x_res[:, tb, :]).then_inc(s_out, 16)
    sp.wait_ge(s_out, 16 * NT)


_INS = ['x', 'pre_mix_norm', 'post_mix_norm', 'pre_ffn_norm', 'post_ffn_norm', 'w_in', 'w_out', 'lru_conv_w',
        'lru_conv_b', 'lru_wa', 'lru_ba', 'lru_wx', 'lru_bx', 'lru_lambda', 'gla_gate_w2', 'gla_gate_b', 'gla_norm',
        'rel_bias', 'w_ffn_gate', 'w_ffn_up', 'w_ffn_down', 'c_2', 'w_ada_2', 'b_ada_2', 'conv_w_in_2', 'conv_w_2',
        'conv_w_out_2', 'w_ada_kv_2', 'b_ada_kv_2', 'w_k_2', 'w_v_2', 'w_f_2', 'b_f_2', 'attn_w_q_2', 'attn_w_o_2',
        'ffn_w_gate_2', 'ffn_w_up_2', 'ffn_w_down_2', 'ln1_g_2', 'ln1_b_2', 'ln2_g_2', 'ln2_b_2']


def bucket_onehot():
    n = 255 - np.arange(S)
    nf = np.maximum(n, 1).astype(np.float32)
    large = 16 + (np.log(nf / np.float32(16)) / np.float32(math.log(128 / 16)) * np.float32(16)).astype(np.int32)
    bucket = np.where(n < 16, n, np.minimum(large, 31))
    return (np.arange(32)[:, None] == bucket[None, :]).astype(np.float32)


def kernel(**inputs):
    import numpy as _np
    import concourse.bacc as _bacc
    from concourse import mybir as _mybir
    from concourse.bass_utils import run_bass_kernel_spmd as _run

    nc = _bacc.Bacc("TRN2", target_bir_lowering=False, num_devices=1)
    arrays, t = {}, {}
    for name in _INS:
        a = _np.ascontiguousarray(inputs[name])
        arrays[f"in_{name}"] = a
        t[name] = nc.dram_tensor(f"in_{name}", a.shape, _mybir.dt.from_np(a.dtype), kind="ExternalInput").ap()
    arrays["bucket_onehot"] = bucket_onehot()
    t["bucket_onehot"] = nc.dram_tensor("bucket_onehot", (32, S), _mybir.dt.float32, kind="ExternalInput").ap()
    t["bias_table"] = nc.dram_tensor("bias_table", (8, 512), _mybir.dt.float32, kind="Internal").ap()
    t["out"] = nc.dram_tensor("out_0", (1, S, D), _mybir.dt.float32, kind="ExternalOutput").ap()
    build(nc, t)
    r = _run(nc, [arrays], core_ids=[0])
    return r.results[0]["out_0"]
```

```python
import math

import numpy as np

import concourse.bass as bass
from concourse import mybir
from concourse.alu_op_type import AluOpType as ALU

F32 = mybir.dt.float32
F32R = mybir.dt.float32r
BF16 = mybir.dt.bfloat16
ACT = mybir.ActivationFunctionType
AX = mybir.AxisListType

P = 128
S = 256
NT = S // P
D = 1024
KB = D // P
DFF = 2816
COLS = 256
TURNS = DFF // COLS
SLOT = KB * COLS
NRAW, NHL, NADA = 6, 3, 2
AHEAD = 2
RMS_EPS, LN_EPS = 1e-6, 1e-5
DEEPNORM_ALPHA = 4.0 ** 0.25
NEG = -1.0e30
LRU, GLA_V, GLA_QK, RANK, MOBA = 256, 256, 128, 16, 512
OFF = dict(zip(("lru_x", "lru_g", "gq", "gk", "gv", "g_lr", "g_out", "mq", "mk", "mv"),
               np.cumsum([0, LRU, LRU, GLA_QK, GLA_QK, GLA_V, RANK, GLA_V, MOBA, MOBA]).tolist()))
CHUNK = 64
FOX_HEADS, DH = 16, 64


class Track:

    def __init__(self, nc, engine, name):
        self.engine, self.sem, self.n = engine, nc.alloc_semaphore(name), 0

    def __call__(self, instruction):
        instruction.then_inc(self.sem, 1)
        self.n += 1
        return (self.sem, self.n)

    def wait(self, *tokens):
        for token in tokens:
            if token is not None:
                self.engine.wait_ge(*token)


def build(nc, t):
    pe, act, dve, pool, sp = nc.tensor, nc.scalar, nc.vector, nc.gpsimd, nc.sync
    PE, AC, DV, PO = (Track(nc, e, n) for e, n in ((pe, "pe_done"), (act, "act_done"), (dve, "dve_done"), (pool, "pool_done")))

    def sb(name, shape, dt=F32):
        return nc.alloc_sbuf_tensor(name, list(shape), dt)

    raw = sb("raw", [P, NRAW, SLOT])
    hi = sb("hi", [P, NHL, SLOT], F32R)
    lo = sb("lo", [P, NHL, SLOT], F32R)
    ada_raw = sb("ada_raw", [P, NADA, SLOT])
    x_res = sb("x_res", [P, NT, D])
    xs_a = sb("xs_a", [P, KB, 2, S], F32R)
    xs_b = sb("xs_b", [P, KB, 2, S], F32R)
    half = sb("half", [P, 2, 2, S])
    WORK = 11264
    work = sb("work", [P, WORK])
    ident = sb("ident", [P, P])
    ones = sb("ones", [P, P])
    zeros16 = sb("zeros16", [P, 512], BF16)
    cols_a = sb("cols_a", [P, 88])
    cols_b = sb("cols_b", [P, 96])
    cols_c = sb("cols_c", [P, 64])
    folded = sb("folded", [P, 2, 2, KB])
    ada_cols = sb("ada_cols", [P, 14 * KB])
    c_act = sb("c_act", [P, KB])
    small = sb("small", [P, 160])
    ps = nc.alloc_psum_tensor("ps", [P, 8, 512], F32)

    def view(base, at, *shape):
        n = int(np.prod(shape))
        ap = base[:, at:at + n]
        if len(shape) == 2:
            ap = ap.rearrange("p (a b) -> p a b", a=shape[0])
        if len(shape) == 3:
            ap = ap.rearrange("p (a b c) -> p a b c", a=shape[0], b=shape[1])
        return ap

    lent = raw[:, 3:6, :].rearrange("p a n -> p (a n)")

    raw_landed = [nc.alloc_semaphore(f"raw_landed{j}") for j in range(NRAW)]
    s_hi, s_lo, s_used = (nc.alloc_semaphore(n) for n in ("s_hi", "s_lo", "s_used"))
    ada_landed = [nc.alloc_semaphore(f"ada_landed{j}") for j in range(NADA)]
    s_ada_used, s_ada_mul = nc.alloc_semaphore("s_ada_used"), nc.alloc_semaphore("s_ada_mul")

    loads = [0] * NRAW
    where = {}
    free = [[] for _ in range(NRAW)]
    next_place = 0
    loaded, split_next, ada_loaded, ada_next, ada_muls = 0, 0, 0, 0, 0

    def load(source, place=None):
        nonlocal loaded, next_place
        if place is None:
            place, next_place = next_place, (next_place + 1) % NRAW
        for token in free[place]:
            sp.wait_ge(*token)
        s = loaded
        loads[place] += 1
        dst = raw[:, place, :].rearrange("p (k n) -> p k n", k=source.shape[1])
        if source.shape[1] * source.shape[2] < SLOT:
            dst = raw[:, place, :].rearrange("p (k n) -> p k n", k=KB)[:, :, 0:source.shape[2]]
        sp.dma_start(dst, source).then_inc(raw_landed[place], 16)
        where[s] = (place, 16 * loads[place])
        free[place] = [(s_lo, s + 1)]
        loaded += 1

    def split(s=None, place=None, landed=None, s_value=None):
        nonlocal split_next
        if s is None:
            s = s_value = split_next
            place, landed = where[s]
            split_next += 1
        h = s % NHL
        act.wait_ge(raw_landed[place], landed)
        if s >= NHL:
            act.wait_ge(s_used, s_value - NHL + 1)
        act.activation(hi[:, h, :], raw[:, place, :], ACT.Copy).then_inc(s_hi, 1)
        dve.wait_ge(s_hi, s_value + 1)
        dve.tensor_tensor(lo[:, h, :], raw[:, place, :], hi[:, h, :].bitcast(F32), ALU.subtract).then_inc(s_lo, 1)

    def f_source(w, col, n=COLS):
        return w.rearrange("(k p) n -> p k n", p=P)[:, :, col:col + n]

    def t_source(w, row):
        return w[row:row + 2 * P, :].rearrange("(k p) n -> p k n", p=P)

    def f_matmuls(h, bank, xs, blocks=2):
        for b in range(blocks):
            out = ps[:, bank + b, :]
            for k in range(KB):
                w = slice(k * COLS + b * P, k * COLS + b * P + P)
                if k:
                    pe.matmul(out[:, 0:S], lo[:, h, w], xs[:, k, 0, :], start=False, stop=False)
                last = pe.matmul(out, hi[:, h, w], xs[:, k, :, :].rearrange("p a n -> p (a n)"),
                                 start=(k == 0), stop=(k == KB - 1))
                if not k:
                    pe.matmul(out[:, 0:S], lo[:, h, w], xs[:, k, 0, :], start=False, stop=False)
        return last

    def t_matmuls(h, base, xs, k0, first, final):
        for tb in range(NT):
            tok = slice(tb * P, tb * P + P)
            for k in range(2):
                for half_, (xpart, wpart) in [(a, b) for b in ((0, hi), (0, lo), (1, hi)) for a in range(2)]:
                    w = wpart[:, h, k * D + half_ * 512:k * D + half_ * 512 + 512]
                    start = first and k == 0 and xpart == 0 and wpart is hi
                    stop = final and k == 1 and xpart == 1
                    last = pe.matmul(ps[:, base + 2 * tb + half_, :], xs[:, k0 + k, xpart, tok], w,
                                     start=start, stop=stop, skip_group_check=True)
        return last

    def v_matmuls(h, bank, xs):
        for tb in range(NT):
            out, tok = ps[:, bank, tb * S:tb * S + S], slice(tb * P, tb * P + P)
            for k in range(KB):
                w = slice(k * COLS, k * COLS + COLS)
                for n, (xpart, wpart) in enumerate(((0, hi), (0, lo), (1, hi))):
                    last = pe.matmul(out, xs[:, k, xpart, tok], wpart[:, h, w],
                                     start=(k == 0 and n == 0), stop=(k == KB - 1 and n == 2))
        return last

    gemm_next = 0

    def gemm(kind, *args):
        nonlocal gemm_next
        s = gemm_next
        gemm_next += 1
        while split_next <= min(s + AHEAD, loaded - 1):
            split()
        pe.wait_ge(s_lo, s + 1)
        kind(s % NHL, *args).then_inc(s_used, 1)
        return (s_used, s + 1)

    acc = view(work, 0, 6, D)

    def ada_source(w, col, part):
        return w[part * 2 * P:(part + 1) * 2 * P, :].rearrange("(k p) n -> p k n", p=P)[:, :, col:col + D]

    ada_queue = []

    def ada_fill():
        nonlocal ada_loaded
        while ada_queue and ada_loaded < ada_next + NADA:
            q = ada_loaded
            if q >= NADA:
                pool.wait_ge(s_ada_used, q - NADA + 1)
            pool.dma_start(ada_raw[:, q % NADA, :].rearrange("p (k n) -> p k n", k=2), ada_queue.pop(0)).then_inc(ada_landed[q % NADA], 16)
            ada_loaded += 1

    def ada_multiply(dst, part, q_place, landed, muls):
        dve.wait_ge(ada_landed[q_place], landed)
        for k in range(2):
            w = ada_raw[:, q_place, k * D:(k + 1) * D]
            scalar = c_act[:, 2 * part + k:2 * part + k + 1]
            if part == 0 and k == 0:
                last = dve.tensor_scalar(dst, w, scalar, None, ALU.mult)
            else:
                dve.wait_ge(s_ada_mul, muls + k)
                last = dve.scalar_tensor_tensor(dst, w, scalar, dst, ALU.mult, ALU.add)
            last.then_inc(s_ada_mul, 1)
        dve.wait_ge(s_ada_mul, muls + 2)
        dve.sem_inc(s_ada_used, 1)

    def ada_step(index, part):
        nonlocal ada_next, ada_muls
        q = ada_next
        ada_multiply(acc[:, index, :], part, q % NADA, 16 * (q // NADA + 1), ada_muls)
        ada_next += 1
        ada_muls += 2
        ada_fill()

    def ada_finish(pairs, bank, *after):
        PE.wait((s_ada_mul, ada_muls), *after)
        for n, (chunk, index) in enumerate(pairs):
            for b in range(KB):
                last = pe.matmul(ps[:, bank, n * KB + b:n * KB + b + 1], acc[:, index, b * P:(b + 1) * P], ones[:, 0:1],
                                 start=True, stop=True)
        return pairs, bank, PE(last)

    def ada_columns(summed):
        pairs, bank, token = summed
        DV.wait(token)
        tokens = []
        for n, (chunk, index) in enumerate(pairs):
            kv = row_at["b_ada_kv_2"]
            if chunk < 6:
                bias, at = cols_b[:, 0:48], chunk * KB
            elif chunk < 8:
                bias, at = cols_a[:, kv:kv + 16], (chunk - 6) * KB
            else:
                bias, at = cols_b[:, 48:96], (chunk - 8) * KB
            dst = ada_cols[:, chunk * KB:(chunk + 1) * KB]
            tokens.append(DV(dve.tensor_tensor(dst, ps[:, bank, n * KB:(n + 1) * KB], bias[:, at:at + KB], ALU.add)))
            if chunk in (1, 4, 7, 9, 12):
                DV.wait(tokens[-1])
                tokens[-1] = DV(dve.tensor_scalar(dst, dst, 1.0, None, ALU.add))
        return tokens[-1]

    def spread(chunk, dst, scratch, bank, *after):
        AC.wait(*after)
        for b in range(KB):
            token = AC(act.activation(scratch[:, b * P:(b + 1) * P], ident[:, :], ACT.Copy,
                                      scale=ada_cols[:, chunk * KB + b:chunk * KB + b + 1]))
        PE.wait(token)
        for b in range(KB):
            last = pe.matmul(ps[:, bank + b // 4, (b % 4) * P:(b % 4) * P + P], ones[:, :], scratch[:, b * P:(b + 1) * P],
                             start=True, stop=True)
        AC.wait(PE(last))
        return AC(act.activation(dst, ps[:, bank:bank + 2, :].rearrange("p a n -> p (a n)"), ACT.Copy))


    small_landed = [nc.alloc_semaphore(f"small_landed{n}") for n in range(12)]
    n_small = [0] * 12

    def small_load(engine, group, dst, src):
        engine.dma_start(dst, src).then_inc(small_landed[group], 16)
        n_small[group] += 16
        return (small_landed[group], n_small[group])

    def as_rows(vector):
        letters = " ".join("abcd"[:len(vector.shape)])
        if len(vector.shape) > 1:
            vector = vector.rearrange(f"{letters} -> ({letters})")
        return vector.rearrange("(r p) -> r p", p=P)

    x_view = t["x"].rearrange("a (t p) n -> p (a t) n", p=P)
    x_in = [small_load(sp, tb, x_res[:, tb, :], x_view[:, tb, :]) for tb in range(NT)]
    rows_a, rows_b, rows_c = (view(work, 10240 + P * n, P) for n in range(3))
    row_at, n_rows = {}, 0
    for name in ("pre_mix_norm", "pre_ffn_norm", "c_2", "lru_conv_w", "lru_conv_b", "lru_ba", "lru_bx", "lru_lambda",
                 "gla_gate_b", "gla_norm", "conv_w_2", "b_ada_kv_2"):
        flat = as_rows(t[name])
        rows_in = small_load(act, 2, rows_a[n_rows:n_rows + flat.shape[0], :], flat)
        row_at[name] = n_rows
        n_rows += flat.shape[0]
    rows_in = small_load(act, 2, rows_b[0:96, :], as_rows(t["b_ada_2"]))
    onehot = view(work, 9216, S)[0:32, :]
    rel = view(work, 9472, 8)[0:32, :]
    rel_in = small_load(act, 3, onehot, t["bucket_onehot"])
    rel_in = small_load(act, 3, rel, t["rel_bias"])
    ln_at = {}
    for n, name in enumerate(("ln1_g_2", "ln1_b_2", "ln2_g_2", "ln2_b_2")):
        ln_at[name] = n * 16
        ln_in = small_load(act, 4, rows_c[n * 16:n * 16 + 16, :], as_rows(t[name]))
    gate_w2 = small[0:RANK, 32:160]
    w2_in = small_load(act, 5, gate_w2, t["gla_gate_w2"][0])
    b_f = small[0:FOX_HEADS, 0:1]
    w2_in = small_load(act, 5, b_f, t["b_f_2"].rearrange("(h a) -> h a", a=1))

    def col(name, n=0):
        return cols_a[:, row_at[name] + n:row_at[name] + n + 1]

    def serial(instruction):
        token = PO(instruction)
        PO.wait(token)
        return token

    masks = sb("masks", [P, 264])
    gla_mask = masks[:, 0:128]
    head_ones = masks[:, 128:256]
    head_cols = masks[:, 256:260]
    pow_half = masks[:, 260:262]
    serial(pool.memset(ident[:, :], 0.0))
    ident_ok = serial(pool.affine_select(out=ident[:, :], in_=ident[:, :], compare_op=ALU.not_equal, fill=1.0, base=0,
                                         pattern=[[-1, P]], channel_multiplier=1))
    serial(pool.memset(pow_half, -0.5))

    scr = [view(work, 6 * D + n * D, D) for n in range(2)]
    row_gain = [view(work, 8 * D + n * D, D) for n in range(3)]
    stats = small[:, 4:32]
    bn_tile = sb("bn_tile", [P, NT, 16])
    half_free = [None, None]
    halves = [0]

    def next_half():
        halves[0] ^= 1
        return halves[0]

    def rstd(mean_square, dst, eps, scale, *after):
        PO.wait(*after)
        a = PO(pool.tensor_scalar(dst, mean_square, scale, eps, ALU.mult, ALU.add))
        PO.wait(a)
        return PO(pool.tensor_tensor(dst, dst, pow_half[:, 0:dst.shape[1]], ALU.pow))

    def split_into(dst, k, source, ready):
        AC.wait(ready)
        h_ok = AC(act.activation(dst[:, k:k + 2, 0, :], source, ACT.Copy))
        DV.wait(h_ok, ready)
        return DV(dve.tensor_tensor(dst[:, k:k + 2, 1, :], source, dst[:, k:k + 2, 0, :].bitcast(F32), ALU.subtract))

    def turn(source, ready, base, bank_free):
        got = []
        for tb in range(NT):
            PE.wait(ready[tb], *(bank_free if tb == 0 else ()))
            for k in range(KB):
                at = (k % 2) * S + tb * P
                tr = pe.transpose(ps[:, base + k // 2, at:at + P], source[tb][:, k * P:(k + 1) * P], ident[:, :])
                if tb == NT - 1 and k % 2:
                    got.append(PE(tr))
        return base, got

    def take(turned, dst, scale, shift=None, *after):
        base, got = turned
        AC.wait(*after)
        DV.wait(*after)
        pending = None

        def lower(j, h, hi_ok, tmp_ok):
            DV.wait(hi_ok, tmp_ok)
            half_free[h] = DV(dve.tensor_tensor(dst[:, 2 * j:2 * j + 2, 1, :], half[:, h, :, :],
                                                dst[:, 2 * j:2 * j + 2, 0, :].bitcast(F32), ALU.subtract))
            return half_free[h]

        for j in range(KB // 2):
            h = next_half()
            for k in (2 * j, 2 * j + 1):
                src, tmp = ps[:, base + j, (k % 2) * S:(k % 2) * S + S], half[:, h, k % 2, :]
                if j % 2:
                    AC.wait(got[j], half_free[h])
                    more = {} if shift is None else {"bias": shift(k)}
                    tmp_ok = AC(act.activation(tmp, src, ACT.Copy if shift is None else ACT.Identity, scale=scale(k), **more))
                else:
                    DV.wait(got[j], half_free[h])
                    if shift is None:
                        tmp_ok = DV(dve.tensor_scalar(tmp, src, scale(k), None, ALU.mult))
                    else:
                        tmp_ok = DV(dve.tensor_scalar(tmp, src, scale(k), shift(k), ALU.mult, ALU.add))
            AC.wait(tmp_ok)
            hi_ok = AC(act.activation(dst[:, 2 * j:2 * j + 2, 0, :], half[:, h, :, :], ACT.Copy))
            if pending is not None:
                lower(*pending)
            pending = (j, h, hi_ok, tmp_ok)
        return lower(*pending)

    def f_sum(bank, done, dst, *dst_free):
        h = next_half()
        AC.wait(done, half_free[h])
        low = AC(act.activation(half[:, h, :, :], ps[:, bank:bank + 2, S:2 * S], ACT.Copy))
        DV.wait(low, *dst_free)
        token = DV(dve.tensor_tensor(dst, ps[:, bank:bank + 2, 0:S], half[:, h, :, :], ALU.add))
        half_free[h] = token
        return token

    def f_sum16(bank, done, dst, *dst_free):
        h = next_half()
        AC.wait(done, half_free[h])
        low = AC(act.activation(half[0:16, h, 0, :], ps[0:16, bank, S:2 * S], ACT.Copy))
        DV.wait(low, *dst_free)
        token = DV(dve.tensor_tensor(dst, ps[0:16, bank, 0:S], half[0:16, h, 0, :], ALU.add))
        half_free[h] = token
        return token

    def tokens_out(base):
        return [ps[:, base + 2 * tb:base + 2 * tb + 2, :].rearrange("p a n -> p (a n)") for tb in range(NT)]

    def add_rms(done, Y, gain, gain_ok, scratch_free=None):
        out, r_ok = [], []
        for tb in range(NT):
            ss, r = stats[:, tb:tb + 1], stats[:, 2 + tb:3 + tb]
            AC.wait(done, scratch_free)
            sq = AC(act.activation(scr[tb], Y[tb], ACT.Square, accum_out=ss))
            r_ok.append(rstd(ss, r, RMS_EPS, 1.0 / D, sq))
        for tb in range(NT):
            DV.wait(r_ok[tb], gain_ok)
            a = DV(dve.scalar_tensor_tensor(scr[tb], Y[tb], stats[:, 2 + tb:3 + tb], gain, ALU.mult, ALU.mult))
            DV.wait(a)
            out.append(DV(dve.tensor_tensor(x_res[:, tb, :], x_res[:, tb, :], scr[tb], ALU.add)))
        return out

    def normed(ready, on_vector=False):
        out, r_ok = [], []
        for tb in range(NT):
            ss, r = stats[:, 4 + tb:5 + tb], stats[:, 6 + tb:7 + tb]
            if on_vector:
                DV.wait(ready[tb])
                sq = DV(dve.scalar_tensor_tensor(scr[tb], x_res[:, tb, :], 1.0, x_res[:, tb, :], ALU.mult, ALU.mult, accum_out=ss))
            else:
                AC.wait(ready[tb])
                sq = AC(act.activation(scr[tb], x_res[:, tb, :], ACT.Square, accum_out=ss))
            r_ok.append(rstd(ss, r, RMS_EPS, 1.0 / D, sq))
        for tb in range(NT):
            DV.wait(r_ok[tb])
            out.append(DV(dve.tensor_scalar(scr[tb], x_res[:, tb, :], stats[:, 6 + tb:7 + tb], None, ALU.mult)))
        return out

    def layer_norm(done, Y, gate, gate_ok, *scratch_free):
        norm = []
        DV.wait(done, gate_ok, *scratch_free)
        for tb in range(NT):
            a = DV(dve.tensor_tensor(scr[tb], Y[tb], gate, ALU.mult))
            DV.wait(a)
            z = DV(dve.scalar_tensor_tensor(scr[tb], x_res[:, tb, :], DEEPNORM_ALPHA, scr[tb], ALU.mult, ALU.add))
            DV.wait(z)
            bn = bn_tile[:, tb, :]
            dve.bn_stats(bn[:, 0:6], scr[tb][:, 0:512])
            b2 = DV(dve.bn_stats(bn[:, 6:12], scr[tb][:, 512:1024]))
            DV.wait(b2)
            ag = DV(dve.bn_aggr(bn[:, 12:14], bn[:, 0:12]))
            norm.append(rstd(bn[:, 13:14], bn[:, 14:15], LN_EPS, 1.0, ag))
        out = []
        for tb in range(NT):
            DV.wait(norm[tb])
            bn = bn_tile[:, tb, :]
            out.append(DV(dve.tensor_scalar(scr[tb], scr[tb], bn[:, 12:13], bn[:, 14:15], ALU.subtract, ALU.mult)))
        return out, a

    def residual(ready, gain, bias, rows_ok, turned):
        for tb in range(NT):
            PO.wait(ready[tb], rows_ok, turned[1][-1])
            serial(pool.tensor_tensor(scr[tb], scr[tb], gain, ALU.mult))
            token = serial(pool.tensor_tensor(x_res[:, tb, :], scr[tb], bias, ALU.add))
        return token

    def acol(chunk):
        return lambda k: ada_cols[:, chunk * KB + k:chunk * KB + k + 1]

    def fold(n, ln, layer, scale_chunk, after):
        g, b = (cols_c[:, ln_at[ln + x] + layer * KB:ln_at[ln + x] + (layer + 1) * KB] for x in ("_g_2", "_b_2"))
        sc = ada_cols[:, scale_chunk * KB:(scale_chunk + 1) * KB]
        sh = ada_cols[:, (scale_chunk - 1) * KB:scale_chunk * KB]
        DV.wait(after)
        DV(dve.tensor_tensor(folded[:, n, 0, :], g, sc, ALU.mult))
        c = DV(dve.tensor_tensor(folded[:, n, 1, :], b, sc, ALU.mult))
        DV.wait(c)
        c = DV(dve.tensor_tensor(folded[:, n, 1, :], folded[:, n, 1, :], sh, ALU.add))
        return (lambda k: folded[:, n, 0, k:k + 1]), (lambda k: folded[:, n, 1, k:k + 1]), c

    def row_load(n, source, *after):
        PO.wait(*after)
        flat = bass.AP(tensor=source.tensor, offset=source.offset, ap=[[0, P], [1, D]])
        with nc.allow_non_contiguous_dma(reason="one row on all partitions"):
            return small_load(pool, 9 + n, row_gain[n], flat)

    QUERY_BLOCKS = ((0, P), (P, S))

    def scores(q, k, minus_f=None, *after):
        PE.wait(*after)
        for j in range(4):
            for tb, (at, n) in enumerate(QUERY_BLOCKS):
                out = ps[:, 4 + j, at:at + n]
                last = pe.matmul(out, q(j)[:, tb * P:tb * P + P], k(j)[:, 0:n], start=True, stop=(minus_f is None))
                if minus_f is not None:
                    last = pe.matmul(out, minus_f[0](j), minus_f[1][:, 0:n], start=False, stop=True)
        return PE(last)

    def softmax(probs, tile, logits, done, *free_):
        DV.wait(done, *free_)
        for j in range(4):
            for tb, (at, n) in enumerate(QUERY_BLOCKS):
                read = DV(logits(j, tb, probs[:, j, at:at + n], ps[:, 4 + j, at:at + n]))
        DV.wait(read)
        neg, total = tile[:, 0:8], tile[:, 8:16]
        for tb, (at, n) in enumerate(QUERY_BLOCKS):
            m = DV(dve.tensor_reduce(neg[:, tb * 4:tb * 4 + 4], probs[:, :, at:at + n], AX.X, ALU.max))
        DV.wait(m)
        m = DV(dve.tensor_scalar(neg, neg, -1.0, None, ALU.mult))
        AC.wait(m)
        for j in range(4):
            for tb, (at, n) in enumerate(QUERY_BLOCKS):
                e = AC(act.activation(probs[:, j, at:at + n], probs[:, j, at:at + n], ACT.Exp,
                                      bias=neg[:, tb * 4 + j:tb * 4 + j + 1], accum_out=total[:, tb * 4 + j:tb * 4 + j + 1]))
        return e, total

    def divide(probs, summed):
        e, total = summed
        DV.wait(e)
        r = DV(dve.reciprocal(total, total))
        PO.wait(r)
        DV.wait(r)
        out = []
        for j in range(4):
            engine, track = (dve, DV) if j < 2 else (pool, PO)
            for tb, (at, n) in enumerate(QUERY_BLOCKS):
                ok = track(engine.tensor_scalar(probs[:, j, at:at + n], probs[:, j, at:at + n],
                                                total[:, tb * 4 + j:tb * 4 + j + 1], None, ALU.mult))
            out.append(ok)
        return out

    def turn_probs(probs, probs_t, ready, *free_):
        for j in range(4):
            PE.wait(ready[j])
            for c in range(3):
                tr = pe.transpose(ps[:, 4 + j, c * P:(c + 1) * P], probs[:, j, c * P:(c + 1) * P], ident[:, :])
            AC.wait(PE(tr), *free_)
            last = AC(act.activation(probs_t[:, j, :], ps[:, 4 + j, 0:384], ACT.Copy))
        return last

    def weigh(probs_t, values, dst, k, ready, *after):
        PE.wait(ready, *after)
        for j in range(4):
            out = ps[64 * (j % 2):64 * (j % 2) + 64, 4, (j // 2) * S:(j // 2) * S + S]
            pe.matmul(out, values(0, j), probs_t[:, j, 0:S], start=True, stop=False, skip_group_check=True)
            last = pe.matmul(out[:, P:S], values(1, j), probs_t[:, j, S:S + P], start=False, stop=True, skip_group_check=True)
        return split_into(dst, k, ps[:, 4, :].rearrange("p (a n) -> p a n", a=2), PE(last))

    def values(tile, j0):
        return lambda kb, j: tile[:, kb, 64 * (j0 + j):64 * (j0 + j) + 64]

    def head(tile, j0):
        return lambda j: tile[64 * (j % 2):64 * (j % 2) + 64, (j0 + j) // 2, :]

    bank_free = {0: None, 2: None, 4: None, 6: None}
    which = [0]

    def next_bank(bank):
        if bank is None:
            which[0] ^= 2
            bank = which[0]
        return bank

    def project(dst, xs, *dst_free, bank=None):
        b = next_bank(bank)
        PE.wait(xs_ready, bank_free[b])
        bank_free[b] = f_sum(b, gemm(f_matmuls, b, xs), dst, *dst_free)
        return bank_free[b]

    def project16(dst, xs, *dst_free, bank=None):
        b = next_bank(bank)
        PE.wait(xs_ready, bank_free[b])
        bank_free[b] = f_sum16(b, gemm(f_matmuls, b, xs, 1), dst, *dst_free)
        return bank_free[b]

    def project_v(dst, xs, *dst_free):
        b = next_bank(None)
        PE.wait(xs_ready, bank_free[b])
        AC.wait(gemm(v_matmuls, b, xs), *dst_free)
        bank_free[b] = AC(act.activation(dst, ps[:, b, :].rearrange("p (a n) -> p a n", a=NT), ACT.Copy))
        return bank_free[b]

    w_in, w_out = t["w_in"][0], t["w_out"][0]
    order = ["g_lr", "gq", "mq", "mk", "lru_x", "gv", "mv", "mq+", "mk+", "mv+", "lru_g", "g_out"]
    for n, name in enumerate(order):
        load(f_source(w_in, OFF[name.strip("+")] + COLS * name.count("+")), (n + 2) % 3)
    ada_queue += [ada_source(t["w_ada_2"][0], 0, part) for part in range(4)]

    mq, mk = view(work, 1024, 4, S), view(work, 2048, 4, S)
    mv = view(work, 3072, NT, MOBA)
    moba_bias = view(work, 4096, 8, S)
    probs, probs_t = view(work, 6144, 4, 384), view(work, 7680, 4, 384)
    gqk, gout, gv, lru_g = (view(work, 9216 + 512 * n, 2, S) for n in range(4))
    from_last = view(lent, 0, 8, S)
    xpad = view(lent, 0, 2, S + 3)
    xc = view(lent, 520, 2, S)
    ri = view(lent, 1032, 4, S)
    aa, uu, hh, tt = (view(lent, 2056 + 512 * n, 2, S) for n in range(4))
    zz, ee, cum, qd = (view(lent, 4104 + 256 * n, S) for n in range(4))
    wab = view(lent, 5128, 4, P)
    glr = view(lent, 5640, S)[0:16, :]
    kd = view(work, 6144, 4, S)
    klast_t = view(work, 7168, NT, P)
    oo, osq = view(work, 7424, 2, S), view(work, 7936, 2, S)
    attn = view(work, 1024, 8, P)
    state = view(work, 2048, 3, S)
    soft, soft2 = sb("soft", [P, 16]), sb("soft2", [P, 16])

    x_ready = normed(x_in, on_vector=True)

    ones_ok = serial(pool.memset(ones[:, :], 1.0))
    table = view(work, 9728, 512)[0:8, :]
    t0 = serial(pool.memset(table, NEG))
    flip = view(work, 1024, P)
    serial(pool.memset(flip, 0.0))
    flip_ok = serial(pool.affine_select(out=flip, in_=flip, compare_op=ALU.not_equal, fill=1.0, base=1 - P, pattern=[[1, P]],
                                        channel_multiplier=1))

    PE.wait(ident_ok, rows_in)
    pe.transpose(ps[:, 0, 0:n_rows], rows_a[0:n_rows, :], ident[0:n_rows, 0:n_rows])
    rows_t = PE(pe.transpose(ps[:, 1, 0:96], rows_b[0:96, :], ident[0:96, 0:96]))
    DV.wait(rows_t)
    cols_ok = DV(dve.tensor_copy(cols_a[:, 0:n_rows], ps[:, 0, 0:n_rows]))
    colsb_ok = DV(dve.tensor_copy(cols_b[:, :], ps[:, 1, 0:96]))
    turned = turn(scr, x_ready, 4, [])
    PE.wait(rel_in)
    bias_mm = PE(pe.matmul(ps[0:8, 2, 0:S], rel, onehot, start=True, stop=True))
    AC.wait(bias_mm, t0)
    table_ok = AC(act.activation(table[:, 0:S], ps[0:8, 2, 0:S], ACT.Copy))
    PO.wait(table_ok)
    written = small_load(pool, 6, t["bias_table"], table)
    xs_ready = take(turned, xs_a, lambda k: col("pre_mix_norm", k), None, cols_ok)
    PO.wait(written)
    toeplitz = bass.AP(tensor=t["bias_table"].tensor, offset=t["bias_table"].offset, ap=[[1, P], [512, 8], [1, S]])
    with nc.allow_non_contiguous_dma(reason="Toeplitz rows overlap"):
        bias_in = small_load(pool, 7, from_last, toeplitz)
    serial(pool.memset(gla_mask, 1.0))
    serial(pool.memset(masks[:, 128:260], 0.0))
    serial(pool.affine_select(out=gla_mask, in_=gla_mask, compare_op=ALU.is_ge, fill=0.0, base=0, pattern=[[1, P]],
                              channel_multiplier=-1))
    serial(pool.memset(gla_mask[0:64, 64:128], 0.0))
    for h in range(2):
        serial(pool.memset(head_ones[64 * h:64 * h + 64, 64 * h:64 * h + 64], 1.0))
    for h in range(4):
        masks_ok = serial(pool.memset(head_cols[32 * h:32 * h + 32, h:h + 1], 1.0))
    serial(pool.memset(zeros16[:, :], 0.0))
    serial(pool.memset(wab, 0.0))
    for g in range(4):
        part = slice(64 * (g % 2), 64 * (g % 2) + 64)
        small_load(pool, 8, wab[part, g // 2, part], t["lru_wa"][0, g])
        wab_in = small_load(pool, 8, wab[part, 2 + g // 2, part], t["lru_wx"][0, g])
    bank_free[0] = bank_free[2] = table_ok
    bank_free[4] = bank_free[6] = xs_ready

    AC.wait(cols_ok)
    c_cols = cols_a[:, row_at["c_2"]:row_at["c_2"] + KB]
    c_sig = AC(act.activation(c_act[:, :], c_cols, ACT.Sigmoid))
    DV.wait(c_sig)
    c_ok = DV(dve.tensor_tensor(c_act[:, :], c_act[:, :], c_cols, ALU.mult))
    DV.wait(c_ok)
    ada_fill()

    def moba_logits(g):
        def write(j, tb, out, s_):
            b = moba_bias[:, 4 * g + j, :] if tb else moba_bias[:, 4 * g + j, P:S]
            return dve.scalar_tensor_tensor(out, s_, DH ** -0.5, b, ALU.mult, ALU.add)
        return write

    def conv(dst, src, taps, weight, bias, ready, *free_):
        DV.wait(ready, *free_)
        for b in range(2):
            if bias is None:
                token = DV(dve.tensor_scalar(dst[:, b, :], src[:, b, 0:S], weight(0, b), None, ALU.mult))
            else:
                token = DV(dve.tensor_scalar(dst[:, b, :], src[:, b, 0:S], weight(0, b), bias(b), ALU.mult, ALU.add))
        for j in range(1, taps):
            DV.wait(token)
            for b in range(2):
                token = DV(dve.scalar_tensor_tensor(dst[:, b, :], src[:, b, j:j + S], weight(j, b), dst[:, b, :], ALU.mult, ALU.add))
        return token

    glr_ok = project16(glr, xs_a, colsb_ok)
    PE.wait(flip_ok, bias_in, bank_free[4])
    for n in range(4):
        last = pe.matmul(ps[:, 4 + n, :], flip, from_last[:, 2 * n:2 * n + 2, :].rearrange("p a n -> p (a n)"), start=True, stop=True)
    AC.wait(PE(last))
    bias_ok = AC(act.activation(moba_bias.rearrange("p a n -> p (a n)"), ps[:, 4:8, :].rearrange("p a n -> p (a n)"), ACT.Copy))
    PE.wait(ln_in, w2_in, glr_ok, bias_ok)
    pe.transpose(ps[:, 4, 0:64], rows_c[0:64, :], ident[0:64, 0:64])
    gz = PE(pe.matmul(ps[:, 5, 0:S], gate_w2, glr, start=True, stop=True))
    DV.wait(gz)
    lnc_ok = DV(dve.tensor_copy(cols_c[:, :], ps[:, 4, 0:64]))
    c1 = DV(dve.tensor_scalar(zz, ps[:, 5, 0:S], col("gla_gate_b"), None, ALU.add))
    qk_ok = project(gqk, xs_a, lnc_ok)
    q_ok = project(mq[:, 0:2, :], xs_a, bias_ok)
    k_ok = project(mk[:, 0:2, :], xs_a)
    s_ok = scores(head(mq, 0), head(mk, 0), None, q_ok, k_ok, c1)
    e_ok = softmax(probs, soft, moba_logits(0), s_ok, bias_ok)
    PO.wait(bias_ok)
    pz = serial(pool.memset(xpad[:, :, 0:3], 0.0))
    lx_ok = project(xpad[:, :, 3:], xs_a, pz)
    p_ok = divide(probs, e_ok)
    AC.wait(c1)
    c2 = AC(act.activation(ee, zz, ACT.Abs)); AC.wait(c2)
    c2 = AC(act.activation(ee, ee, ACT.Exp, scale=-1.0)); AC.wait(c2)
    c2 = AC(act.activation(ee, ee, ACT.Ln, bias=1.0))
    gv_ok = project_v(gv, xs_a)
    pt_ok = turn_probs(probs, probs_t, p_ok)
    xc_ok = conv(xc, xpad, 4, lambda j, b: col("lru_conv_w", 2 * j + b), lambda b: col("lru_conv_b", b), lx_ok)
    ada_step(0, 0)
    v_ok = project_v(mv[:, :, 0:COLS], xs_a)
    o_ok = weigh(probs_t, values(mv, 0), xs_b, 4, pt_ok, v_ok)
    q_ok = project(mq[:, 2:4, :], xs_a)
    DV.wait(c2)
    c3 = DV(dve.tensor_scalar(zz, zz, 0.0, 1.0 / 16, ALU.min, ALU.mult)); DV.wait(c3)
    c3 = DV(dve.scalar_tensor_tensor(zz, ee, -1.0 / 16, zz, ALU.mult, ALU.add)); DV.wait(c3, ones_ok)
    for c in range(S // CHUNK):
        part = slice(c * CHUNK, (c + 1) * CHUNK)
        cum_ok = DV(dve.tensor_tensor_scan(cum[:, part], ones[:, 0:CHUNK], zz[:, part], 0.0, ALU.mult, ALU.add))
    ada_step(0, 1)
    k_ok = project(mk[:, 2:4, :], xs_a)
    s_ok = scores(head(mq, 4), head(mk, 4), None, q_ok, k_ok, o_ok)
    e_ok = softmax(probs, soft, moba_logits(1), s_ok, pt_ok)
    v_ok = project_v(mv[:, :, COLS:], xs_a)
    b = next_bank(None)
    PE.wait(xc_ok, wab_in, bank_free[b])
    for n in range(4):
        last = pe.matmul(ps[:, b + n // 2, (n % 2) * S:(n % 2) * S + S], wab[:, n, :], xc[:, n % 2, :], start=True, stop=True)
    gates = PE(last)
    p_ok = divide(probs, e_ok)
    AC.wait(gates)
    for n in range(4):
        ri_ok = AC(act.activation(ri[:, n, :], ps[:, b + n // 2, (n % 2) * S:(n % 2) * S + S], ACT.Sigmoid,
                                  bias=col("lru_ba" if n < 2 else "lru_bx", n % 2)))
    bank_free[b] = ri_ok
    lam = cols_a[:, row_at["lru_lambda"]:row_at["lru_lambda"] + 2]
    sv = lambda n: soft2[:, 2 * n:2 * n + 2]
    a0 = AC(act.activation(sv(0), lam, ACT.Abs))
    AC.wait(a0)
    a1 = AC(act.activation(sv(0), sv(0), ACT.Exp, scale=-1.0))
    DV.wait(a1)
    a2 = DV(dve.tensor_scalar(sv(1), sv(0), 2.0, None, ALU.add)); DV.wait(a2)
    a2 = DV(dve.reciprocal(sv(1), sv(1))); PO.wait(a2)
    serial(pool.tensor_tensor(sv(1), sv(1), sv(0), ALU.mult))
    serial(pool.tensor_tensor(sv(2), sv(1), sv(1), ALU.mult))
    serial(pool.tensor_scalar(sv(3), sv(2), 1.0 / 17, 1.0 / 15, ALU.mult, ALU.add))
    for m in (13, 11, 9, 7, 5, 3, 1):
        serial(pool.tensor_tensor(sv(3), sv(3), sv(2), ALU.mult))
        serial(pool.tensor_scalar(sv(3), sv(3), 1.0 / m, None, ALU.add))
    serial(pool.tensor_tensor(sv(3), sv(3), sv(1), ALU.mult))
    serial(pool.tensor_scalar(sv(4), lam, -1.0, 0.0, ALU.mult, ALU.max))
    serial(pool.tensor_scalar(sv(3), sv(3), 2.0, None, ALU.mult))
    serial(pool.tensor_tensor(sv(3), sv(3), sv(4), ALU.add))
    sp_ok = serial(pool.tensor_scalar(sv(3), sv(3), 4.0, None, ALU.mult))
    lg_ok = project(lru_g, xs_a)
    pt_ok = turn_probs(probs, probs_t, p_ok)
    AC.wait(cum_ok)
    e1 = AC(act.activation(ee, cum, ACT.Exp))
    DV.wait(e1, qk_ok)
    qd_ok = DV(dve.scalar_tensor_tensor(qd, gqk[:, 0, :], 32.0 ** -0.5, ee, ALU.mult, ALU.mult))
    AC.wait(qd_ok)
    e2 = AC(act.activation(ee, cum, ACT.Exp, scale=-1.0))
    PO.wait(e2, qk_ok, masks_ok, pt_ok)
    serial(pool.tensor_tensor(zz, gqk[:, 1, :], ee, ALU.mult))
    for h in range(4):
        kd_ok = PO(pool.tensor_scalar(kd[:, h, :], zz, head_cols[:, h:h + 1], None, ALU.mult))
    last_cum = cum.rearrange("p (c n) -> p c n", n=CHUNK)[:, :, CHUNK - 1]
    AC.wait(kd_ok)
    for c in range(S // CHUNK):
        e4 = AC(act.activation(ee[:, c * CHUNK:(c + 1) * CHUNK], cum[:, c * CHUNK:(c + 1) * CHUNK], ACT.Exp, scale=-1.0,
                               bias=cum[:, (c + 1) * CHUNK - 1:(c + 1) * CHUNK]))
    decay = soft[:, 0:4]
    AC.wait(p_ok[1], p_ok[3])
    e5 = AC(act.activation(decay, last_cum, ACT.Exp))
    PO.wait(e4, kd_ok)
    kl_ok = PO(pool.tensor_tensor(zz, gqk[:, 1, :], ee, ALU.mult))
    AC.wait(sp_ok, ri_ok)
    for b in range(2):
        w_ok = AC(act.activation(tt[:, b, :], ri[:, b, :], ACT.Tanh, scale=sv(3)[:, b:b + 1]))
    PO.wait(w_ok)
    b1 = PO(pool.tensor_scalar(aa, tt, -1.0, 1.0, ALU.mult, ALU.add))
    DV.wait(w_ok)
    b2 = DV(dve.tensor_scalar(hh, tt, 1.0, None, ALU.add)); DV.wait(b2, b1)
    b3 = DV(dve.tensor_scalar(tt, tt, 1e-30, None, ALU.max))
    b4 = DV(dve.reciprocal(hh, hh)); DV.wait(b4)
    a_ok = DV(dve.tensor_tensor(aa, aa, hh, ALU.mult))
    AC.wait(b3)
    rt = AC(act.activation(tt, tt, ACT.Sqrt))
    PO.wait(ri_ok)
    b7 = serial(pool.tensor_tensor(xc, xc, ri[:, 2:4, :], ALU.mult))
    o_ok = weigh(probs_t, values(mv, 4), xs_b, 6, pt_ok, v_ok)
    go_ok = project(gout, xs_a)
    DV.wait(rt, a_ok)
    b5 = DV(dve.scalar_tensor_tensor(uu, tt, 2.0, hh, ALU.mult, ALU.mult)); DV.wait(b5)
    b6 = DV(dve.memset(uu[:, :, 0:1], 1.0)); DV.wait(b6, b7)
    b8 = DV(dve.tensor_tensor(uu, uu, xc, ALU.mult)); DV.wait(b8)
    PE.wait(kd_ok, qd_ok, o_ok)
    for h in range(4):
        for pr in range(2):
            n = 2 * h + pr
            last = pe.matmul(ps[:, 4 + n // 4, (n % 4) * P:(n % 4) * P + P], kd[:, h, pr * P:(pr + 1) * P], qd[:, pr * P:(pr + 1) * P],
                             start=True, stop=True)
    at_ok = PE(last)
    PE.wait(kl_ok)
    for tb in range(NT):
        last = pe.transpose(ps[:, 6, tb * P:(tb + 1) * P], zz[:, tb * P:(tb + 1) * P], ident[:, :])
    kt = PE(last)
    AC.wait(kt, kl_ok)
    klt_ok = AC(act.activation(klast_t, ps[:, 6, 0:S].rearrange("p (a n) -> p a n", a=NT), ACT.Copy))
    DV.wait(at_ok)
    for n in range(2):
        am_ok = DV(dve.tensor_tensor(attn[:, 4 * n:4 * n + 4, :], ps[:, 4 + n, :].rearrange("p (a n) -> p a n", a=4),
                                     gla_mask[:, None, :].to_broadcast([P, 4, P]), ALU.mult))
    PE.wait(klt_ok, gv_ok)
    kv_bank = ((6, 0), (7, 0), (6, S))
    for c in range(3):
        rows = slice(64 * (c % 2), 64 * (c % 2) + 64)
        bank, at = kv_bank[c]
        last = pe.matmul(ps[:, bank, at:at + S], klast_t[rows, c // 2, :], gv[rows, c // 2, :], start=True, stop=True)
    kv_ok = PE(last)
    kvs = [ps[:, bank, at:at + S] for bank, at in kv_bank]
    DV.wait(kv_ok, e5)
    f0 = DV(dve.tensor_copy(state[:, 0, :], kvs[0])); DV.wait(f0)
    for c in (1, 2):
        f0 = DV(dve.scalar_tensor_tensor(state[:, c, :], state[:, c - 1, :], decay[:, c:c + 1], kvs[c], ALU.mult, ALU.add)); DV.wait(f0)
    for h in range(4):
        part = state[:, :, 64 * h:64 * h + 64]
        st_ok = DV(dve.tensor_scalar(part, part, head_cols[:, h:h + 1], None, ALU.mult))
    PE.wait(st_ok, am_ok)
    first = True
    for hp in range(2):
        for c in range(1, 4):
            pe.matmul(ps[:, 4, hp * S + c * CHUNK:hp * S + (c + 1) * CHUNK], state[:, c - 1, hp * P:(hp + 1) * P],
                      qd[:, c * CHUNK:(c + 1) * CHUNK], start=first, stop=False, skip_group_check=True)
            first = False
    for h in range(4):
        for pr in range(2):
            last = pe.matmul(ps[64 * (h % 2):64 * (h % 2) + 64, 4, (h // 2) * S + pr * P:(h // 2) * S + (pr + 1) * P],
                             gv[:, pr, 64 * h:64 * h + 64], attn[:, 2 * h + pr, :], start=False, stop=True, skip_group_check=True)
    og = PE(last)
    out_gla = ps[:, 4, :].rearrange("p (a n) -> p a n", a=2)

    for n, row in enumerate((512, 768, 0, 256)):
        load(t_source(w_out, row), (len(order) + n + 2) % 3)

    for b in range(2):
        h_ok = DV(dve.tensor_tensor_scan(hh[:, b, :], aa[:, b, :], uu[:, b, :], 0.0, ALU.mult, ALU.add))
    PO.wait(lg_ok, w_ok, rt, b5)
    serial(pool.tensor_tensor(tt, lru_g, lru_g, ALU.mult))
    serial(pool.tensor_scalar(tt, tt, 0.044715, 1.0, ALU.mult, ALU.add))
    k1 = serial(pool.tensor_tensor(tt, tt, lru_g, ALU.mult))
    AC.wait(k1, go_ok, klt_ok, am_ok)
    k2 = AC(act.activation(tt, tt, ACT.Sigmoid, scale=2.0 * math.sqrt(2.0 / math.pi)))
    gsig = view(work, 7936 + 512, 2, S)
    g9 = AC(act.activation(gsig, gout, ACT.Sigmoid))
    AC.wait(og)
    g2 = AC(act.activation(osq, out_gla, ACT.Square))
    g1 = AC(act.activation(oo, out_gla, ACT.Copy))
    PO.wait(k2)
    k3 = serial(pool.tensor_tensor(tt, tt, lru_g, ALU.mult))
    DV.wait(k3, h_ok)
    k4 = DV(dve.tensor_tensor(hh, hh, tt, ALU.mult))
    lru_ok = split_into(xs_b, 0, hh, k4)
    PE.wait(lru_ok, o_ok, bank_free[0], bank_free[2])
    Y = tokens_out(0)
    for n, k0 in enumerate((4, 6, 0)):
        done = gemm(t_matmuls, 0, xs_b, k0, n == 0, False)
        if n == 0:
            PE.wait(g2, masks_ok)
            g3 = PE(pe.matmul(ps[:, 5, :], head_ones, osq.rearrange("p a n -> p (a n)"), start=True, stop=True))
            DV.wait(g3)
            g4 = DV(dve.tensor_scalar(osq, ps[:, 5, :].rearrange("p (a n) -> p a n", a=2), 1.0 / 64, RMS_EPS, ALU.mult, ALU.add))
            AC.wait(g4)
            g5 = AC(act.activation(osq, osq, ACT.Sqrt))
            PO.wait(g9)
            g10 = serial(pool.tensor_tensor(gsig, gsig, gout, ALU.mult))
            DV.wait(g5)
            g6 = DV(dve.reciprocal(osq, osq))
            DV.wait(g1, g10)
            for b in range(2):
                g8 = DV(dve.scalar_tensor_tensor(oo[:, b, :], oo[:, b, :], col("gla_norm", b), gsig[:, b, :], ALU.mult, ALU.mult))
            DV.wait(g6, g8)
            g11 = DV(dve.tensor_tensor(oo, oo, osq, ALU.mult))
            gla_ok = split_into(xs_b, 2, oo, g11)
    for place in (3, 4, 5):
        free[place] = [lru_ok, gla_ok]
    next_place = 3

    names = ("gate_low", "gate_sum", "gate_sig", "silu_ok", "up_low", "up_sum", "h_ok", "h_hi", "h_lo")
    F = {n: nc.alloc_semaphore("ffn_" + n) for n in names}
    hs = xs_b[:, :, :, :].rearrange("p (u k) a n -> p u k a n", u=4)[:, 0:2]
    gg = view(work, 6 * D, 2, 2, S)
    sig = view(work, 7 * D, 2, S)

    def ffn_load(w_gate, w_up, w_down):
        s0, p0 = loaded, next_place
        for w in (w_gate, w_up):
            load(f_source(w, 0))
        return w_gate, w_up, w_down, s0, p0

    def feed_forward(number, weights, x_ok, y_free, scr_free, ada=None):
        nonlocal loaded, next_place, split_next, gemm_next, ada_loaded, ada_next, ada_muls
        w_gate, w_up, w_down, s0, p0 = weights
        base = number * TURNS
        assert s0 == gemm_next
        wg = w_gate.rearrange("(k p) n -> p k n", p=P)
        wu = w_up.rearrange("(k p) n -> p k n", p=P)

        def gate_part(turn_, s):
            for d, before in enumerate(("gate_sum", "up_sum")):
                pe.wait_ge(s_lo, s[1] + d + 1)
                if turn_ is not 0:
                    pe.wait_ge(F[before], base + turn_)
                f_matmuls((s[0] + d) % NHL, 2 * d, xs_a).then_inc(s_used, 1)

        def hidden(turn_, s, u):
            n = turn_ + (base + 1)
            for d, name in enumerate(("gate", "up")):
                act.wait_ge(s_used, s[1] + d + 1)
                if turn_ is not 0:
                    act.wait_ge(F[name + "_sum"], base + turn_)
                act.activation(half[:, d, :, :], ps[:, 2 * d:2 * d + 2, S:2 * S], ACT.Copy).then_inc(F[name + "_low"], 1)
                dve.wait_ge(F[name + "_low"], n)
                if turn_ is not 0:
                    dve.wait_ge(F["h_lo"], base + turn_)
                dve.tensor_tensor(gg[:, d, :, :], ps[:, 2 * d:2 * d + 2, 0:S], half[:, d, :, :], ALU.add).then_inc(F[name + "_sum"], 1)
                if d == 0:
                    act.wait_ge(F["gate_sum"], n)
                    act.activation(sig, gg[:, 0, :, :], ACT.Sigmoid).then_inc(F["gate_sig"], 1)
                    pool.wait_ge(F["gate_sig"], n)
                    pool.tensor_tensor(gg[:, 0, :, :], gg[:, 0, :, :], sig, ALU.mult).then_inc(F["silu_ok"], 1)
                    yield
            dve.wait_ge(F["up_sum"], n)
            dve.wait_ge(F["silu_ok"], n)
            dve.tensor_tensor(gg[:, 1, :, :], gg[:, 0, :, :], gg[:, 1, :, :], ALU.mult).then_inc(F["h_ok"], 1)
            act.wait_ge(F["h_ok"], n)
            act.activation(hs[:, u, :, 0, :], gg[:, 1, :, :], ACT.Copy).then_inc(F["h_hi"], 1)
            dve.wait_ge(F["h_hi"], n)
            dve.tensor_tensor(hs[:, u, :, 1, :], gg[:, 1, :, :], hs[:, u, :, 0, :].bitcast(F32), ALU.subtract).then_inc(F["h_lo"], 1)
            yield

        def down_part(turn_, s, u):
            pe.wait_ge(s_lo, s[1] + 1)
            pe.wait_ge(F["h_lo"], turn_ + (base + 1))
            t_matmuls(s[0] % NHL, 4, hs[:, u], 0, False, False).then_inc(s_used, 1)

        PE.wait(y_free)
        for n in range(4):
            pe.matmul(ps[:, 4 + n, :], zeros16[:, 0:P], zeros16[:, :], start=True, stop=False, skip_group_check=True)
        s = (s0, s0)
        while split_next < s0 + AHEAD:
            split()
        PE.wait(x_ok)
        gate_part(0, s)
        AC.wait(x_ok)
        DV.wait(x_ok, scr_free)
        parts = hidden(0, s, 0)
        next(parts)
        next(parts)
        loop_s = s0 + 2
        place_of = lambda n: (n - s0 + p0) % NRAW
        count = {place_of(loop_s + n): 16 * (loads[place_of(loop_s + n)] + 1) for n in range(6)}
        iterations = (TURNS - 1) // 2
        with nc.Fori(0, iterations, 1) as i:
            s_reg = i * 6 + loop_s
            for n in range(6):
                turn_col = (i * 2 + (1 + n // 3)) * COLS
                place = place_of(loop_s + n)
                if n % 3 < 2:
                    src = (wg, wu)[n % 3][:, :, bass.ds(turn_col, COLS)]
                else:
                    src = w_down[bass.ds(turn_col - COLS, COLS), :].rearrange("(k p) n -> p k n", p=P)
                sp.wait_ge(s_lo, s_reg + (n - NRAW + 1))
                sp.dma_start(raw[:, place, :].rearrange("p (k n) -> p k n", k=src.shape[1]), src).then_inc(raw_landed[place], 16)
            for v in range(2):
                turn_ = i * 2 + (1 + v)
                s = (loop_s + 3 * v, s_reg + 3 * v)
                u = (1 + v) % 2
                parts = hidden(turn_, s, u)

                def split_at(n):
                    n += 3 * v
                    place = place_of(loop_s + n)
                    split(loop_s + n, place, i * 16 + count[place], s_reg + n)

                def ada_at(part):
                    if ada is not None:
                        q = ada_next + part
                        src = ada[part * 2 * P:(part + 1) * 2 * P, bass.ds(i * D + D, D)].rearrange("(k p) n -> p k n", p=P)
                        pool.wait_ge(s_ada_used, i * 4 + (q - NADA + 1))
                        pool.dma_start(ada_raw[:, q % NADA, :].rearrange("p (k n) -> p k n", k=2), src).then_inc(ada_landed[q % NADA], 16)
                        yield
                        ada_multiply(acc[:, bass.ds(i + 1, 1), :].rearrange("p a n -> p (a n)"), part, q % NADA,
                                     i * 32 + 16 * (q // NADA + 1), i * 8 + (ada_muls + 2 * part))
                    yield

                ada_parts = [ada_at(2 * v), ada_at(2 * v + 1)]
                for a in ada_parts:
                    next(a)
                split_at(0)
                if ada is not None:
                    next(ada_parts[0])
                split_at(1)
                gate_part(turn_, s)
                next(parts)
                if ada is not None:
                    next(ada_parts[1])
                split_at(2)
                next(parts)
                down_part(turn_ - 1, (s[0] + 2, s[1] + 2), 1 - u)
        for n in range(6):
            loads[place_of(loop_s + n)] += iterations
        loaded += 6 * iterations
        split_next += 6 * iterations
        gemm_next += 2 + 6 * iterations
        if ada is not None:
            ada_loaded += 4 * iterations
            ada_next += 4 * iterations
            ada_muls += 8 * iterations
        for place in range(NRAW):
            free[place] = [(s_lo, loaded)]
        next_place = place_of(loaded)
        load(t_source(w_down, DFF - COLS))

    def last_down(number):
        pe.wait_ge(F["h_lo"], (number + 1) * TURNS)
        return gemm(t_matmuls, 4, hs[:, (TURNS - 1) % 2], 0, False, True)

    rows_ok = row_load(0, t["post_mix_norm"][0], table_ok, gla_ok)
    ffn = ffn_load(t["w_ffn_gate"][0], t["w_ffn_up"][0], t["w_ffn_down"][0])
    ada_step(0, 2)
    ada_step(0, 3)
    PE.wait(gla_ok)
    done = gemm(t_matmuls, 0, xs_b, 2, False, True)
    ready = add_rms(done, Y, row_gain[0], rows_ok, gla_ok)
    y_read = ready[-1]
    ready = normed(ready)
    turned = turn(scr, ready, 4, [g4])
    xs_ready = take(turned, xs_a, lambda k: col("pre_ffn_norm", k))
    feed_forward(0, ffn, xs_ready, xs_ready, xs_ready, t["w_ada_2"][0])

    rows_ok = row_load(0, t["post_ffn_norm"][0], y_read)
    conv_in = t["conv_w_in_2"][0]
    for j in range(4):
        for third in (1, 2, 0):
            load(f_source(conv_in, third * D + j * COLS))
    for n in range(4):
        load(t_source(t["conv_w_out_2"][0], n * 2 * P))
    ada_queue += [ada_source(w, c, part) for w, c in ((t["w_ada_kv_2"], 0), (t["w_ada_kv_2"], D), (t["w_ada_2"][1], 0)) for part in range(4)]
    done = last_down(0)
    sums = ada_finish([(c, c) for c in range(6)], 0, (F["up_sum"], TURNS))
    Y = tokens_out(4)
    ready = add_rms(done, Y, row_gain[0], rows_ok)
    mods = ada_columns(sums)
    half_free[0] = half_free[1] = (F["up_sum"], TURNS)
    turned = turn([x_res[:, tb, :] for tb in range(NT)], ready, 0, [mods])
    xs_ready = take(turned, xs_a, acol(1), acol(0), mods)
    bank_free.update({0: xs_ready, 2: xs_ready, 4: ready[-1], 6: ready[-1]})
    cpad, cc_, vv_, bb_ = view(work, 3 * D, 2, S + 2), view(work, 3 * D + 520, 2, S), view(work, 3 * D + 1032, 2, S), view(work, 3 * D + 1544, 2, S)
    PO.wait(ready[-1], mods)
    pz = serial(pool.memset(cpad[:, :, 0:2], 0.0))
    ada_fill()
    mixed, step = None, 0
    for j in range(4):
        c_ok = project(cc_, xs_a, mixed, mods)
        ada_step(step // 4, step % 4)
        v_ok = project(vv_, xs_a, mixed)
        PO.wait(c_ok, v_ok, mixed)
        u_ok = serial(pool.tensor_tensor(cpad[:, :, 2:], cc_, vv_, ALU.mult))
        ada_step((step + 1) // 4, (step + 1) % 4)
        b_ok = project(bb_, xs_a, mixed)
        cv = conv(cc_, cpad, 3, lambda n, b: col("conv_w_2", 8 * n + 2 * j + b), None, u_ok)
        DV.wait(b_ok, cv)
        m_ok = DV(dve.tensor_tensor(bb_, bb_, cc_, ALU.mult))
        mixed = split_into(xs_b, 2 * j, bb_, m_ok)
        ada_step((step + 2) // 4, (step + 2) % 4)
        step += 3
        if j == 1:
            gate_ok = spread(2, row_gain[1], row_gain[2], 4, mods, ready[-1])
    row_gain_ok = row_load(0, t["ln1_g_2"][0], ready[-1])
    rows_ok = [row_gain_ok, row_load(2, t["ln1_b_2"][0], gate_ok)]
    ffn = ffn_load(t["ffn_w_gate_2"][0], t["ffn_w_up_2"][0], t["ffn_w_down_2"][0])
    PE.wait(mixed, gate_ok, ready[-1])
    for n in range(4):
        done = gemm(t_matmuls, 4, xs_b, 2 * n, n == 0, n == 3)
    sums = ada_finish([(6, 0), (7, 1), (8, 2)], 0, bank_free[0])
    ready, y_read = layer_norm(done, Y, row_gain[1], gate_ok)
    mods = ada_columns(sums)
    scale, shift, f_ok = fold(0, "ln1", 0, 4, mods)
    turned = turn(scr, ready, 0, [mods, bank_free[2]])
    xs_ready = take(turned, xs_a, scale, shift, f_ok)
    PO.wait(*rows_ok)
    res_ok = residual(ready, row_gain[0], row_gain[2], None, turned)
    feed_forward(1, ffn, xs_ready, y_read, res_ok, t["w_ada_2"][1])

    rows_ok = row_load(0, t["ln2_g_2"][0], res_ok)
    w_k, w_v, w_q, w_o = t["w_k_2"], t["w_v_2"], t["attn_w_q_2"][0], t["attn_w_o_2"][0]
    fox_base = loaded
    fox = [t_source(w_v, n * 2 * P) for n in range(4)] + [t["w_f_2"].rearrange("(k p) n -> p k n", p=P)]
    fox += [f_source(w, j * COLS) for w, j in ((w_k, 0), (w_q, 0), (w_k, 1), (w_q, 1), (w_k, 2), (w_k, 3), (w_q, 2), (w_q, 3))]
    fox += [t_source(w_o, n * 2 * P) for n in range(4)]
    for n, src in enumerate(fox):
        load(src, (n + 1) % 3)
    gate_ok = spread(5, row_gain[1], row_gain[2], 0, (F["up_sum"], 2 * TURNS), res_ok, y_read)
    rows_ok = [rows_ok, row_load(2, t["ln2_b_2"][0], gate_ok)]
    done = last_down(1)
    PE.wait(gate_ok)
    sums = ada_finish([(8 + c, c) for c in range(1, 6)], 0)
    ready, y_read = layer_norm(done, Y, row_gain[1], gate_ok)
    mods = ada_columns(sums)
    scale, shift, f_ok = fold(0, "ln2", 0, 7, mods)
    scale2, shift2, f_ok = fold(1, "ln2", 0, 9, mods)
    half_free[0] = half_free[1] = (F["up_sum"], 2 * TURNS)
    turned = turn(scr, ready, 4, [y_read])
    xs_ready = take(turned, xs_b, scale, shift, f_ok)
    PO.wait(*rows_ok)
    res_ok = residual(ready, row_gain[0], row_gain[2], None, turned)
    kT = view(lent, 0, KB, S)
    vN = view(lent, 2048, NT, D)
    qT = [view(lent, 4096 + 512 * n, 2, S) for n in range(4)]
    probs, probs_t = view(work, 0, 4, 384), view(work, 1536, 4, 384)
    sel = view(work, 3072, FOX_HEADS, P)[0:16]
    zf, ef, ff, nf = (view(work, 5120 + S * n, S)[0:16, :] for n in range(4))
    f_cols = small[:, 32:64]
    lent_free = (s_lo, fox_base)
    PO.wait(mods)
    serial(pool.memset(sel, 0.0))
    serial(pool.affine_select(out=sel, in_=sel, compare_op=ALU.not_equal, fill=1.0, base=0,
                              pattern=[[1, FOX_HEADS], [0, P]], channel_multiplier=-1))
    causal = scr[1][:, 0:384]
    serial(pool.memset(causal, 0.0))
    serial(pool.affine_select(out=causal[:, 0:P], in_=causal[:, 0:P], compare_op=ALU.is_ge, fill=NEG, base=0, pattern=[[-1, P]],
                              channel_multiplier=1))
    causal_ok = serial(pool.affine_select(out=causal[:, P:], in_=causal[:, P:], compare_op=ALU.is_ge, fill=NEG, base=P,
                                          pattern=[[-1, S]], channel_multiplier=1))
    PE.wait(xs_ready, mods)
    for n in range(4):
        v_done = gemm(t_matmuls, 0, xs_b, 2 * n, n == 0, n == 3)
        if n == 0:
            q_ready = take(turned, xs_a, scale2, shift2, f_ok)
    V = tokens_out(0)
    DV.wait(v_done, lent_free)
    v_ok = DV(dve.tensor_copy(vN[:, 0, :], V[0]))
    AC.wait(v_done, lent_free)
    v_ok2 = AC(act.activation(vN[:, 1, :], V[1], ACT.Copy))
    bank_free.update({0: v_ok, 2: v_ok2, 4: q_ready, 6: q_ready})
    zf_ok = project16(zf, xs_b, mods, bank=4)
    k_ok = project(kT[:, 0:2, :], xs_b, lent_free, bank=6)
    DV.wait(zf_ok)
    c1 = DV(dve.tensor_scalar(zf, zf, b_f, None, ALU.add))
    AC.wait(c1)
    c2 = AC(act.activation(ef, zf, ACT.Abs)); AC.wait(c2)
    c2 = AC(act.activation(ef, ef, ACT.Exp, scale=-1.0)); AC.wait(c2)
    c2 = AC(act.activation(ef, ef, ACT.Ln, bias=1.0))
    DV.wait(c1, c2)
    c3 = DV(dve.tensor_scalar(zf, zf, 0.0, None, ALU.min)); DV.wait(c3)
    c3 = DV(dve.tensor_tensor(zf, zf, ef, ALU.subtract)); DV.wait(c3)
    c4 = DV(dve.memset(nf, 1.0)); DV.wait(c4)
    c5 = DV(dve.tensor_tensor_scan(ff, nf, zf, 0.0, ALU.mult, ALU.add)); DV.wait(c5)
    nf_ok = DV(dve.tensor_scalar(nf, ff, -1.0, None, ALU.mult))

    def fox_logits(g):
        def write(j, tb, out, s_):
            h = 4 * g + j
            c = causal[:, P:] if tb else causal[:, 0:P]
            return dve.scalar_tensor_tensor(out, s_, f_cols[:, tb * 16 + h:tb * 16 + h + 1], c, ALU.add, ALU.add)
        return write

    def fox_scores(g, *after):
        s_ok = scores(head(qT[g], 0), head(kT, 4 * g), (lambda j: sel[:, 4 * g + j, :], nf), *after)
        return softmax(probs, soft, fox_logits(g), s_ok, causal_ok)

    def fox_query(g):
        ok = project(qT[g], xs_a)
        DV.wait(ok)
        return DV(dve.tensor_scalar(qT[g], qT[g], DH ** -0.5, None, ALU.mult))

    def fox_keys(j):
        return project(kT[:, 2 * j:2 * j + 2, :], xs_b)

    def fox_output(n):
        return gemm(t_matmuls, 0, xs_b, 2 * n, n == 0, n == 3)

    PE.wait(q_ready)
    q_ok = fox_query(0)
    PE.wait(c5, bank_free[4])
    for tb in range(NT):
        last = pe.transpose(ps[:, 4, tb * 16:tb * 16 + 16], ff[:, tb * P:(tb + 1) * P], ident[0:16, 0:16])
    DV.wait(PE(last))
    fc_ok = DV(dve.tensor_copy(f_cols, ps[:, 4, 0:32]))
    e_ok = fox_scores(0, q_ok, fc_ok, causal_ok, nf_ok, k_ok, bank_free[6])
    k_ok = fox_keys(1)
    q_ok = fox_query(1)
    p_ok = divide(probs, e_ok)
    k_ok2 = fox_keys(2)
    pt_ok = turn_probs(probs, probs_t, p_ok)
    k_ok3 = fox_keys(3)
    AC.wait(k_ok3)
    o_ok0 = weigh(probs_t, values(vN, 0), xs_b, 0, pt_ok, v_ok, v_ok2)
    e_ok = fox_scores(1, q_ok, k_ok, o_ok0)
    q_ok2 = fox_query(2)
    p_ok = divide(probs, e_ok)
    q_ok3 = fox_query(3)
    pt_ok = turn_probs(probs, probs_t, p_ok, o_ok0)
    gate_ok = spread(10, row_gain[1], row_gain[2], 2, res_ok, q_ok2, q_ok3)
    o_ok1 = weigh(probs_t, values(vN, 4), xs_b, 2, pt_ok)
    e_ok = fox_scores(2, q_ok2, k_ok2, o_ok1)
    PE.wait(gate_ok, q_ok3)
    fox_output(0)
    p_ok = divide(probs, e_ok)
    fox_output(1)
    pt_ok = turn_probs(probs, probs_t, p_ok, o_ok1)
    o_ok2 = weigh(probs_t, values(vN, 8), xs_b, 4, pt_ok)
    e_ok = fox_scores(3, q_ok3, k_ok3, o_ok2)
    fox_output(2)
    p_ok = divide(probs, e_ok)
    pt_ok = turn_probs(probs, probs_t, p_ok, o_ok2)
    o_ok3 = weigh(probs_t, values(vN, 12), xs_b, 6, pt_ok)
    for place in (3, 4, 5):
        free[place] = [pt_ok, o_ok3]
    next_place = 3
    rows_ok = [row_load(0, t["ln1_g_2"][1], res_ok), row_load(2, t["ln1_b_2"][1], gate_ok)]
    ffn = ffn_load(t["ffn_w_gate_2"][1], t["ffn_w_up_2"][1], t["ffn_w_down_2"][1])
    PE.wait(o_ok3)
    done = fox_output(3)
    ready, y_read = layer_norm(done, tokens_out(0), row_gain[1], gate_ok, res_ok)
    scale, shift, f_ok = fold(0, "ln1", 1, 12, mods)
    turned = turn(scr, ready, 4, [o_ok3])
    xs_ready = take(turned, xs_a, scale, shift, f_ok)
    PO.wait(*rows_ok)
    res_ok = residual(ready, row_gain[0], row_gain[2], None, turned)
    PE.wait(y_read)
    feed_forward(2, ffn, xs_ready, xs_ready, res_ok)
    rows_ok = row_load(0, t["ln2_g_2"][1], res_ok)
    gate_ok = spread(13, row_gain[1], row_gain[2], 0, (F["up_sum"], 3 * TURNS), res_ok)
    rows_ok = [rows_ok, row_load(2, t["ln2_b_2"][1], gate_ok)]
    PE.wait(gate_ok)
    done = last_down(2)
    ready, y_read = layer_norm(done, tokens_out(4), row_gain[1], gate_ok, res_ok)
    DV.wait(*rows_ok)
    s_out = nc.alloc_semaphore("s_out")
    out = t["out"].rearrange("a (t p) n -> p (a t) n", p=P)
    for tb in range(NT):
        DV.wait(ready[tb])
        token = DV(dve.tensor_tensor(scr[tb], scr[tb], row_gain[0], ALU.mult))
        DV.wait(token)
        token = DV(dve.tensor_tensor(scr[tb], scr[tb], row_gain[2], ALU.add))
        sp.wait_ge(*token)
        sp.dma_start(out[:, tb, :], scr[tb]).then_inc(s_out, 16)
    sp.wait_ge(s_out, 16 * NT)


_INS = ['x', 'pre_mix_norm', 'post_mix_norm', 'pre_ffn_norm', 'post_ffn_norm', 'w_in', 'w_out', 'lru_conv_w',
        'lru_conv_b', 'lru_wa', 'lru_ba', 'lru_wx', 'lru_bx', 'lru_lambda', 'gla_gate_w2', 'gla_gate_b', 'gla_norm',
        'rel_bias', 'w_ffn_gate', 'w_ffn_up', 'w_ffn_down', 'c_2', 'w_ada_2', 'b_ada_2', 'conv_w_in_2', 'conv_w_2',
        'conv_w_out_2', 'w_ada_kv_2', 'b_ada_kv_2', 'w_k_2', 'w_v_2', 'w_f_2', 'b_f_2', 'attn_w_q_2', 'attn_w_o_2',
        'ffn_w_gate_2', 'ffn_w_up_2', 'ffn_w_down_2', 'ln1_g_2', 'ln1_b_2', 'ln2_g_2', 'ln2_b_2']


def bucket_onehot():
    n = 255 - np.arange(S)
    nf = np.maximum(n, 1).astype(np.float32)
    large = 16 + (np.log(nf / np.float32(16)) / np.float32(math.log(128 / 16)) * np.float32(16)).astype(np.int32)
    bucket = np.where(n < 16, n, np.minimum(large, 31))
    return (np.arange(32)[:, None] == bucket[None, :]).astype(np.float32)


def kernel(**inputs):
    import numpy as _np
    import concourse.bacc as _bacc
    from concourse import mybir as _mybir
    from concourse.bass_utils import run_bass_kernel_spmd as _run

    nc = _bacc.Bacc("TRN2", target_bir_lowering=False, num_devices=1)
    arrays, t = {}, {}
    for name in _INS:
        a = _np.ascontiguousarray(inputs[name])
        arrays[f"in_{name}"] = a
        t[name] = nc.dram_tensor(f"in_{name}", a.shape, _mybir.dt.from_np(a.dtype), kind="ExternalInput").ap()
    arrays["bucket_onehot"] = bucket_onehot()
    t["bucket_onehot"] = nc.dram_tensor("bucket_onehot", (32, S), _mybir.dt.float32, kind="ExternalInput").ap()
    t["bias_table"] = nc.dram_tensor("bias_table", (8, 512), _mybir.dt.float32, kind="Internal").ap()
    t["out"] = nc.dram_tensor("out_0", (1, S, D), _mybir.dt.float32, kind="ExternalOutput").ap()
    build(nc, t)
    r = _run(nc, [arrays], core_ids=[0])
    return r.results[0]["out_0"]
```

```python
import math

import numpy as np

import concourse.bass as bass
from concourse import mybir
from concourse.alu_op_type import AluOpType as ALU

F32 = mybir.dt.float32
F32R = mybir.dt.float32r
BF16 = mybir.dt.bfloat16
ACT = mybir.ActivationFunctionType
AX = mybir.AxisListType

P = 128
S = 256
NT = S // P
D = 1024
KB = D // P
DFF = 2816
COLS = 256
TURNS = DFF // COLS
SLOT = KB * COLS
NRAW, NHL, NADA = 6, 3, 2
AHEAD = 2
RMS_EPS, LN_EPS = 1e-6, 1e-5
DEEPNORM_ALPHA = 4.0 ** 0.25
NEG = -1.0e30
LRU, GLA_V, GLA_QK, RANK, MOBA = 256, 256, 128, 16, 512
OFF = dict(zip(("lru_x", "lru_g", "gq", "gk", "gv", "g_lr", "g_out", "mq", "mk", "mv"),
               np.cumsum([0, LRU, LRU, GLA_QK, GLA_QK, GLA_V, RANK, GLA_V, MOBA, MOBA]).tolist()))
CHUNK = 64
FOX_HEADS, DH = 16, 64


class Track:

    def __init__(self, nc, engine, name):
        self.engine, self.sem, self.n = engine, nc.alloc_semaphore(name), 0

    def __call__(self, instruction):
        instruction.then_inc(self.sem, 1)
        self.n += 1
        return (self.sem, self.n)

    def wait(self, *tokens):
        for token in tokens:
            if token is not None:
                self.engine.wait_ge(*token)


def build(nc, t):
    pe, act, dve, pool, sp = nc.tensor, nc.scalar, nc.vector, nc.gpsimd, nc.sync
    PE, AC, DV, PO = (Track(nc, e, n) for e, n in ((pe, "pe_done"), (act, "act_done"), (dve, "dve_done"), (pool, "pool_done")))

    def sb(name, shape, dt=F32):
        return nc.alloc_sbuf_tensor(name, list(shape), dt)

    raw = sb("raw", [P, NRAW, SLOT])
    hi = sb("hi", [P, NHL, SLOT], F32R)
    lo = sb("lo", [P, NHL, SLOT], F32R)
    ada_raw = sb("ada_raw", [P, NADA, SLOT])
    x_res = sb("x_res", [P, NT, D])
    xs_a = sb("xs_a", [P, KB, 2, S], F32R)
    xs_b = sb("xs_b", [P, KB, 2, S], F32R)
    half = sb("half", [P, 2, 2, S])
    WORK = 11264
    work = sb("work", [P, WORK])
    ident = sb("ident", [P, P])
    ones = sb("ones", [P, P])
    zeros16 = sb("zeros16", [P, P], BF16)
    cols_a = sb("cols_a", [P, 88])
    cols_b = sb("cols_b", [P, 96])
    cols_c = sb("cols_c", [P, 64])
    folded = sb("folded", [P, 2, 2, KB])
    ada_cols = sb("ada_cols", [P, 14 * KB])
    c_act = sb("c_act", [P, KB])
    small = sb("small", [P, 160])
    ps = nc.alloc_psum_tensor("ps", [P, 8, 512], F32)

    def view(base, at, *shape):
        n = int(np.prod(shape))
        ap = base[:, at:at + n]
        if len(shape) == 2:
            ap = ap.rearrange("p (a b) -> p a b", a=shape[0])
        if len(shape) == 3:
            ap = ap.rearrange("p (a b c) -> p a b c", a=shape[0], b=shape[1])
        return ap

    lent = raw[:, 3:6, :].rearrange("p a n -> p (a n)")

    raw_landed = [nc.alloc_semaphore(f"raw_landed{j}") for j in range(NRAW)]
    s_hi, s_lo, s_used = (nc.alloc_semaphore(n) for n in ("s_hi", "s_lo", "s_used"))
    ada_landed = [nc.alloc_semaphore(f"ada_landed{j}") for j in range(NADA)]
    s_ada_used, s_ada_mul = nc.alloc_semaphore("s_ada_used"), nc.alloc_semaphore("s_ada_mul")

    loads = [0] * NRAW
    where = {}
    free = [[] for _ in range(NRAW)]
    next_place = 0
    loaded, split_next, ada_loaded, ada_next, ada_muls = 0, 0, 0, 0, 0

    def load(source, place=None):
        nonlocal loaded, next_place
        if place is None:
            place, next_place = next_place, (next_place + 1) % NRAW
        for token in free[place]:
            sp.wait_ge(*token)
        s = loaded
        loads[place] += 1
        dst = raw[:, place, :].rearrange("p (k n) -> p k n", k=source.shape[1])
        if source.shape[1] * source.shape[2] < SLOT:
            dst = raw[:, place, :].rearrange("p (k n) -> p k n", k=KB)[:, :, 0:source.shape[2]]
        sp.dma_start(dst, source).then_inc(raw_landed[place], 16)
        where[s] = (place, 16 * loads[place])
        free[place] = [(s_lo, s + 1)]
        loaded += 1

    held = []

    def split(s=None, place=None, landed=None, s_value=None, hold=False):
        nonlocal split_next
        assert not held
        if s is None:
            s = s_value = split_next
            place, landed = where[s]
            split_next += 1
        h = s % NHL
        act.wait_ge(raw_landed[place], landed)
        if s >= NHL:
            act.wait_ge(s_used, s_value - NHL + 1)
        act.activation(hi[:, h, :], raw[:, place, :], ACT.Copy).then_inc(s_hi, 1)
        held.append((h, place, s_value))
        if not hold:
            lower_held()

    def lower_held():
        if not held:
            return
        h, place, s_value = held.pop()
        dve.wait_ge(s_hi, s_value + 1)
        dve.tensor_tensor(lo[:, h, :], raw[:, place, :], hi[:, h, :].bitcast(F32), ALU.subtract).then_inc(s_lo, 1)

    def f_source(w, col, n=COLS):
        return w.rearrange("(k p) n -> p k n", p=P)[:, :, col:col + n]

    def t_source(w, row):
        return w[row:row + 2 * P, :].rearrange("(k p) n -> p k n", p=P)

    def f_matmuls(h, bank, xs, blocks=2, xs_in=None):
        for b in range(blocks):
            out = ps[:, bank + b, :]
            for k in range(KB):
                w = slice(k * COLS + b * P, k * COLS + b * P + P)
                if xs_in is not None and b == 0 and k % 2 == 0:
                    PE.wait(xs_in[k // 2])
                if k:
                    pe.matmul(out[:, 0:S], lo[:, h, w], xs[:, k, 0, :], start=False, stop=False)
                last = pe.matmul(out, hi[:, h, w], xs[:, k, :, :].rearrange("p a n -> p (a n)"),
                                 start=(k == 0), stop=(k == KB - 1))
                if not k:
                    pe.matmul(out[:, 0:S], lo[:, h, w], xs[:, k, 0, :], start=False, stop=False)
        return last

    first_block = [None]

    def t_matmuls(h, base, xs, k0, first, final):
        for tb in range(NT):
            tok = slice(tb * P, tb * P + P)
            for k in range(2):
                for half_, (xpart, wpart) in [(a, b) for b in ((0, hi), (0, lo), (1, hi)) for a in range(2)]:
                    w = wpart[:, h, k * D + half_ * 512:k * D + half_ * 512 + 512]
                    start = first and k == 0 and xpart == 0 and wpart is hi
                    stop = final and k == 1 and xpart == 1
                    last = pe.matmul(ps[:, base + 2 * tb + half_, :], xs[:, k0 + k, xpart, tok], w,
                                     start=start, stop=stop, skip_group_check=True)
            if final and tb == 0:
                first_block[0] = PE(last)
        return last

    def v_matmuls(h, bank, xs):
        for tb in range(NT):
            out, tok = ps[:, bank, tb * S:tb * S + S], slice(tb * P, tb * P + P)
            for k in range(KB):
                w = slice(k * COLS, k * COLS + COLS)
                for n, (xpart, wpart) in enumerate(((0, hi), (0, lo), (1, hi))):
                    last = pe.matmul(out, xs[:, k, xpart, tok], wpart[:, h, w],
                                     start=(k == 0 and n == 0), stop=(k == KB - 1 and n == 2))
        return last

    gemm_next = 0

    def gemm(kind, *args, hold=False):
        nonlocal gemm_next
        s = gemm_next
        gemm_next += 1
        while split_next <= min(s + AHEAD, loaded - 1):
            split(hold=hold and split_next == s + AHEAD)
        pe.wait_ge(s_lo, s + 1)
        kind(s % NHL, *args).then_inc(s_used, 1)
        return (s_used, s + 1)

    acc = view(work, 0, 7, D)

    def ada_source(w, col, part):
        return w[part * 2 * P:(part + 1) * 2 * P, :].rearrange("(k p) n -> p k n", p=P)[:, :, col:col + D]

    ada_queue = []

    def ada_fill():
        nonlocal ada_loaded
        while ada_queue and ada_loaded < ada_next + NADA:
            q = ada_loaded
            if q >= NADA:
                pool.wait_ge(s_ada_used, q - NADA + 1)
            pool.dma_start(ada_raw[:, q % NADA, :].rearrange("p (k n) -> p k n", k=2), ada_queue.pop(0)).then_inc(ada_landed[q % NADA], 16)
            ada_loaded += 1

    def ada_multiply(dst, part, q_place, landed, muls):
        dve.wait_ge(ada_landed[q_place], landed)
        for k in range(2):
            w = ada_raw[:, q_place, k * D:(k + 1) * D]
            scalar = c_act[:, 2 * part + k:2 * part + k + 1]
            if part == 0 and k == 0:
                last = dve.tensor_scalar(dst, w, scalar, None, ALU.mult)
            else:
                dve.wait_ge(s_ada_mul, muls + k)
                last = dve.scalar_tensor_tensor(dst, w, scalar, dst, ALU.mult, ALU.add)
            last.then_inc(s_ada_mul, 1)
        dve.wait_ge(s_ada_mul, muls + 2)
        dve.sem_inc(s_ada_used, 1)

    def ada_step(index, part):
        nonlocal ada_next, ada_muls
        q = ada_next
        ada_multiply(acc[:, index, :], part, q % NADA, 16 * (q // NADA + 1), ada_muls)
        ada_next += 1
        ada_muls += 2
        ada_fill()

    def ada_finish(pairs, bank, *after):
        PE.wait((s_ada_mul, ada_muls), *after)
        for n, (chunk, index) in enumerate(pairs):
            for b in range(KB):
                last = pe.matmul(ps[:, bank, n * KB + b:n * KB + b + 1], acc[:, index, b * P:(b + 1) * P], ones[:, 0:1],
                                 start=True, stop=True)
        return pairs, bank, PE(last)

    def ada_columns(summed):
        pairs, bank, token = summed
        DV.wait(token)
        tokens = []
        for n, (chunk, index) in enumerate(pairs):
            kv = row_at["b_ada_kv_2"]
            if chunk < 6:
                bias, at = cols_b[:, 0:48], chunk * KB
            elif chunk < 8:
                bias, at = cols_a[:, kv:kv + 16], (chunk - 6) * KB
            else:
                bias, at = cols_b[:, 48:96], (chunk - 8) * KB
            dst = ada_cols[:, chunk * KB:(chunk + 1) * KB]
            tokens.append(DV(dve.tensor_tensor(dst, ps[:, bank, n * KB:(n + 1) * KB], bias[:, at:at + KB], ALU.add)))
            if chunk in (1, 4, 7, 9, 12):
                DV.wait(tokens[-1])
                tokens[-1] = DV(dve.tensor_scalar(dst, dst, 1.0, None, ALU.add))
        return tokens[-1]

    def diagonal(chunk, scratch, *after):
        PO.wait(*after)
        out = scratch.rearrange("p (a n) -> p a n", a=KB)
        column = ada_cols[:, chunk * KB:(chunk + 1) * KB]
        return PO(pool.tensor_tensor(out, ident[:, None, :].to_broadcast([P, KB, P]),
                                     column[:, :, None].to_broadcast([P, KB, P]), ALU.mult))

    def spread(diagonals, dst, scratch, bank, *after):
        PE.wait(diagonals, *after)
        for b in range(KB):
            last = pe.matmul(ps[:, bank + b // 4, (b % 4) * P:(b % 4) * P + P], ones[:, :], scratch[:, b * P:(b + 1) * P],
                             start=True, stop=True)
        AC.wait(PE(last))
        return AC(act.activation(dst, ps[:, bank:bank + 2, :].rearrange("p a n -> p (a n)"), ACT.Copy))

    small_landed = [nc.alloc_semaphore(f"small_landed{n}") for n in range(13)]
    n_small = [0] * 13

    def small_load(engine, group, dst, src):
        engine.dma_start(dst, src).then_inc(small_landed[group], 16)
        n_small[group] += 16
        return (small_landed[group], n_small[group])

    def as_rows(vector):
        letters = " ".join("abcd"[:len(vector.shape)])
        if len(vector.shape) > 1:
            vector = vector.rearrange(f"{letters} -> ({letters})")
        return vector.rearrange("(r p) -> r p", p=P)

    x_view = t["x"].rearrange("a (t p) n -> p (a t) n", p=P)
    x_in = [small_load(sp, tb, x_res[:, tb, :], x_view[:, tb, :]) for tb in range(NT)]
    turns = [0]

    def either():
        turns[0] += 1
        return (sp, act, sp)[turns[0] % 3]

    rows_a, rows_b, rows_c = (view(work, 10240 + P * n, P) for n in range(3))
    row_at, n_rows = {}, 0
    for name in ("pre_mix_norm", "pre_ffn_norm", "c_2", "lru_conv_w", "lru_conv_b", "lru_ba", "lru_bx", "lru_lambda",
                 "gla_gate_b", "gla_norm", "conv_w_2", "b_ada_kv_2"):
        flat = as_rows(t[name])
        rows_in = small_load(*((act, 12) if n_rows == 0 else (either(), 2)), rows_a[n_rows:n_rows + flat.shape[0], :], flat)
        row_at[name] = n_rows
        if n_rows == 0:
            first_in = rows_in
            load(f_source(t["w_in"][0], OFF["g_lr"]), 2)
        n_rows += flat.shape[0]
    rows_in = small_load(either(), 2, rows_b[0:96, :], as_rows(t["b_ada_2"]))
    onehot = view(work, 9216, S)[0:32, :]
    rel = view(work, 9472, 8)[0:32, :]
    rel_in = small_load(either(), 3, onehot, t["bucket_onehot"])
    rel_in = small_load(either(), 3, rel, t["rel_bias"])
    ln_at = {}
    for n, name in enumerate(("ln1_g_2", "ln1_b_2", "ln2_g_2", "ln2_b_2")):
        ln_at[name] = n * 16
        ln_in = small_load(either(), 4, rows_c[n * 16:n * 16 + 16, :], as_rows(t[name]))
    gate_w2 = small[0:RANK, 32:160]
    w2_in = small_load(either(), 5, gate_w2, t["gla_gate_w2"][0])
    b_f = small[0:FOX_HEADS, 0:1]
    w2_in = small_load(either(), 5, b_f, t["b_f_2"].rearrange("(h a) -> h a", a=1))

    def col(name, n=0):
        return cols_a[:, row_at[name] + n:row_at[name] + n + 1]

    def serial(instruction):
        token = PO(instruction)
        PO.wait(token)
        return token

    masks = sb("masks", [P, 264])
    gla_mask = masks[:, 0:128]
    head_ones = masks[:, 128:256]
    head_cols = masks[:, 256:260]
    pow_half = masks[:, 260:262]
    serial(pool.memset(ident[:, :], 0.0))
    ident_ok = serial(pool.affine_select(out=ident[:, :], in_=ident[:, :], compare_op=ALU.not_equal, fill=1.0, base=0,
                                         pattern=[[-1, P]], channel_multiplier=1))
    serial(pool.memset(pow_half, -0.5))

    scr = [view(work, 6 * D + n * D, D) for n in range(2)]
    row_gain = [view(work, 8 * D + n * D, D) for n in range(3)]
    stats = small[:, 4:32]
    norm_cols = sb("norm_cols", [P, NT, 16])
    squares = half[:, :, :, :].rearrange("p a b n -> p (a b n)")
    half_free = [None, None]
    halves, which = [0], [0]

    def next_half():
        halves[0] ^= 1
        return halves[0]

    def rstd(mean_square, dst, eps, scale, *after):
        PO.wait(*after)
        a = PO(pool.tensor_scalar(dst, mean_square, scale, eps, ALU.mult, ALU.add))
        PO.wait(a)
        return PO(pool.tensor_tensor(dst, dst, pow_half[:, 0:dst.shape[1]], ALU.pow))

    def split_into(dst, k, source, ready):
        AC.wait(ready)
        h_ok = AC(act.activation(dst[:, k:k + 2, 0, :], source, ACT.Copy))
        DV.wait(h_ok, ready)
        return DV(dve.tensor_tensor(dst[:, k:k + 2, 1, :], source, dst[:, k:k + 2, 0, :].bitcast(F32), ALU.subtract))

    def turn(source, ready, base, bank_free):
        got = []
        for tb in range(NT):
            PE.wait(ready[tb], *(bank_free if tb == 0 else ()))
            for k in range(KB):
                at = (k % 2) * S + tb * P
                tr = pe.transpose(ps[:, base + k // 2, at:at + P], source[tb][:, k * P:(k + 1) * P], ident[:, :])
                if tb == NT - 1 and k % 2:
                    got.append(PE(tr))
        return base, got

    def take(turned, dst, scale, shift=None, *after):
        base, got = turned
        AC.wait(*after)
        DV.wait(*after)
        pending, out = None, []

        def lower(j, h, hi_ok, tmp_ok):
            DV.wait(hi_ok, tmp_ok)
            half_free[h] = DV(dve.tensor_tensor(dst[:, 2 * j:2 * j + 2, 1, :], half[:, h, :, :],
                                                dst[:, 2 * j:2 * j + 2, 0, :].bitcast(F32), ALU.subtract))
            return half_free[h]

        for j in range(KB // 2):
            h = next_half()
            for k in (2 * j, 2 * j + 1):
                src, tmp = ps[:, base + j, (k % 2) * S:(k % 2) * S + S], half[:, h, k % 2, :]
                if j % 2:
                    AC.wait(got[j], half_free[h])
                    more = {} if shift is None else {"bias": shift(k)}
                    tmp_ok = AC(act.activation(tmp, src, ACT.Copy if shift is None else ACT.Identity, scale=scale(k), **more))
                else:
                    DV.wait(got[j], half_free[h])
                    if shift is None:
                        tmp_ok = DV(dve.tensor_scalar(tmp, src, scale(k), None, ALU.mult))
                    else:
                        tmp_ok = DV(dve.tensor_scalar(tmp, src, scale(k), shift(k), ALU.mult, ALU.add))
            AC.wait(tmp_ok)
            hi_ok = AC(act.activation(dst[:, 2 * j:2 * j + 2, 0, :], half[:, h, :, :], ACT.Copy))
            if pending is not None:
                out.append(lower(*pending))
            pending = (j, h, hi_ok, tmp_ok)
        out.append(lower(*pending))
        return out

    def f_sum(bank, done, dst, *dst_free):
        h = next_half()
        AC.wait(done, half_free[h])
        low = AC(act.activation(half[:, h, :, :], ps[:, bank:bank + 2, S:2 * S], ACT.Copy))
        DV.wait(low, *dst_free)
        token = DV(dve.tensor_tensor(dst, ps[:, bank:bank + 2, 0:S], half[:, h, :, :], ALU.add))
        half_free[h] = token
        return token

    def f_sum16(bank, done, dst, *dst_free):
        h = next_half()
        AC.wait(done, half_free[h])
        low = AC(act.activation(half[0:16, h, 0, :], ps[0:16, bank, S:2 * S], ACT.Copy))
        DV.wait(low, *dst_free)
        token = DV(dve.tensor_tensor(dst, ps[0:16, bank, 0:S], half[0:16, h, 0, :], ALU.add))
        half_free[h] = token
        return token

    def closed(done):
        return first_block[0], done

    def tokens_out(base):
        return [ps[:, base + 2 * tb:base + 2 * tb + 2, :].rearrange("p a n -> p (a n)") for tb in range(NT)]

    def add_rms(done, Y, gain, gain_ok, scratch_free=None):
        out, r_ok = [], []
        for tb in range(NT):
            ss, r = stats[:, tb:tb + 1], stats[:, 2 + tb:3 + tb]
            AC.wait(done[tb], scratch_free)
            sq = AC(act.activation(scr[tb], Y[tb], ACT.Square, accum_out=ss))
            r_ok.append(rstd(ss, r, RMS_EPS, 1.0 / D, sq))
        for tb in range(NT):
            DV.wait(r_ok[tb], gain_ok)
            a = DV(dve.scalar_tensor_tensor(scr[tb], Y[tb], stats[:, 2 + tb:3 + tb], gain, ALU.mult, ALU.mult))
            DV.wait(a)
            out.append(DV(dve.tensor_tensor(x_res[:, tb, :], x_res[:, tb, :], scr[tb], ALU.add)))
        return out

    def normed(ready, on_vector=False):
        out, r_ok = [], []
        for tb in range(NT):
            ss, r = stats[:, 4 + tb:5 + tb], stats[:, 6 + tb:7 + tb]
            if on_vector:
                DV.wait(ready[tb])
                sq = DV(dve.scalar_tensor_tensor(scr[tb], x_res[:, tb, :], 1.0, x_res[:, tb, :], ALU.mult, ALU.mult, accum_out=ss))
            else:
                AC.wait(ready[tb])
                sq = AC(act.activation(scr[tb], x_res[:, tb, :], ACT.Square, accum_out=ss))
            r_ok.append(rstd(ss, r, RMS_EPS, 1.0 / D, sq))
        for tb in range(NT):
            DV.wait(r_ok[tb])
            out.append(DV(dve.tensor_scalar(scr[tb], x_res[:, tb, :], stats[:, 6 + tb:7 + tb], None, ALU.mult)))
            lower_held()
        return out

    def layer_norm(done, Y, gate, gate_ok, *scratch_free):
        norm = []
        DV.wait(gate_ok, *scratch_free)
        for tb in range(NT):
            DV.wait(done[tb])
            a = DV(dve.tensor_tensor(scr[tb], Y[tb], gate, ALU.mult))
            DV.wait(a)
            total, minus_mean, square, r, shift = (norm_cols[:, tb, n:n + 1] for n in range(5))
            z = DV(dve.scalar_tensor_tensor(scr[tb], x_res[:, tb, :], DEEPNORM_ALPHA, scr[tb], ALU.mult, ALU.add, accum_out=total))
            PO.wait(z)
            AC.wait(PO(pool.tensor_scalar(minus_mean, total, -1.0 / D, None, ALU.mult)))
            sq = AC(act.activation(squares, scr[tb], ACT.Square, bias=minus_mean, accum_out=square))
            norm.append(rstd(square, r, LN_EPS, 1.0 / D, sq))
            PO.wait(norm[-1])
            norm[-1] = PO(pool.tensor_tensor(shift, minus_mean, r, ALU.mult))
        out = []
        for tb in range(NT):
            total, minus_mean, square, r, shift = (norm_cols[:, tb, n:n + 1] for n in range(5))
            if tb == 0:
                DV.wait(norm[tb])
                out.append(DV(dve.tensor_scalar(scr[tb], scr[tb], r, shift, ALU.mult, ALU.add)))
                lower_held()
            else:
                AC.wait(norm[tb])
                out.append(AC(act.activation(scr[tb], scr[tb], ACT.Identity, bias=shift, scale=r)))
        return out, a

    def residual(ready, gain, bias, rows_ok, turned):
        for tb in range(NT):
            PO.wait(ready[tb], rows_ok, turned[1][-1])
            serial(pool.tensor_tensor(scr[tb], scr[tb], gain, ALU.mult))
            token = serial(pool.tensor_tensor(x_res[:, tb, :], scr[tb], bias, ALU.add))
        return token

    def acol(chunk):
        return lambda k: ada_cols[:, chunk * KB + k:chunk * KB + k + 1]

    def fold(n, ln, layer, scale_chunk, after):
        g, b = (cols_c[:, ln_at[ln + x] + layer * KB:ln_at[ln + x] + (layer + 1) * KB] for x in ("_g_2", "_b_2"))
        sc = ada_cols[:, scale_chunk * KB:(scale_chunk + 1) * KB]
        sh = ada_cols[:, (scale_chunk - 1) * KB:scale_chunk * KB]
        DV.wait(after)
        DV(dve.tensor_tensor(folded[:, n, 0, :], g, sc, ALU.mult))
        c = DV(dve.tensor_tensor(folded[:, n, 1, :], b, sc, ALU.mult))
        DV.wait(c)
        c = DV(dve.tensor_tensor(folded[:, n, 1, :], folded[:, n, 1, :], sh, ALU.add))
        return (lambda k: folded[:, n, 0, k:k + 1]), (lambda k: folded[:, n, 1, k:k + 1]), c

    def row_load(n, source, *after):
        PO.wait(*after)
        flat = bass.AP(tensor=source.tensor, offset=source.offset, ap=[[0, P], [1, D]])
        with nc.allow_non_contiguous_dma(reason="one row on all partitions"):
            return small_load(pool, 9 + n, row_gain[n], flat)

    QUERY_BLOCKS = ((0, P), (P, S))

    HEAD_ORDER = (1, 2, 3, 0)

    def scores(q, k, minus_f=None, *after, bank_4=None):
        PE.wait(*after)
        done = {}
        for j in HEAD_ORDER:
            if j == 0:
                PE.wait(bank_4)
            if minus_f is not None:
                pick, parts = minus_f
                for n in range(2):
                    pe.matmul(ps[:, 4 + j, 0:P + S], pick(j), parts[n], start=(n == 0), stop=False, skip_group_check=True)
            for at, n in QUERY_BLOCKS:
                tb = at // P
                last = pe.matmul(ps[:, 4 + j, at:at + n], q(j)[:, tb * P:tb * P + P], k(j)[:, 0:n], start=(minus_f is None), stop=True,
                                 skip_group_check=True)
            done[j] = PE(last)
        return done

    def softmax(probs, tile, logits, done, *free_):
        DV.wait(*free_)
        for j in HEAD_ORDER:
            DV.wait(done[j])
            for tb, (at, n) in enumerate(QUERY_BLOCKS):
                read = DV(logits(j, tb, probs[:, j, at:at + n], ps[:, 4 + j, at:at + n]))
        DV.wait(read)
        neg, total = tile[:, 0:8], tile[:, 8:16]
        for tb, (at, n) in enumerate(QUERY_BLOCKS):
            m = DV(dve.tensor_reduce(neg[:, tb * 4:tb * 4 + 4], probs[:, :, at:at + n], AX.X, ALU.max))
        DV.wait(m)
        m = DV(dve.tensor_scalar(neg, neg, -1.0, None, ALU.mult))
        AC.wait(m)
        for j in range(4):
            for tb, (at, n) in enumerate(QUERY_BLOCKS):
                e = AC(act.activation(probs[:, j, at:at + n], probs[:, j, at:at + n], ACT.Exp,
                                      bias=neg[:, tb * 4 + j:tb * 4 + j + 1], accum_out=total[:, tb * 4 + j:tb * 4 + j + 1]))
        return e, total

    def divide(probs, summed):
        e, total = summed
        DV.wait(e)
        DV.wait(DV(dve.reciprocal(total, total)))
        out = []
        for j in range(4):
            for tb, (at, n) in enumerate(QUERY_BLOCKS):
                ok = DV(dve.tensor_scalar(probs[:, j, at:at + n], probs[:, j, at:at + n], total[:, tb * 4 + j:tb * 4 + j + 1], None, ALU.mult))
            out.append(ok)
        return out

    def turn_probs(probs, probs_t, ready, *free_):
        for j in range(4):
            PE.wait(ready[j])
            for c in range(3):
                tr = pe.transpose(ps[:, 4 + j, c * P:(c + 1) * P], probs[:, j, c * P:(c + 1) * P], ident[:, :])
            AC.wait(PE(tr), *free_)
            last = AC(act.activation(probs_t[:, j, :], ps[:, 4 + j, 0:384], ACT.Copy))
        return last

    def weigh(probs_t, values, dst, k, ready, *after):
        PE.wait(ready, *after)
        for j in range(4):
            out = ps[64 * (j % 2):64 * (j % 2) + 64, 4, (j // 2) * S:(j // 2) * S + S]
            pe.matmul(out, values(0, j), probs_t[:, j, 0:S], start=True, stop=False, skip_group_check=True)
            last = pe.matmul(out[:, P:S], values(1, j), probs_t[:, j, S:S + P], start=False, stop=True, skip_group_check=True)
        return split_into(dst, k, ps[:, 4, :].rearrange("p (a n) -> p a n", a=2), PE(last))

    def values(tile, j0):
        return lambda kb, j: tile[:, kb, 64 * (j0 + j):64 * (j0 + j) + 64]

    def head(tile, j0):
        return lambda j: tile[64 * (j % 2):64 * (j % 2) + 64, (j0 + j) // 2, :]

    bank_free = {0: None, 2: None, 4: None, 6: None}

    def next_bank(bank):
        if bank is None:
            which[0] ^= 2
            bank = which[0]
        return bank

    def project(dst, xs, *dst_free, bank=None, xs_in=None):
        b = next_bank(bank)
        PE.wait(bank_free[b])
        bank_free[b] = f_sum(b, gemm(f_matmuls, b, xs, 2, xs_in), dst, *dst_free)
        return bank_free[b]

    def project16(dst, xs, *dst_free, bank=None, xs_in=None):
        b = next_bank(bank)
        PE.wait(bank_free[b])
        bank_free[b] = f_sum16(b, gemm(f_matmuls, b, xs, 1, xs_in), dst, *dst_free)
        return bank_free[b]

    def project_v(dst, xs, *dst_free):
        b = next_bank(None)
        PE.wait(bank_free[b])
        AC.wait(gemm(v_matmuls, b, xs), *dst_free)
        bank_free[b] = AC(act.activation(dst, ps[:, b, :].rearrange("p (a n) -> p a n", a=NT), ACT.Copy))
        return bank_free[b]

    w_in, w_out = t["w_in"][0], t["w_out"][0]
    order = ["g_lr", "gq", "mq", "mk", "lru_x", "gv", "mv", "mq+", "mk+", "mv+", "lru_g", "g_out"]
    for n, name in list(enumerate(order))[1:]:
        load(f_source(w_in, OFF[name.strip("+")] + COLS * name.count("+")), (n + 2) % 3)
    for n, row in enumerate((512, 768, 0, 256)):
        load(t_source(w_out, row), (len(order) + n + 2) % 3)
    ada_queue += [ada_source(t["w_ada_2"][0], 0, part) for part in range(4)]

    mq, mk = view(work, 1024, 4, S), view(work, 2048, 4, S)
    mv = view(work, 3072, NT, MOBA)
    moba_bias = view(work, 4096, 8, S)
    probs, probs_t = view(work, 6144, 4, 384), view(work, 7680, 4, 384)
    gqk, gout, gv, lru_g = (view(work, 9216 + 512 * n, 2, S) for n in range(4))
    from_last = view(lent, 0, 8, S)
    xpad = view(lent, 0, 2, S + 3)
    xc = view(lent, 520, 2, S)
    ri = view(lent, 1032, 4, S)
    aa, uu, hh, tt = (view(lent, 2056 + 512 * n, 2, S) for n in range(4))
    zz, ee, cum, qd = (view(lent, 4104 + 256 * n, S) for n in range(4))
    wab = view(lent, 5128, 4, P)
    glr = view(lent, 5640, S)[0:16, :]
    kd = view(work, 6144, 4, S)
    klast_t = view(work, 7168, NT, P)
    oo, osq = view(work, 7424, 2, S), view(work, 7936, 2, S)
    attn = view(work, 1024, 8, P)
    state = view(work, 2048, 3, S)
    soft, soft2 = sb("soft", [P, 16]), sb("soft2", [P, 16])

    x_ready = normed(x_in, on_vector=True)

    ones_ok = serial(pool.memset(ones[:, :], 1.0))
    table = view(work, 9728, 512)[0:8, :]
    t0 = serial(pool.memset(table, NEG))
    flip = view(lent, 4872, P)
    serial(pool.memset(flip, 0.0))
    flip_ok = serial(pool.affine_select(out=flip, in_=flip, compare_op=ALU.not_equal, fill=1.0, base=1 - P, pattern=[[1, P]],
                                        channel_multiplier=1))

    PE.wait(first_in, ident_ok)
    first_t = PE(pe.transpose(ps[:, 2, 0:8], rows_a[0:8, :], ident[0:8, 0:8]))
    turned = turn(scr, x_ready, 4, [])
    DV.wait(first_t)
    cols_ok = DV(dve.tensor_copy(cols_a[:, 0:8], ps[:, 2, 0:8]))
    split()
    PE.wait(rows_in, ln_in, rel_in, cols_ok)
    pe.transpose(ps[:, 2, 0:n_rows], rows_a[0:n_rows, :], ident[0:n_rows, 0:n_rows])
    pe.transpose(ps[:, 3, 0:96], rows_b[0:96, :], ident[0:96, 0:96])
    pe.transpose(ps[:, 3, 96:160], rows_c[0:64, :], ident[0:64, 0:64])
    rows_t = PE(pe.matmul(ps[0:8, 1, 0:S], rel, onehot, start=True, stop=True))
    xs_ready = take(turned, xs_a, lambda k: col("pre_mix_norm", k), None, cols_ok)
    DV.wait(rows_t, t0)
    DV(dve.tensor_copy(cols_a[:, 8:n_rows], ps[:, 2, 8:n_rows]))
    DV(dve.tensor_copy(cols_b[:, :], ps[:, 3, 0:96]))
    DV(dve.tensor_copy(cols_c[:, :], ps[:, 3, 96:160]))
    table_ok = colsb_ok = DV(dve.tensor_copy(table[:, 0:S], ps[0:8, 1, 0:S]))
    glr_ok = project16(glr, xs_a, bank=0, xs_in=xs_ready)
    PO.wait(table_ok)
    written = small_load(pool, 6, t["bias_table"], table)
    serial(pool.memset(gla_mask, 1.0))
    serial(pool.memset(masks[:, 128:260], 0.0))
    serial(pool.affine_select(out=gla_mask, in_=gla_mask, compare_op=ALU.is_ge, fill=0.0, base=0, pattern=[[1, P]],
                              channel_multiplier=-1))
    serial(pool.memset(gla_mask[0:64, 64:128], 0.0))
    for h in range(2):
        serial(pool.memset(head_ones[64 * h:64 * h + 64, 64 * h:64 * h + 64], 1.0))
    for h in range(4):
        masks_ok = serial(pool.memset(head_cols[32 * h:32 * h + 32, h:h + 1], 1.0))
    serial(pool.memset(zeros16[:, :], 0.0))
    PO.wait(written)
    toeplitz = bass.AP(tensor=t["bias_table"].tensor, offset=t["bias_table"].offset, ap=[[1, P], [512, 8], [1, S]])
    with nc.allow_non_contiguous_dma(reason="Toeplitz rows overlap"):
        bias_in = small_load(pool, 7, from_last, toeplitz)
    serial(pool.memset(wab, 0.0))
    for g in range(4):
        part = slice(64 * (g % 2), 64 * (g % 2) + 64)
        small_load(pool, 8, wab[part, g // 2, part], t["lru_wa"][0, g])
        wab_in = small_load(pool, 8, wab[part, 2 + g // 2, part], t["lru_wx"][0, g])
    bank_free[2] = colsb_ok
    bank_free[4] = bank_free[6] = xs_ready[-1]
    which[0] = 2

    def moba_logits(g):
        def write(j, tb, out, s_):
            b = moba_bias[:, 4 * g + j, :] if tb else moba_bias[:, 4 * g + j, P:S]
            return dve.scalar_tensor_tensor(out, s_, DH ** -0.5, b, ALU.mult, ALU.add)
        return write

    def conv(dst, src, taps, weight, bias, ready, *free_):
        DV.wait(ready, *free_)
        for b in range(2):
            if bias is None:
                token = DV(dve.tensor_scalar(dst[:, b, :], src[:, b, 0:S], weight(0, b), None, ALU.mult))
            else:
                token = DV(dve.tensor_scalar(dst[:, b, :], src[:, b, 0:S], weight(0, b), bias(b), ALU.mult, ALU.add))
        for j in range(1, taps):
            DV.wait(token)
            for b in range(2):
                token = DV(dve.scalar_tensor_tensor(dst[:, b, :], src[:, b, j:j + S], weight(j, b), dst[:, b, :], ALU.mult, ALU.add))
        return token

    PE.wait(table_ok)
    qk_ok = project(gqk, xs_a, bank=2)
    PE.wait(flip_ok, bias_in, bank_free[4])
    for n in range(4):
        last = pe.matmul(ps[:, 4 + n, :], flip, from_last[:, 2 * n:2 * n + 2, :].rearrange("p a n -> p (a n)"), start=True, stop=True)
    AC.wait(PE(last))
    bias_ok = AC(act.activation(moba_bias.rearrange("p a n -> p (a n)"), ps[:, 4:8, :].rearrange("p a n -> p (a n)"), ACT.Copy))
    q_ok = project(mq[:, 0:2, :], xs_a)
    PE.wait(w2_in, glr_ok, bias_ok)
    gz = PE(pe.matmul(ps[:, 5, 0:S], gate_w2, glr, start=True, stop=True))
    DV.wait(gz)
    c1 = DV(dve.tensor_scalar(zz, ps[:, 5, 0:S], col("gla_gate_b"), None, ALU.add))
    k_ok = project(mk[:, 0:2, :], xs_a)
    AC.wait(cols_ok)
    c_cols = cols_a[:, row_at["c_2"]:row_at["c_2"] + KB]
    c_sig = AC(act.activation(c_act[:, :], c_cols, ACT.Sigmoid))
    DV.wait(c_sig)
    c_ok = DV(dve.tensor_tensor(c_act[:, :], c_act[:, :], c_cols, ALU.mult))
    DV.wait(c_ok)
    ada_fill()

    PO.wait(bias_ok)
    pz = serial(pool.memset(xpad[:, :, 0:3], 0.0))
    lx_ok = project(xpad[:, :, 3:], xs_a, pz)
    s_ok = scores(head(mq, 0), head(mk, 0), None, q_ok, k_ok, c1)
    e_ok = softmax(probs, soft, moba_logits(0), s_ok, bias_ok)
    p_ok = divide(probs, e_ok)
    AC.wait(c1)
    c2 = AC(act.activation(ee, zz, ACT.Abs)); AC.wait(c2)
    c2 = AC(act.activation(ee, ee, ACT.Exp, scale=-1.0)); AC.wait(c2)
    c2 = AC(act.activation(ee, ee, ACT.Ln, bias=1.0))
    gv_ok = project_v(gv, xs_a)
    pt_ok = turn_probs(probs, probs_t, p_ok)
    xc_ok = conv(xc, xpad, 4, lambda j, b: col("lru_conv_w", 2 * j + b), lambda b: col("lru_conv_b", b), lx_ok)
    ada_step(0, 0)
    v_ok = project_v(mv[:, :, 0:COLS], xs_a)
    o_ok = weigh(probs_t, values(mv, 0), xs_b, 4, pt_ok, v_ok)
    q_ok = project(mq[:, 2:4, :], xs_a)
    DV.wait(c2)
    c3 = DV(dve.tensor_scalar(zz, zz, 0.0, 1.0 / 16, ALU.min, ALU.mult)); DV.wait(c3)
    c3 = DV(dve.scalar_tensor_tensor(zz, ee, -1.0 / 16, zz, ALU.mult, ALU.add)); DV.wait(c3, ones_ok)
    for c in range(S // CHUNK):
        part = slice(c * CHUNK, (c + 1) * CHUNK)
        cum_ok = DV(dve.tensor_tensor_scan(cum[:, part], ones[:, 0:CHUNK], zz[:, part], 0.0, ALU.mult, ALU.add))
    ada_step(0, 1)
    k_ok = project(mk[:, 2:4, :], xs_a)
    v_ok = project_v(mv[:, :, COLS:], xs_a)
    s_ok = scores(head(mq, 4), head(mk, 4), None, q_ok, k_ok, pt_ok, bank_4=o_ok)
    e_ok = softmax(probs, soft, moba_logits(1), s_ok, pt_ok)
    b = next_bank(None)
    PE.wait(xc_ok, wab_in, bank_free[b])
    for n in range(4):
        last = pe.matmul(ps[:, b + n // 2, (n % 2) * S:(n % 2) * S + S], wab[:, n, :], xc[:, n % 2, :], start=True, stop=True)
    gates = PE(last)
    p_ok = divide(probs, e_ok)
    AC.wait(gates)
    for n in range(4):
        ri_ok = AC(act.activation(ri[:, n, :], ps[:, b + n // 2, (n % 2) * S:(n % 2) * S + S], ACT.Sigmoid,
                                  bias=col("lru_ba" if n < 2 else "lru_bx", n % 2)))
    bank_free[b] = ri_ok
    lam = cols_a[:, row_at["lru_lambda"]:row_at["lru_lambda"] + 2]
    sv = lambda n: soft2[:, 2 * n:2 * n + 2]
    a0 = AC(act.activation(sv(0), lam, ACT.Abs))
    AC.wait(a0)
    a1 = AC(act.activation(sv(0), sv(0), ACT.Exp, scale=-1.0))
    DV.wait(a1)
    a2 = DV(dve.tensor_scalar(sv(1), sv(0), 2.0, None, ALU.add)); DV.wait(a2)
    a2 = DV(dve.reciprocal(sv(1), sv(1))); PO.wait(a2)
    serial(pool.tensor_tensor(sv(1), sv(1), sv(0), ALU.mult))
    serial(pool.tensor_tensor(sv(2), sv(1), sv(1), ALU.mult))
    serial(pool.tensor_scalar(sv(3), sv(2), 1.0 / 17, 1.0 / 15, ALU.mult, ALU.add))
    for m in (13, 11, 9, 7, 5, 3, 1):
        serial(pool.tensor_tensor(sv(3), sv(3), sv(2), ALU.mult))
        serial(pool.tensor_scalar(sv(3), sv(3), 1.0 / m, None, ALU.add))
    serial(pool.tensor_tensor(sv(3), sv(3), sv(1), ALU.mult))
    serial(pool.tensor_scalar(sv(4), lam, -1.0, 0.0, ALU.mult, ALU.max))
    serial(pool.tensor_scalar(sv(3), sv(3), 2.0, None, ALU.mult))
    serial(pool.tensor_tensor(sv(3), sv(3), sv(4), ALU.add))
    sp_ok = serial(pool.tensor_scalar(sv(3), sv(3), 4.0, None, ALU.mult))
    lg_ok = project(lru_g, xs_a)
    go_ok = project(gout, xs_a)
    pt_ok = turn_probs(probs, probs_t, p_ok)
    o_ok2 = weigh(probs_t, values(mv, 4), xs_b, 6, pt_ok, v_ok)
    e_neg, e_last, klast = uu[:, 0, :], uu[:, 1, :], hh[:, 0, :]
    AC.wait(cum_ok)
    e1 = AC(act.activation(ee, cum, ACT.Exp))
    e2 = AC(act.activation(e_neg, cum, ACT.Exp, scale=-1.0))
    last_cum = cum.rearrange("p (c n) -> p c n", n=CHUNK)[:, :, CHUNK - 1]
    for c in range(S // CHUNK):
        e4 = AC(act.activation(e_last[:, c * CHUNK:(c + 1) * CHUNK], cum[:, c * CHUNK:(c + 1) * CHUNK], ACT.Exp, scale=-1.0,
                               bias=cum[:, (c + 1) * CHUNK - 1:(c + 1) * CHUNK]))
    decay = soft[:, 0:4]
    AC.wait(p_ok[1], p_ok[3])
    e5 = AC(act.activation(decay, last_cum, ACT.Exp))
    DV.wait(e1, e2, qk_ok, masks_ok, pt_ok)
    qd_ok = DV(dve.scalar_tensor_tensor(qd, gqk[:, 0, :], 32.0 ** -0.5, ee, ALU.mult, ALU.mult))
    DV.wait(DV(dve.tensor_tensor(zz, gqk[:, 1, :], e_neg, ALU.mult)))
    for h in range(4):
        kd_ok = DV(dve.tensor_scalar(kd[:, h, :], zz, head_cols[:, h:h + 1], None, ALU.mult))
    DV.wait(e4)
    kl_ok = DV(dve.tensor_tensor(klast, gqk[:, 1, :], e_last, ALU.mult))
    PE.wait(kd_ok, qd_ok, o_ok2)
    for h in range(4):
        for pr in range(2):
            n = 2 * h + pr
            last = pe.matmul(ps[:, 4 + n // 4, (n % 4) * P:(n % 4) * P + P], kd[:, h, pr * P:(pr + 1) * P], qd[:, pr * P:(pr + 1) * P],
                             start=True, stop=True)
    at_ok = PE(last)
    PE.wait(kl_ok)
    for tb in range(NT):
        last = pe.transpose(ps[:, 6, tb * P:(tb + 1) * P], klast[:, tb * P:(tb + 1) * P], ident[:, :])
    kt = PE(last)
    AC.wait(kt, kl_ok)
    klt_ok = AC(act.activation(klast_t, ps[:, 6, 0:S].rearrange("p (a n) -> p a n", a=NT), ACT.Copy))
    DV.wait(at_ok)
    for n in range(2):
        am_ok = DV(dve.tensor_tensor(attn[:, 4 * n:4 * n + 4, :], ps[:, 4 + n, :].rearrange("p (a n) -> p a n", a=4),
                                     gla_mask[:, None, :].to_broadcast([P, 4, P]), ALU.mult))
    PE.wait(klt_ok, gv_ok)
    kv_bank = ((6, 0), (7, 0), (6, S))
    for c in range(3):
        rows = slice(64 * (c % 2), 64 * (c % 2) + 64)
        bank, at = kv_bank[c]
        last = pe.matmul(ps[:, bank, at:at + S], klast_t[rows, c // 2, :], gv[rows, c // 2, :], start=True, stop=True)
    kv_ok = PE(last)
    kvs = [ps[:, bank, at:at + S] for bank, at in kv_bank]
    PE.wait(o_ok, bank_free[0], bank_free[2])
    Y = tokens_out(0)
    gemm(t_matmuls, 0, xs_b, 4, True, False)
    DV.wait(kv_ok, e5)
    f0 = DV(dve.tensor_copy(state[:, 0, :], kvs[0])); DV.wait(f0)
    for c in (1, 2):
        f0 = DV(dve.scalar_tensor_tensor(state[:, c, :], state[:, c - 1, :], decay[:, c:c + 1], kvs[c], ALU.mult, ALU.add)); DV.wait(f0)
    for h in range(4):
        part = state[:, :, 64 * h:64 * h + 64]
        st_ok = DV(dve.tensor_scalar(part, part, head_cols[:, h:h + 1], None, ALU.mult))
    AC.wait(sp_ok, ri_ok)
    for b in range(2):
        w_ok = AC(act.activation(tt[:, b, :], ri[:, b, :], ACT.Tanh, scale=sv(3)[:, b:b + 1]))
    PO.wait(w_ok)
    b1 = PO(pool.tensor_scalar(aa, tt, -1.0, 1.0, ALU.mult, ALU.add))
    DV.wait(w_ok, kt)
    b2 = DV(dve.tensor_scalar(hh, tt, 1.0, None, ALU.add)); DV.wait(b2, b1)
    b3 = DV(dve.tensor_scalar(tt, tt, 1e-30, None, ALU.max))
    b4 = DV(dve.reciprocal(hh, hh)); DV.wait(b4)
    a_ok = DV(dve.tensor_tensor(aa, aa, hh, ALU.mult))
    AC.wait(b3)
    rt = AC(act.activation(tt, tt, ACT.Sqrt))
    PO.wait(ri_ok)
    b7 = serial(pool.tensor_tensor(xc, xc, ri[:, 2:4, :], ALU.mult))
    DV.wait(rt, a_ok)
    b5 = DV(dve.scalar_tensor_tensor(uu, tt, 2.0, hh, ALU.mult, ALU.mult)); DV.wait(b5)
    b6 = DV(dve.memset(uu[:, :, 0:1], 1.0)); DV.wait(b6, b7)
    b8 = DV(dve.tensor_tensor(uu, uu, xc, ALU.mult)); DV.wait(b8)
    PE.wait(st_ok, am_ok)
    first = True
    for hp in range(2):
        for c in range(1, 4):
            pe.matmul(ps[:, 4, hp * S + c * CHUNK:hp * S + (c + 1) * CHUNK], state[:, c - 1, hp * P:(hp + 1) * P],
                      qd[:, c * CHUNK:(c + 1) * CHUNK], start=first, stop=False, skip_group_check=True)
            first = False
    for h in range(4):
        for pr in range(2):
            last = pe.matmul(ps[64 * (h % 2):64 * (h % 2) + 64, 4, (h // 2) * S + pr * P:(h // 2) * S + (pr + 1) * P],
                             gv[:, pr, 64 * h:64 * h + 64], attn[:, 2 * h + pr, :], start=False, stop=True, skip_group_check=True)
    og = PE(last)
    out_gla = ps[:, 4, :].rearrange("p (a n) -> p a n", a=2)

    for b in range(2):
        h_ok = DV(dve.tensor_tensor_scan(hh[:, b, :], aa[:, b, :], uu[:, b, :], 0.0, ALU.mult, ALU.add))
    gelu = ri[:, 0:2, :]
    PO.wait(lg_ok, w_ok)
    serial(pool.tensor_tensor(gelu, lru_g, lru_g, ALU.mult))
    serial(pool.tensor_scalar(gelu, gelu, 0.044715, 1.0, ALU.mult, ALU.add))
    k1 = serial(pool.tensor_tensor(gelu, gelu, lru_g, ALU.mult))
    AC.wait(og, am_ok)
    g2 = AC(act.activation(osq, out_gla, ACT.Square))
    g1 = AC(act.activation(oo, out_gla, ACT.Copy))
    PE.wait(g2, masks_ok)
    g3 = PE(pe.matmul(ps[:, 5, :], head_ones, osq.rearrange("p a n -> p (a n)"), start=True, stop=True))
    AC.wait(k1, go_ok, klt_ok)
    k2 = AC(act.activation(gelu, gelu, ACT.Sigmoid, scale=2.0 * math.sqrt(2.0 / math.pi)))
    gsig = view(work, 7936 + 512, 2, S)
    g9 = AC(act.activation(gsig, gout, ACT.Sigmoid))
    PO.wait(k2)
    k3 = serial(pool.tensor_tensor(gelu, gelu, lru_g, ALU.mult))
    PO.wait(g9)
    g10 = serial(pool.tensor_tensor(gsig, gsig, gout, ALU.mult))
    rows_ok = row_load(2, t["post_mix_norm"][0], og, colsb_ok)
    DV.wait(g3)
    g4 = DV(dve.tensor_scalar(osq, ps[:, 5, :].rearrange("p (a n) -> p a n", a=2), 1.0 / 64, RMS_EPS, ALU.mult, ALU.add))
    AC.wait(g4)
    g5 = AC(act.activation(osq, osq, ACT.Sqrt))
    DV.wait(k3, h_ok)
    k4 = DV(dve.tensor_tensor(hh, hh, gelu, ALU.mult))
    lru_ok = split_into(xs_b, 0, hh, k4)
    DV.wait(g5)
    g6 = DV(dve.reciprocal(osq, osq))
    DV.wait(g1, g10)
    for b in range(2):
        g8 = DV(dve.scalar_tensor_tensor(oo[:, b, :], oo[:, b, :], col("gla_norm", b), gsig[:, b, :], ALU.mult, ALU.mult))
    DV.wait(g6, g8)
    g11 = DV(dve.tensor_tensor(oo, oo, osq, ALU.mult))
    gla_ok = split_into(xs_b, 2, oo, g11)
    gemm(t_matmuls, 0, xs_b, 6, False, False)
    PE.wait(lru_ok)
    gemm(t_matmuls, 0, xs_b, 0, False, False)
    for place in (3, 4, 5):
        free[place] = [lru_ok, og]
    next_place = 3

    names = ("gate_low", "gate_sum", "gate_sig", "silu_ok", "up_low", "up_sum", "h_ok", "h_hi", "h_lo")
    F = {n: nc.alloc_semaphore("ffn_" + n) for n in names}
    hs = xs_b[:, :, :, :].rearrange("p (u k) a n -> p u k a n", u=4)[:, 0:2]
    gg = view(work, 6 * D, 2, 2, S)
    sig = view(work, 7 * D, 2, S)

    def ffn_load(w_gate, w_up, w_down):
        s0, p0 = loaded, next_place
        for w in (w_gate, w_up):
            load(f_source(w, 0))
        return w_gate, w_up, w_down, s0, p0

    def feed_forward(number, weights, x_ok, y_free, scr_free, ada=None, ada_col=0):
        nonlocal loaded, next_place, split_next, gemm_next, ada_loaded, ada_next, ada_muls
        w_gate, w_up, w_down, s0, p0 = weights
        base = number * TURNS
        assert s0 == gemm_next
        wg = w_gate.rearrange("(k p) n -> p k n", p=P)
        wu = w_up.rearrange("(k p) n -> p k n", p=P)

        def gate_part(turn_, s):
            first = isinstance(turn_, int)
            for d, before in enumerate(("gate_sum", "up_sum")):
                pe.wait_ge(s_lo, s[1] + d + 1)
                if not first:
                    pe.wait_ge(F[before], base + turn_)
                f_matmuls((s[0] + d) % NHL, 2 * d, xs_a, 2, x_ok if first and d == 0 else None).then_inc(s_used, 1)

        def hidden(turn_, s, u):
            first = isinstance(turn_, int)
            n = turn_ + (base + 1)
            for d, name in enumerate(("gate", "up")):
                act.wait_ge(s_used, s[1] + d + 1)
                if not first:
                    act.wait_ge(F[name + "_sum"], base + turn_)
                act.activation(half[:, d, :, :], ps[:, 2 * d:2 * d + 2, S:2 * S], ACT.Copy).then_inc(F[name + "_low"], 1)
                dve.wait_ge(F[name + "_low"], n)
                if not first:
                    dve.wait_ge(F["h_lo"], base + turn_)
                dve.tensor_tensor(gg[:, d, :, :], ps[:, 2 * d:2 * d + 2, 0:S], half[:, d, :, :], ALU.add).then_inc(F[name + "_sum"], 1)
                if d == 0:
                    yield
                    act.wait_ge(F["gate_sum"], n)
                    act.activation(sig, gg[:, 0, :, :], ACT.Sigmoid).then_inc(F["gate_sig"], 1)
                    pool.wait_ge(F["gate_sig"], n)
                    pool.tensor_tensor(gg[:, 0, :, :], gg[:, 0, :, :], sig, ALU.mult).then_inc(F["silu_ok"], 1)
                    yield
            dve.wait_ge(F["up_sum"], n)
            dve.wait_ge(F["silu_ok"], n)
            dve.tensor_tensor(gg[:, 1, :, :], gg[:, 0, :, :], gg[:, 1, :, :], ALU.mult).then_inc(F["h_ok"], 1)
            yield
            act.wait_ge(F["h_ok"], n)
            act.activation(hs[:, u, :, 0, :], gg[:, 1, :, :], ACT.Copy).then_inc(F["h_hi"], 1)
            dve.wait_ge(F["h_hi"], n)
            dve.tensor_tensor(hs[:, u, :, 1, :], gg[:, 1, :, :], hs[:, u, :, 0, :].bitcast(F32), ALU.subtract).then_inc(F["h_lo"], 1)
            yield

        def down_part(turn_, s, u):
            pe.wait_ge(s_lo, s[1] + 1)
            pe.wait_ge(F["h_lo"], turn_ + (base + 1))
            t_matmuls(s[0] % NHL, 4, hs[:, u], 0, False, False).then_inc(s_used, 1)

        s = (s0, s0)
        while split_next < s0 + AHEAD:
            split()
        gate_part(0, s)
        PE.wait(y_free)
        for n in range(4):
            pe.matmul(ps[:, 4 + n, :], zeros16[:, :], zeros16[:, 0:1].to_broadcast([P, 512]), start=True, stop=False, skip_group_check=True)
        AC.wait(x_ok[-1])
        DV.wait(x_ok[-1], scr_free)
        loop_s = s0 + 2
        place_of = lambda n: (n - s0 + p0) % NRAW
        count = {place_of(loop_s + n): 16 * (loads[place_of(loop_s + n)] + 1) for n in range(6)}
        split(loop_s, place_of(loop_s), count[place_of(loop_s)], loop_s)
        parts = hidden(0, s, 0)
        for _ in range(4):
            next(parts)
        iterations = (TURNS - 1) // 2
        for token in [token for place in free for token in place if token[0] is not s_lo]:
            sp.wait_ge(*token)
        with nc.Fori(0, iterations, 1) as i:
            s_reg = i * 6 + loop_s
            for n in range(6):
                turn_col = (i * 2 + (1 + n // 3)) * COLS
                place = place_of(loop_s + n)
                if n % 3 < 2:
                    src = (wg, wu)[n % 3][:, :, bass.ds(turn_col, COLS)]
                else:
                    src = w_down[bass.ds(turn_col - COLS, COLS), :].rearrange("(k p) n -> p k n", p=P)
                sp.wait_ge(s_lo, s_reg + (n - NRAW + 1))
                sp.dma_start(raw[:, place, :].rearrange("p (k n) -> p k n", k=src.shape[1]), src).then_inc(raw_landed[place], 16)
            for v in range(2):
                turn_ = i * 2 + (1 + v)
                s = (loop_s + 3 * v, s_reg + 3 * v)
                u = (1 + v) % 2
                parts = hidden(turn_, s, u)

                def split_at(n):
                    n += 3 * v
                    place = place_of(loop_s + n)
                    split(loop_s + n, place, i * 16 + count[place] + 16 * (n // 6), s_reg + n)

                def ada_at(part):
                    if ada is not None:
                        q = ada_next + part
                        src = ada[part * 2 * P:(part + 1) * 2 * P, bass.ds(i * D + ada_col, D)].rearrange("(k p) n -> p k n", p=P)
                        pool.wait_ge(s_ada_used, i * 4 + (q - NADA + 1))
                        pool.dma_start(ada_raw[:, q % NADA, :].rearrange("p (k n) -> p k n", k=2), src).then_inc(ada_landed[q % NADA], 16)
                        yield
                        ada_multiply(acc[:, bass.ds(i + 1, 1), :].rearrange("p a n -> p (a n)"), part, q % NADA,
                                     i * 32 + 16 * (q // NADA + 1), i * 8 + (ada_muls + 2 * part))
                    yield

                ada_parts = [ada_at(2 * v), ada_at(2 * v + 1)]
                for a in ada_parts:
                    next(a)
                split_at(1)
                split_at(2)
                gate_part(turn_, s)
                next(parts)
                if ada is not None:
                    next(ada_parts[0])
                split_at(3)
                next(parts)
                next(parts)
                if ada is not None:
                    next(ada_parts[1])
                next(parts)
                down_part(turn_ - 1, (s[0] + 2, s[1] + 2), 1 - u)
        for n in range(6):
            loads[place_of(loop_s + n)] += iterations
        loaded += 6 * iterations
        split_next = loaded + 1
        gemm_next += 2 + 6 * iterations
        if ada is not None:
            ada_loaded += 4 * iterations
            ada_next += 4 * iterations
            ada_muls += 8 * iterations
        for place in range(NRAW):
            free[place] = [(s_lo, loaded)]
        next_place = place_of(loaded)
        load(t_source(w_down, DFF - COLS))

    def last_down(number):
        pe.wait_ge(F["h_lo"], (number + 1) * TURNS)
        return closed(gemm(t_matmuls, 4, hs[:, (TURNS - 1) % 2], 0, False, True, hold=True))

    ffn = ffn_load(t["w_ffn_gate"][0], t["w_ffn_up"][0], t["w_ffn_down"][0])
    ada_step(0, 2)
    ada_step(0, 3)
    PE.wait(gla_ok)
    done = closed(gemm(t_matmuls, 0, xs_b, 2, False, True, hold=True))
    ready = add_rms(done, Y, row_gain[2], rows_ok, gla_ok)
    y_read = ready[-1]
    ready = normed(ready)
    turned = turn(scr, ready, 4, [g4])
    xs_ready = take(turned, xs_a, lambda k: col("pre_ffn_norm", k))
    rows_ok = row_load(0, t["post_ffn_norm"][0], y_read)
    feed_forward(0, ffn, xs_ready, None, None, t["w_ada_2"][0], D)

    conv_in = t["conv_w_in_2"][0]
    for j in range(4):
        for third in (1, 2, 0):
            load(f_source(conv_in, third * D + j * COLS))
    for n in range(4):
        load(t_source(t["conv_w_out_2"][0], n * 2 * P))
    ada_queue += [ada_source(w, c, part) for w, c in ((t["w_ada_kv_2"], 0), (t["w_ada_kv_2"], D)) for part in range(4)]
    done = last_down(0)
    sums = ada_finish([(c, c) for c in range(3)], 0, (F["up_sum"], TURNS))
    Y = tokens_out(4)
    ready = add_rms(done, Y, row_gain[0], rows_ok)
    mods = ada_columns(sums)
    lower_held()
    half_free[0] = half_free[1] = (F["up_sum"], TURNS)
    turned = turn([x_res[:, tb, :] for tb in range(NT)], ready, 0, [mods])
    xs_ready = take(turned, xs_a, acol(1), acol(0), mods)
    which[0] = 0
    bank_free.update({0: xs_ready[0], 2: xs_ready[-1], 4: ready[-1], 6: ready[-1]})
    cpad, cc_, vv_, bb_ = view(work, 6 * D, 2, S + 2), view(work, 6 * D + 520, 2, S), view(work, 6 * D + 1032, 2, S), view(work, 6 * D + 1544, 2, S)
    PO.wait(ready[-1], mods)
    pz = serial(pool.memset(cpad[:, :, 0:2], 0.0))
    ada_fill()
    diag_ok = diagonal(2, row_gain[2])
    mixed, step, mixed_j = None, 0, []
    for j in range(4):
        c_ok = project(cc_, xs_a, mixed, mods, bank=0 if j == 0 else None, xs_in=xs_ready if j == 0 else None)
        ada_step(step // 4, step % 4)
        if j == 2:
            gate_ok = spread(diag_ok, row_gain[1], row_gain[2], 4, ready[-1])
        v_ok = project(vv_, xs_a, mixed)
        PO.wait(c_ok, v_ok, mixed)
        u_ok = serial(pool.tensor_tensor(cpad[:, :, 2:], cc_, vv_, ALU.mult))
        b_ok = project(bb_, xs_a, mixed)
        cv = conv(cc_, cpad, 3, lambda n, b: col("conv_w_2", 8 * n + 2 * j + b), None, u_ok)
        PO.wait(b_ok, cv)
        m_ok = PO(pool.tensor_tensor(bb_, bb_, cc_, ALU.mult))
        ada_step((step + 1) // 4, (step + 1) % 4)
        mixed = split_into(xs_b, 2 * j, bb_, m_ok)
        step += 2
        mixed_j.append(mixed)
    rows_ok = [row_load(0, t["ln1_g_2"][0], mixed), row_load(2, t["ln1_b_2"][0], gate_ok)]
    ffn = ffn_load(t["ffn_w_gate_2"][0], t["ffn_w_up_2"][0], t["ffn_w_down_2"][0])
    PE.wait(gate_ok, ready[-1])
    for n in range(4):
        PE.wait(mixed_j[n])
        done = closed(gemm(t_matmuls, 4, xs_b, 2 * n, n == 0, n == 3, hold=(n == 3)))
    sums = ada_finish([(c, c) for c in range(3, 6)], 0, bank_free[0])
    ready, y_read = layer_norm(done, Y, row_gain[1], gate_ok, mixed)
    mods = ada_columns(sums)
    scale, shift, f_ok = fold(0, "ln1", 0, 4, mods)
    turned = turn(scr, ready, 0, [mods, bank_free[0], bank_free[2]])
    sums = ada_finish([(6, 0), (7, 1)], 4, y_read)
    xs_ready = take(turned, xs_a, scale, shift, f_ok)
    mods = ada_columns(sums)
    PO.wait(*rows_ok)
    res_ok = residual(ready, row_gain[0], row_gain[2], None, turned)
    rows_ok = row_load(0, t["ln2_g_2"][0], res_ok)
    diag_ok = diagonal(5, row_gain[2], mods)
    feed_forward(1, ffn, xs_ready, mods, res_ok, t["w_ada_2"][1])

    w_k, w_v, w_q, w_o = t["w_k_2"], t["w_v_2"], t["attn_w_q_2"][0], t["attn_w_o_2"][0]
    fox_base = loaded
    fox = [t_source(w_v, n * 2 * P) for n in range(4)] + [t["w_f_2"].rearrange("(k p) n -> p k n", p=P)]
    fox += [f_source(w, j * COLS) for w, j in ((w_k, 0), (w_q, 0), (w_k, 1), (w_q, 1), (w_k, 2), (w_k, 3), (w_q, 2), (w_q, 3))]
    fox += [t_source(w_o, n * 2 * P) for n in range(4)]
    for n, src in enumerate(fox):
        load(src, (n + 1) % 3)
    gate_ok = spread(diag_ok, row_gain[1], row_gain[2], 0, (F["gate_sum"], 2 * TURNS))
    rows_ok = [rows_ok, row_load(2, t["ln2_b_2"][0], gate_ok)]
    done = last_down(1)
    PE.wait(gate_ok)
    sums = ada_finish([(8, 1), (9, 2), (10, 3)], 0)
    ready, y_read = layer_norm(done, Y, row_gain[1], gate_ok)
    mods = ada_columns(sums)
    scale, shift, f_ok = fold(0, "ln2", 0, 7, mods)
    scale2, shift2, f_ok = fold(1, "ln2", 0, 9, mods)
    half_free[0] = half_free[1] = (F["up_sum"], 2 * TURNS)
    turned = turn(scr, ready, 4, [y_read])
    xs_ready = take(turned, xs_b, scale, shift, f_ok)
    PO.wait(*rows_ok)
    res_ok = residual(ready, row_gain[0], row_gain[2], None, turned)
    kT = view(lent, 0, KB, S)
    qT = [view(lent, 2048 + 512 * n, 2, S) for n in range(4)]
    vN = view(lent, 4096, NT, D)
    probs, probs_t = view(work, 0, 4, 384), view(work, 1536, 4, 384)
    zf, ef, one, ff = (view(work, 3 * D + S * n, S)[0:16, :] for n in range(4))
    minus_f_tile = sb("minus_f", [16, 2, 384], F32R)
    minus_f = [minus_f_tile[:, n, :] for n in range(2)]
    pick = sb("pick", [16, 16], F32R)
    pick_ok = AC(act.activation(pick[:, :], ident[0:16, 0:16], ACT.Copy))
    f_cols = small[:, 32:64]
    lent_free = (s_lo, fox_base)
    ada_queue += [ada_source(t["w_ada_2"][1], 5 * D, part) for part in range(4)]
    causal = scr[1][:, 0:384]
    serial(pool.memset(causal, 0.0))
    serial(pool.affine_select(out=causal[:, 0:P], in_=causal[:, 0:P], compare_op=ALU.is_ge, fill=NEG, base=0, pattern=[[-1, P]],
                              channel_multiplier=1))
    causal_ok = serial(pool.affine_select(out=causal[:, P:], in_=causal[:, P:], compare_op=ALU.is_ge, fill=NEG, base=P,
                                          pattern=[[-1, S]], channel_multiplier=1))
    ada_fill()
    PE.wait(mods)
    for n in range(4):
        PE.wait(xs_ready[n])
        v_done = gemm(t_matmuls, 0, xs_b, 2 * n, n == 0, n == 3)
        if n == 0:
            q_ready = take(turned, xs_a, scale2, shift2, f_ok)
    V = tokens_out(0)
    DV.wait(v_done, lent_free)
    v_ok = DV(dve.tensor_copy(vN[:, 0, :], V[0]))
    AC.wait(v_done, lent_free)
    v_ok2 = AC(act.activation(vN[:, 1, :], V[1], ACT.Copy))
    bank_free.update({0: v_ok, 2: v_ok2, 4: q_ready[-1], 6: q_ready[-1]})
    zf_ok = project16(zf, xs_b, mods, bank=4)
    k_ok0 = project(kT[:, 0:2, :], xs_b, lent_free, bank=6)
    DV.wait(zf_ok)
    c1 = DV(dve.tensor_scalar(zf, zf, b_f, None, ALU.add))
    AC.wait(c1)
    c2 = AC(act.activation(ef, zf, ACT.Abs)); AC.wait(c2)
    c2 = AC(act.activation(ef, ef, ACT.Exp, scale=-1.0)); AC.wait(c2)
    c2 = AC(act.activation(ef, ef, ACT.Ln, bias=1.0))
    DV.wait(c1, c2)
    c3 = DV(dve.tensor_scalar(zf, zf, 0.0, None, ALU.min)); DV.wait(c3)
    c3 = DV(dve.tensor_tensor(zf, zf, ef, ALU.subtract)); DV.wait(c3)
    c4 = DV(dve.memset(one, 1.0)); DV.wait(c4)
    c5 = DV(dve.tensor_tensor_scan(ff, one, zf, 0.0, ALU.mult, ALU.add)); DV.wait(c5)
    AC.wait(c5)
    for n in range(2):
        at, size = QUERY_BLOCKS[n]
        h_ok = AC(act.activation(minus_f[0][:, at:at + size], ff[:, 0:size], ACT.Copy, scale=-1.0))
    DV.wait(h_ok)
    for n in range(2):
        at, size = QUERY_BLOCKS[n]
        nf_ok = DV(dve.scalar_tensor_tensor(minus_f[1][:, at:at + size], ff[:, 0:size], -1.0, minus_f[0][:, at:at + size].bitcast(F32),
                                            ALU.mult, ALU.subtract))

    def fox_logits(g):
        def write(j, tb, out, s_):
            h = 4 * g + j
            c = causal[:, P:] if tb else causal[:, 0:P]
            return dve.scalar_tensor_tensor(out, s_, f_cols[:, tb * 16 + h:tb * 16 + h + 1], c, ALU.add, ALU.add)
        return write

    def fox_scores(g, *after, bank_4=None):
        done = scores(head(qT[g], 0), head(kT, 4 * g), (lambda j: pick[:, 4 * g + j:4 * g + j + 1].to_broadcast([16, P]), minus_f),
                      *after, bank_4=bank_4)
        return done[0], softmax(probs, soft, fox_logits(g), done, causal_ok, fc_ok)

    def fox_query(g):
        ok = project(qT[g], xs_a)
        DV.wait(ok)
        return DV(dve.tensor_scalar(qT[g], qT[g], DH ** -0.5, None, ALU.mult))

    def fox_keys(j):
        return project(kT[:, 2 * j:2 * j + 2, :], xs_b)

    def fox_output(n):
        return gemm(t_matmuls, 0, xs_b, 2 * n, n == 0, n == 3, hold=(n == 3))

    PE.wait(q_ready[-1])
    q_ok = fox_query(0)
    k_ok = fox_keys(1)
    PE.wait(c5, bank_free[4])
    for tb in range(NT):
        last = pe.transpose(ps[:, 4, tb * 16:tb * 16 + 16], ff[:, tb * P:(tb + 1) * P], ident[0:16, 0:16])
    DV.wait(PE(last))
    fc_ok = DV(dve.tensor_copy(f_cols, ps[:, 4, 0:32]))
    _, e_ok = fox_scores(0, q_ok, pick_ok, nf_ok, k_ok0, bank_free[6], bank_4=fc_ok)
    p_ok = divide(probs, e_ok)
    q_ok = fox_query(1)
    k_ok2 = fox_keys(2)
    pt_ok = turn_probs(probs, probs_t, p_ok)
    k_ok3 = fox_keys(3)
    AC.wait(k_ok3)
    o_ok0 = weigh(probs_t, values(vN, 0), xs_b, 0, pt_ok, v_ok, v_ok2)
    _, e_ok = fox_scores(1, q_ok, k_ok, pt_ok, bank_4=o_ok0)
    p_ok = divide(probs, e_ok)
    sums = ada_finish([(11, 4), (12, 5)], which[0], bank_free[which[0]])
    bank_free[which[0]] = late_mods = ada_columns(sums)
    diag_ok = diagonal(10, row_gain[2], res_ok, late_mods)
    q_ok2 = fox_query(2)
    DV.wait(res_ok)
    ada_step(6, 0)
    q_ok3 = fox_query(3)
    ada_step(6, 1)
    pt_ok = turn_probs(probs, probs_t, p_ok, o_ok0)
    gate_ok = spread(diag_ok, row_gain[1], row_gain[2], 2, q_ok2, q_ok3)
    o_ok1 = weigh(probs_t, values(vN, 4), xs_b, 2, pt_ok)
    _, e_ok = fox_scores(2, q_ok2, k_ok2, pt_ok, bank_4=o_ok1)
    p_ok = divide(probs, e_ok)
    PE.wait(gate_ok, q_ok3)
    fox_output(0)
    fox_output(1)
    ada_step(6, 2)
    pt_ok = turn_probs(probs, probs_t, p_ok, o_ok1)
    o_ok2 = weigh(probs_t, values(vN, 8), xs_b, 4, pt_ok)
    last_scores, e_ok = fox_scores(3, q_ok3, k_ok3, pt_ok, bank_4=o_ok2)
    p_ok = divide(probs, e_ok)
    fox_output(2)
    ada_step(6, 3)
    pt_ok = turn_probs(probs, probs_t, p_ok, o_ok2)
    o_ok3 = weigh(probs_t, values(vN, 12), xs_b, 6, pt_ok)
    free[3] = free[4] = [last_scores]
    free[5] = [o_ok3]
    next_place = 3
    rows_ok = [row_load(0, t["ln1_g_2"][1], res_ok), row_load(2, t["ln1_b_2"][1], gate_ok)]
    ffn = ffn_load(t["ffn_w_gate_2"][1], t["ffn_w_up_2"][1], t["ffn_w_down_2"][1])
    sums = ada_finish([(13, 6)], 5, pt_ok)
    DV.wait(sums[2])
    PE.wait(o_ok3)
    done = closed(fox_output(3))
    ready, y_read = layer_norm(done, tokens_out(0), row_gain[1], gate_ok, res_ok)
    scale, shift, f_ok = fold(0, "ln1", 1, 12, late_mods)
    mods = ada_columns(sums)
    turned = turn(scr, ready, 4, [mods])
    xs_ready = take(turned, xs_a, scale, shift, f_ok)
    PO.wait(*rows_ok)
    res_ok = residual(ready, row_gain[0], row_gain[2], None, turned)
    PE.wait(y_read)
    rows_ok = row_load(0, t["ln2_g_2"][1], res_ok)
    diag_ok = diagonal(13, row_gain[2], mods)
    feed_forward(2, ffn, xs_ready, xs_ready[-1], res_ok)
    gate_ok = spread(diag_ok, row_gain[1], row_gain[2], 0, (F["gate_sum"], 3 * TURNS))
    rows_ok = [rows_ok, row_load(2, t["ln2_b_2"][1], gate_ok)]
    PE.wait(gate_ok)
    done = last_down(2)
    s_out = nc.alloc_semaphore("s_out")
    out = t["out"].rearrange("a (t p) n -> p (a t) n", p=P)
    Y, norm = tokens_out(4), []
    DV.wait(gate_ok, res_ok, *rows_ok)
    for tb in range(NT):
        DV.wait(done[tb])
        token = DV(dve.tensor_tensor(scr[tb], Y[tb], row_gain[1], ALU.mult))
        DV.wait(token)
        total, minus_mean, square, r = (norm_cols[:, tb, n:n + 1] for n in range(4))
        z = DV(dve.scalar_tensor_tensor(scr[tb], x_res[:, tb, :], DEEPNORM_ALPHA, scr[tb], ALU.mult, ALU.add, accum_out=total))
        PO.wait(z)
        m_ok = PO(pool.tensor_scalar(minus_mean, total, -1.0 / D, None, ALU.mult))
        AC.wait(m_ok)
        sq = AC(act.activation(squares, scr[tb], ACT.Square, bias=minus_mean, accum_out=square))
        norm.append((m_ok, rstd(square, r, LN_EPS, 1.0 / D, sq)))
    for tb in range(NT):
        DV.wait(norm[tb][0])
        token = DV(dve.scalar_tensor_tensor(x_res[:, tb, :], scr[tb], norm_cols[:, tb, 1:2], row_gain[0], ALU.add, ALU.mult))
        DV.wait(token, norm[tb][1])
        token = DV(dve.scalar_tensor_tensor(x_res[:, tb, :], x_res[:, tb, :], norm_cols[:, tb, 3:4], row_gain[2], ALU.mult, ALU.add))
        sp.wait_ge(*token)
        sp.dma_start(out[:, tb, :], x_res[:, tb, :]).then_inc(s_out, 16)
    sp.wait_ge(s_out, 16 * NT)


_INS = ['x', 'pre_mix_norm', 'post_mix_norm', 'pre_ffn_norm', 'post_ffn_norm', 'w_in', 'w_out', 'lru_conv_w',
        'lru_conv_b', 'lru_wa', 'lru_ba', 'lru_wx', 'lru_bx', 'lru_lambda', 'gla_gate_w2', 'gla_gate_b', 'gla_norm',
        'rel_bias', 'w_ffn_gate', 'w_ffn_up', 'w_ffn_down', 'c_2', 'w_ada_2', 'b_ada_2', 'conv_w_in_2', 'conv_w_2',
        'conv_w_out_2', 'w_ada_kv_2', 'b_ada_kv_2', 'w_k_2', 'w_v_2', 'w_f_2', 'b_f_2', 'attn_w_q_2', 'attn_w_o_2',
        'ffn_w_gate_2', 'ffn_w_up_2', 'ffn_w_down_2', 'ln1_g_2', 'ln1_b_2', 'ln2_g_2', 'ln2_b_2']


def bucket_onehot():
    n = 255 - np.arange(S)
    nf = np.maximum(n, 1).astype(np.float32)
    large = 16 + (np.log(nf / np.float32(16)) / np.float32(math.log(128 / 16)) * np.float32(16)).astype(np.int32)
    bucket = np.where(n < 16, n, np.minimum(large, 31))
    return (np.arange(32)[:, None] == bucket[None, :]).astype(np.float32)


def kernel(**inputs):
    import numpy as _np
    import concourse.bacc as _bacc
    from concourse import mybir as _mybir
    from concourse.bass_utils import run_bass_kernel_spmd as _run

    nc = _bacc.Bacc("TRN2", target_bir_lowering=False, num_devices=1)
    arrays, t = {}, {}
    for name in _INS:
        a = _np.ascontiguousarray(inputs[name])
        arrays[f"in_{name}"] = a
        t[name] = nc.dram_tensor(f"in_{name}", a.shape, _mybir.dt.from_np(a.dtype), kind="ExternalInput").ap()
    arrays["bucket_onehot"] = bucket_onehot()
    t["bucket_onehot"] = nc.dram_tensor("bucket_onehot", (32, S), _mybir.dt.float32, kind="ExternalInput").ap()
    t["bias_table"] = nc.dram_tensor("bias_table", (8, 512), _mybir.dt.float32, kind="Internal").ap()
    t["out"] = nc.dram_tensor("out_0", (1, S, D), _mybir.dt.float32, kind="ExternalOutput").ap()
    build(nc, t)
    r = _run(nc, [arrays], core_ids=[0])
    return r.results[0]["out_0"]
```
